# Optimizing a Trainium2 kernel written in Bass

```python
import jax, jax.numpy as jnp
from jax import lax
import numpy as np

D_MODEL = 1024
BATCH = 1
SEQ = 512
DEPTH = 1

N_META = 16
CHUNK = 64
META_PAD = (-N_META) % CHUNK
DN_HEADS = 8
DN_DK = 128
DN_DV = 128
DN_QK = DN_HEADS * DN_DK
DN_VW = DN_HEADS * DN_DV
DN_CONV = 5
SC_WIDTH = 1024
SC_CONV = 3
D_FF = -(-8 * D_MODEL // (3 * 256)) * 256
RMS_EPS = 1e-6
L2_EPS = 1e-6

SPLIT_SIZES = [DN_QK, DN_QK, DN_VW, DN_VW, 2 * DN_HEADS, 2 * DN_HEADS,
               SC_WIDTH, SC_WIDTH, SC_WIDTH, D_MODEL, D_MODEL]
W_IN_COLS = sum(SPLIT_SIZES)
SPLIT_POINTS = list(np.cumsum(SPLIT_SIZES)[:-1].tolist())


def rmsnorm(x, w):
    xf = x.astype(jnp.float32)
    y = xf * lax.rsqrt(jnp.mean(xf * xf, axis=-1, keepdims=True) + RMS_EPS)
    return (y * w.astype(jnp.float32)).astype(x.dtype)

def l2norm(t):
    return t * lax.rsqrt(jnp.sum(t * t, axis=-1, keepdims=True) + L2_EPS)

def depthwise_conv_centred(x, w):
    K, C = w.shape
    r = K // 2
    return lax.conv_general_dilated(
        x, w[:, None, :].astype(x.dtype), window_strides=(1,), padding=[(r, r)],
        dimension_numbers=("NWC", "WIO", "NWC"), feature_group_count=C)

def chunk_gated_delta_rule(q, k, v, g, beta):
    Bsz, T, H, dk = q.shape
    dv = v.shape[-1]
    N = T // CHUNK

    def chunks(t):
        return t.reshape(Bsz, N, CHUNK, H, t.shape[-1]).transpose(0, 1, 3, 2, 4)

    q, k, v = chunks(q), chunks(k), chunks(v)
    g = g.reshape(Bsz, N, CHUNK, H).transpose(0, 1, 3, 2)
    beta = beta.reshape(Bsz, N, CHUNK, H).transpose(0, 1, 3, 2)
    g = jnp.cumsum(g, axis=-1)

    tri = jnp.tril(jnp.ones((CHUNK, CHUNK), dtype=bool))
    strict = jnp.tril(jnp.ones((CHUNK, CHUNK), dtype=bool), -1)
    decay = jnp.exp(jnp.where(tri, g[..., :, None] - g[..., None, :], -jnp.inf))

    kk = jnp.einsum("bnhid,bnhjd->bnhij", k, k)
    lmat = jnp.where(strict, beta[..., :, None] * kk * decay, 0.0)
    a = lmat + jnp.eye(CHUNK, dtype=lmat.dtype)
    rhs = jnp.concatenate([v * beta[..., None], k * (beta * jnp.exp(g))[..., None]], axis=-1)
    sol = lax.linalg.triangular_solve(a, rhs, left_side=True, lower=True, unit_diagonal=True)
    u, w = sol[..., :dv], sol[..., dv:]

    qk = jnp.einsum("bnhid,bnhjd->bnhij", q, k) * decay
    q_dec = q * jnp.exp(g)[..., None]
    g_last = g[..., -1]
    k_dec = k * jnp.exp(g_last[..., None] - g)[..., None]

    xs = tuple(jnp.moveaxis(t, 1, 0) for t in (qk, q_dec, k_dec, u, w, jnp.exp(g_last)))

    def step(S, inp):
        qk_c, qd_c, kd_c, u_c, w_c, gl_c = inp
        v_new = u_c - jnp.einsum("bhcd,bhde->bhce", w_c, S)
        o_c = (jnp.einsum("bhcd,bhde->bhce", qd_c, S)
               + jnp.einsum("bhij,bhje->bhie", qk_c, v_new))
        S = S * gl_c[..., None, None] + jnp.einsum("bhcd,bhce->bhde", kd_c, v_new)
        return S, o_c

    S0 = jnp.zeros((Bsz, H, dk, dv), jnp.float32)
    _, o = lax.scan(step, S0, xs)
    return o.transpose(1, 0, 3, 2, 4).reshape(Bsz, T, H, dv)

def gated_deltanet_bidir(q, k, v, z, b_raw, a_raw, conv_w, A_log, dt_bias, norm_w):
    Bsz, L, _ = q.shape
    f32 = jnp.float32
    qkv = jax.nn.silu(depthwise_conv_centred(jnp.concatenate([q, k, v], axis=-1), conv_w)).astype(f32)
    qc, kc, vc = jnp.split(qkv, [DN_QK, 2 * DN_QK], axis=-1)
    qc = l2norm(qc.reshape(Bsz, L, DN_HEADS, DN_DK)) * (DN_DK ** -0.5)
    kc = l2norm(kc.reshape(Bsz, L, DN_HEADS, DN_DK))
    vc = vc.reshape(Bsz, L, DN_HEADS, DN_DV)
    beta = jax.nn.sigmoid(b_raw.astype(f32)).reshape(Bsz, L, 2, DN_HEADS)
    g = -jnp.exp(A_log.astype(f32)) * jax.nn.softplus(
        a_raw.astype(f32).reshape(Bsz, L, 2, DN_HEADS) + dt_bias.astype(f32))

    def pad(t):
        return jnp.pad(t, [(0, 0), (META_PAD, 0)] + [(0, 0)] * (t.ndim - 2))

    qp, kp, vp, bp, gp = pad(qc), pad(kc), pad(vc), pad(beta), pad(g)
    o_fwd = chunk_gated_delta_rule(qp, kp, vp, gp[:, :, 0], bp[:, :, 0])

    def flip(t):
        return jnp.flip(t, axis=1)

    o_bwd = flip(chunk_gated_delta_rule(flip(qp), flip(kp), flip(vp), flip(gp[:, :, 1]), flip(bp[:, :, 1])))
    o = (o_fwd + o_bwd)[:, META_PAD:]
    o = o * lax.rsqrt(jnp.mean(o * o, axis=-1, keepdims=True) + RMS_EPS) * norm_w.astype(f32)
    o = o * jax.nn.silu(z.reshape(Bsz, L, DN_HEADS, DN_DV).astype(f32))
    return o.reshape(Bsz, L, DN_VW).astype(z.dtype)

def first_inputs(seed: int = 0) -> dict:
    key = jax.random.key(seed)
    ks = jax.random.split(key, 20)
    f32 = jnp.float32

    def nrm(k, shape, scale):
        return jax.random.normal(k, shape, f32) * scale

    x = jax.random.normal(ks[0], (BATCH, SEQ, D_MODEL), f32)
    meta_tokens = nrm(ks[1], (N_META, D_MODEL), 1.0)
    norm1_w = 1.0 + nrm(ks[2], (DEPTH, D_MODEL), 0.02)
    w_in = nrm(ks[3], (DEPTH, D_MODEL, W_IN_COLS), D_MODEL ** -0.5)
    dn_conv_w = nrm(ks[4], (DEPTH, DN_CONV, DN_QK * 2 + DN_VW), DN_CONV ** -0.5)
    A_log = jnp.log(jax.random.uniform(ks[5], (DEPTH, 2, DN_HEADS), f32, 1.0, 16.0))
    dt = jnp.exp(jax.random.uniform(ks[6], (DEPTH, 2, DN_HEADS), f32, np.log(1e-3), np.log(1e-1)))
    dt_bias = dt + jnp.log(-jnp.expm1(-dt))
    dn_norm_w = 1.0 + nrm(ks[7], (DEPTH, DN_DV), 0.02)
    sc_conv_w = nrm(ks[8], (DEPTH, SC_CONV, SC_WIDTH), SC_CONV ** -0.5)
    w_branch_dn = nrm(ks[9], (DEPTH, DN_VW, D_MODEL), DN_VW ** -0.5)
    w_branch_sc = nrm(ks[10], (DEPTH, SC_WIDTH, D_MODEL), SC_WIDTH ** -0.5)
    w_out = nrm(ks[11], (DEPTH, D_MODEL, D_MODEL), D_MODEL ** -0.5)
    norm2_w = 1.0 + nrm(ks[12], (DEPTH, D_MODEL), 0.02)
    w_gate_up = nrm(ks[13], (DEPTH, D_MODEL, 2 * D_FF), D_MODEL ** -0.5)
    w_down = nrm(ks[14], (DEPTH, D_FF, D_MODEL), D_FF ** -0.5)
    final_norm_w = 1.0 + nrm(ks[15], (D_MODEL,), 0.02)
    return {"x": x, "meta_tokens": meta_tokens, "norm1_w": norm1_w, "w_in": w_in,
            "dn_conv_w": dn_conv_w, "A_log": A_log, "dt_bias": dt_bias, "dn_norm_w": dn_norm_w,
            "sc_conv_w": sc_conv_w, "w_branch_dn": w_branch_dn, "w_branch_sc": w_branch_sc,
            "w_out": w_out, "norm2_w": norm2_w, "w_gate_up": w_gate_up, "w_down": w_down,
            "final_norm_w": final_norm_w}

def first_block(x, meta_tokens, norm1_w, w_in, dn_conv_w, A_log, dt_bias, dn_norm_w,
              sc_conv_w, w_branch_dn, w_branch_sc, w_out, norm2_w, w_gate_up, w_down,
              final_norm_w):
    Bsz = x.shape[0]
    meta = jnp.broadcast_to(meta_tokens[None].astype(x.dtype), (Bsz, N_META, x.shape[-1]))
    h_res = jnp.concatenate([meta, x], axis=1)
    for l in range(DEPTH):
        h = rmsnorm(h_res, norm1_w[l])
        proj = h @ w_in[l]
        (q, k, v, z, b_raw, a_raw, sc_b, sc_c, sc_x, gate_a, gate_b) = jnp.split(proj, SPLIT_POINTS, axis=-1)
        o_dn = gated_deltanet_bidir(q, k, v, z, b_raw, a_raw, dn_conv_w[l], A_log[l], dt_bias[l], dn_norm_w[l])
        y_a = o_dn @ w_branch_dn[l]
        y_b = (sc_b * depthwise_conv_centred(sc_c * sc_x, sc_conv_w[l])) @ w_branch_sc[l]
        merged = jax.nn.sigmoid(gate_a) * y_a + jax.nn.sigmoid(gate_b) * y_b
        h_res = h_res + merged @ w_out[l]
        h2 = rmsnorm(h_res, norm2_w[l])
        gu = h2 @ w_gate_up[l]
        h_res = h_res + (jax.nn.silu(gu[..., :D_FF]) * gu[..., D_FF:]) @ w_down[l]
    out = rmsnorm(h_res, final_norm_w)
    return out[:, N_META:]


DEPTH_2 = 2

HEAD_DIM = 64
A_Q_HEADS = D_MODEL // HEAD_DIM
A_KV_HEADS = A_Q_HEADS // 4
IDX_HEADS = 8
IDX_DIM = 64
B_HEADS = D_MODEL // HEAD_DIM
D_FF_2 = 4 * D_MODEL
BLOCK = 128
TOPK_MAX = 256
ROPE_THETA = 10000.0
EPS = 1e-6
N_A = DEPTH_2 // 2
N_B = DEPTH_2 - N_A

A_Q_W = A_Q_HEADS * HEAD_DIM
A_KV_W = A_KV_HEADS * HEAD_DIM
IDX_Q_W = IDX_HEADS * IDX_DIM
A_SPLITS = (A_Q_W, A_Q_W + A_KV_W, A_Q_W + 2 * A_KV_W,
            A_Q_W + 2 * A_KV_W + IDX_Q_W, A_Q_W + 2 * A_KV_W + IDX_Q_W + IDX_DIM)
A_IN_W = A_SPLITS[-1] + IDX_HEADS
B_W = B_HEADS * HEAD_DIM
KV_IN_W = 2 * B_W + B_HEADS


def rms_norm(x, g):
    xf = x.astype(jnp.float32)
    y = xf * lax.rsqrt(jnp.mean(xf * xf, axis=-1, keepdims=True) + EPS)
    return (y * g.astype(jnp.float32)).astype(x.dtype)

def rope_tables(T, dim):
    inv = 1.0 / (ROPE_THETA ** (jnp.arange(0, dim, 2, dtype=jnp.float32) / dim))
    ang = jnp.arange(T, dtype=jnp.float32)[:, None] * inv[None, :]
    return jnp.cos(ang), jnp.sin(ang)

def rope(x, cos, sin):
    x1, x2 = jnp.split(x, 2, axis=-1)
    c = cos[None, :, None, :]
    s = sin[None, :, None, :]
    return jnp.concatenate([x1 * c - x2 * s, x1 * s + x2 * c], axis=-1).astype(x.dtype)

def sq_relu_mlp(x, w1, w2):
    h = jax.nn.relu(x @ w1)
    return (h * h) @ w2

def dsa_attention(h, w_in, q_gain, k_gain, w_out, cos, sin, topk):
    B, T, _ = h.shape
    R = A_Q_HEADS // A_KV_HEADS
    nblk = T // BLOCK
    q, k, v, qi, ki, wi = jnp.split(h @ w_in, list(A_SPLITS), axis=-1)
    q = rope(rms_norm(q.reshape(B, T, A_Q_HEADS, HEAD_DIM), q_gain), cos, sin)
    k = rope(rms_norm(k.reshape(B, T, A_KV_HEADS, HEAD_DIM), k_gain), cos, sin)
    v = v.reshape(B, T, A_KV_HEADS, HEAD_DIM)
    qi = rope(qi.reshape(B, T, IDX_HEADS, IDX_DIM), cos, sin)
    ki = rope(ki[:, :, None, :], cos, sin)[:, :, 0, :]
    wi = wi.astype(jnp.float32) * (IDX_HEADS ** -0.5 * IDX_DIM ** -0.5)
    qb = q.reshape(B, nblk, BLOCK, A_KV_HEADS, R, HEAD_DIM)
    qib = qi.reshape(B, nblk, BLOCK, IDX_HEADS, IDX_DIM)
    wib = wi.reshape(B, nblk, BLOCK, IDX_HEADS)
    key_pos = jnp.arange(T)
    scale = HEAD_DIM ** -0.5

    def per_seq(args):
        qb_s, qib_s, wib_s, k_s, v_s, ki_s = args

        def per_block(bargs):
            blk, q_blk, qi_blk, w_blk = bargs
            qpos = blk * BLOCK + jnp.arange(BLOCK)
            causal = key_pos[None, :] <= qpos[:, None]
            logits = jnp.einsum('qhd,sd->qhs', qi_blk, ki_s,
                                preferred_element_type=jnp.float32)
            score = jnp.einsum('qh,qhs->qs', w_blk, jax.nn.relu(logits))
            score = jnp.where(causal, score, -jnp.inf)
            _, idx = lax.top_k(score, topk)
            valid = idx <= qpos[:, None]
            k_sel = k_s[idx]
            v_sel = v_s[idx]
            s = jnp.einsum('qgrd,qkgd->qgrk', q_blk, k_sel,
                           preferred_element_type=jnp.float32) * scale
            s = jnp.where(valid[:, None, None, :], s, -jnp.inf)
            p = jax.nn.softmax(s, axis=-1).astype(v_s.dtype)
            return jnp.einsum('qgrk,qkgd->qgrd', p, v_sel)

        return lax.map(per_block, (jnp.arange(nblk), qb_s, qib_s, wib_s))

    o = lax.map(per_seq, (qb, qib, wib, k, v, ki))
    return o.reshape(B, T, A_Q_W) @ w_out

def shared_kv(h, w_kv, f_bias, k_gain):
    B, T, _ = h.shape
    k, v, fl = jnp.split(h @ w_kv, [B_W, 2 * B_W], axis=-1)
    k = rms_norm(k.reshape(B, T, B_HEADS, HEAD_DIM), k_gain)
    v = v.reshape(B, T, B_HEADS, HEAD_DIM)
    log_f = jax.nn.log_sigmoid(fl.astype(jnp.float32) + f_bias.astype(jnp.float32))
    c = jnp.cumsum(log_f, axis=1).transpose(0, 2, 1)
    return k, v, c

def fox_attention(h, w_q, q_gain, w_out, k, v, c):
    B, T, _ = h.shape
    q = rms_norm((h @ w_q).reshape(B, T, B_HEADS, HEAD_DIM), q_gain)
    scale = HEAD_DIM ** -0.5
    outs = []
    for blk in range(T // BLOCK):
        q0, q1 = blk * BLOCK, (blk + 1) * BLOCK
        s = jnp.einsum('bqhd,bshd->bhqs', q[:, q0:q1], k[:, :q1],
                       preferred_element_type=jnp.float32) * scale
        decay = c[:, :, q0:q1, None] - c[:, :, None, :q1]
        causal = jnp.arange(q0, q1)[:, None] >= jnp.arange(q1)[None, :]
        s = jnp.where(causal, s + decay, -jnp.inf)
        p = jax.nn.softmax(s, axis=-1).astype(v.dtype)
        outs.append(jnp.einsum('bhqs,bshd->bqhd', p, v[:, :q1]))
    o = jnp.concatenate(outs, axis=1)
    return o.reshape(B, T, B_W) @ w_out

def second_inputs(seed: int = 0) -> dict:
    key = jax.random.key(seed)
    ks = jax.random.split(key, 18)

    def dense(k, shape, fan_in, scale=1.0):
        return jax.random.normal(k, shape, jnp.float32) * (scale * fan_in ** -0.5)

    def gain(k, shape):
        return 1.0 + 0.02 * jax.random.normal(k, shape, jnp.float32)

    kv_kv = dense(ks[11], (D_MODEL, 2 * B_W), D_MODEL)
    kv_f = dense(ks[17], (D_MODEL, B_HEADS), D_MODEL, 0.25)
    return {
        "x": jax.random.normal(ks[0], (BATCH, SEQ, D_MODEL), jnp.float32),
        "meta_tokens": jax.random.normal(ks[1], (N_META, D_MODEL), jnp.float32),
        "attn_norm": gain(ks[2], (DEPTH_2, D_MODEL)),
        "mlp_norm": gain(ks[3], (DEPTH_2, D_MODEL)),
        "mlp_w1": dense(ks[4], (DEPTH_2, D_MODEL, D_FF_2), D_MODEL),
        "mlp_w2": dense(ks[5], (DEPTH_2, D_FF_2, D_MODEL), D_FF_2),
        "a_w_in": dense(ks[6], (N_A, D_MODEL, A_IN_W), D_MODEL),
        "a_q_gain": gain(ks[7], (N_A, HEAD_DIM)),
        "a_k_gain": gain(ks[8], (N_A, HEAD_DIM)),
        "a_w_out": dense(ks[9], (N_A, A_Q_W, D_MODEL), A_Q_W),
        "kv_norm": gain(ks[10], (D_MODEL,)),
        "kv_w": jnp.concatenate([kv_kv, kv_f], axis=1),
        "kv_f_bias": jax.random.uniform(ks[12], (B_HEADS,), jnp.float32, 1.0, 4.0),
        "kv_k_gain": gain(ks[13], (HEAD_DIM,)),
        "b_w_q": dense(ks[14], (N_B, D_MODEL, B_W), D_MODEL),
        "b_q_gain": gain(ks[15], (N_B, HEAD_DIM)),
        "b_w_out": dense(ks[16], (N_B, B_W, D_MODEL), B_W),
    }

def second_block(x, meta_tokens, attn_norm, mlp_norm, mlp_w1, mlp_w2,
              a_w_in, a_q_gain, a_k_gain, a_w_out,
              kv_norm, kv_w, kv_f_bias, kv_k_gain,
              b_w_q, b_q_gain, b_w_out):
    B, S, D = x.shape
    T = S + N_META
    Tp = -(-T // BLOCK) * BLOCK
    meta = jnp.broadcast_to(meta_tokens.astype(x.dtype)[None], (B, N_META, D))
    h = jnp.concatenate([meta, x], axis=1)
    h = jnp.pad(h, ((0, 0), (0, Tp - T), (0, 0)))
    cos, sin = rope_tables(Tp, HEAD_DIM)
    topk = min(TOPK_MAX, S // 4)
    shared = None
    for i in range(DEPTH_2):
        hn = rms_norm(h, attn_norm[i])
        if i < N_A:
            h = h + dsa_attention(hn, a_w_in[i], a_q_gain[i], a_k_gain[i], a_w_out[i],
                                  cos, sin, topk)
        else:
            if i == N_A:
                shared = shared_kv(rms_norm(h, kv_norm), kv_w, kv_f_bias, kv_k_gain)
            j = i - N_A
            h = h + fox_attention(hn, b_w_q[j], b_q_gain[j], b_w_out[j],
                                  shared[0], shared[1], shared[2])
        h = h + sq_relu_mlp(rms_norm(h, mlp_norm[i]), mlp_w1[i], mlp_w2[i])
    return h[:, N_META:N_META + S]


def setup_inputs(seed=0):
    out = dict(first_inputs(seed))
    for name, value in second_inputs(seed + 1).items():
        if name != "x":
            out[name + "_2"] = value
    return out


def reference(
    x, meta_tokens, norm1_w, w_in, dn_conv_w, A_log, dt_bias, dn_norm_w, sc_conv_w, w_branch_dn,
    w_branch_sc, w_out, norm2_w, w_gate_up, w_down, final_norm_w, meta_tokens_2, attn_norm_2,
    mlp_norm_2, mlp_w1_2, mlp_w2_2, a_w_in_2, a_q_gain_2, a_k_gain_2, a_w_out_2, kv_norm_2,
    kv_w_2, kv_f_bias_2, kv_k_gain_2, b_w_q_2, b_q_gain_2, b_w_out_2,
):
    x = first_block(
        x, meta_tokens, norm1_w, w_in, dn_conv_w, A_log, dt_bias, dn_norm_w, sc_conv_w,
        w_branch_dn, w_branch_sc, w_out, norm2_w, w_gate_up, w_down, final_norm_w,
    )
    return second_block(
        x, meta_tokens_2, attn_norm_2, mlp_norm_2, mlp_w1_2, mlp_w2_2, a_w_in_2, a_q_gain_2,
        a_k_gain_2, a_w_out_2, kv_norm_2, kv_w_2, kv_f_bias_2, kv_k_gain_2, b_w_q_2, b_q_gain_2,
        b_w_out_2,
    )


_drawn_inputs = setup_inputs


def setup_inputs(seed=0):
    import zlib

    import numpy as np

    out = dict(_drawn_inputs(seed))
    spreads = {}
    factors = {'dn_norm_w': 3.881,
     'a_q_gain_2': 8.0,
     'a_k_gain_2': 8.0,
     'kv_norm_2': 8.0,
     'kv_k_gain_2': 8.0,
     'b_q_gain_2': 8.0}
    for name, (base, spread) in spreads.items():
        noise = np.random.default_rng([zlib.crc32(name.encode()), seed]).standard_normal(out[name].shape)
        drawn = base * np.exp(spread * noise) if base else spread * noise
        out[name] = __import__('jax').numpy.asarray(drawn.astype(out[name].dtype))
    for name, factor in factors.items():
        out[name] = (out[name] * factor).astype(out[name].dtype)
    return out
```

```python
from collections import namedtuple

import numpy as np

import concourse.bass as bass
from concourse import mybir

F32 = mybir.dt.float32
F32R = mybir.dt.float32r
ALU = mybir.AluOpType
ACT = mybir.ActivationFunctionType
AX = mybir.AxisListType

P = 128
DM = 1024
KT = DM // P
NMETA, SEQ = 16, 512
T = NMETA + SEQ
HT = T // 2
C = 88
NCH = T // C
H1, NG, GH = 8, 2, 4
FF1 = 2816
FF1_PARTS = [8, 8, 6]
FF2_PARTS = [8, 8, 8, 8]
LEVELS = 7
TOPK = 128
NEG = -1.0e30
LOWEST = -3.0e38
EPS = 1.0e-6

Blk = namedtuple("Blk", "c i")


def num(b):
    return b.c + 2 * b.i


def slot(b):
    return b.c % 2


def nxt(b, n=1):
    return Blk(b.c + n, b.i)


Seg = namedtuple("Seg", "b0 n k")


def plan_segments():
    segs, at = {}, 0

    def add(name, n, k=KT):
        nonlocal at
        segs[name] = Seg(at, n, k)
        at += n

    add("ba", 2)
    add("qkv", 24)
    add("z", 8)
    add("sc", 24)
    add("gates", 16)
    add("ya", 8)
    add("yb", 8)
    add("wout", 8)
    for p, n in enumerate(FF1_PARTS):
        add(f"gu{p}", 2 * n)
        add(f"dn{p}", 8, n)
    add("dsa", 18)
    add("dsa_out", 8)
    for p, n in enumerate(FF2_PARTS):
        add(f"up0_{p}", n)
        add(f"down0_{p}", 8, n)
    add("foxkv", 16)
    add("foxf", 1)
    add("foxq", 8)
    add("fox_out", 8)
    for p, n in enumerate(FF2_PARTS):
        add(f"up1_{p}", n)
        add(f"down1_{p}", 8, n)
    return segs, at


SEGS, NB = plan_segments()


def wait(e, sem, value):
    if isinstance(value, int) and value <= 0:
        return
    e.wait_ge(sem, value)


def blocks(e, seg, body, first=0, last=0):
    pairs = seg.n // 2
    for i in range(first):
        for u in range(2):
            body(2 * i + u, u, Blk(seg.b0 + 2 * i + u, 0))
    if pairs - last > first:
        with e.Fori(first, pairs - last) as i:
            for u in range(2):
                body(i * 2 + u, u, Blk(seg.b0 + u, i))
    for i in range(pairs - last, pairs):
        for u in range(2):
            body(2 * i + u, u, Blk(seg.b0 + 2 * i + u, 0))
    if seg.n % 2:
        body(seg.n - 1, 0, Blk(seg.b0 + seg.n - 1, 0))


def tiles(e, n, body):
    with e.Fori(0, n // 2) as i:
        for u in range(2):
            body(i * 2 + u, u)


def pieces(n):
    return [(0, n)] if n <= 512 else [(0, HT), (HT, HT)]


def build_program(nc, io):
    w, out, nb = io["w"], io["out"], NB

    base = 16512
    F = 4 * T

    def place(name, shape, dt, offset):
        return nc.alloc_sbuf_tensor_at(name, shape, dt, offset=offset)

    def region(start):
        pos = [start]

        def sb(name, shape, dt=F32):
            n = 4
            for s in shape[1:]:
                n *= s
            n = -(-n // 32) * 32
            off = pos[0]
            pos[0] += n
            return place(name, shape, dt, off)

        sb.pos = pos
        return sb

    keep = region(base)
    res = keep("res", [P, KT * T])
    a_at = keep.pos[0]
    xah, xal = keep("xah", [P, KT * T], F32R), keep("xal", [P, KT * T], F32R)
    b_at = keep.pos[0]
    xbh, xbl = keep("xbh", [P, KT * T], F32R), keep("xbl", [P, KT * T], F32R)
    wraw = keep("wraw", [P, 2 * DM])
    wh, wl = keep("wh", [P, 2 * DM], F32R), keep("wl", [P, 2 * DM], F32R)
    stage = keep("stage", [P, 2 * T])
    ident = keep("ident", [P, P])
    ones = keep("ones", [P, P])
    win128 = keep("win128", [P, 31])
    win64 = keep("win64", [P, 30])
    gains = keep("gains", [P, 8 * KT])
    headgain = keep("headgain", [P, 8])
    rowvec = keep("rowvec", [16, 8])
    eps = keep("eps", [P, 1])
    rstd = keep("rstd", [P, T])
    phase_at = keep.pos[0]

    r1 = region(phase_at)
    qkv = r1("qkv", [P, 24 * T])
    oacc = r1("oacc", [P, 8 * T])
    convw = r1("convw", [P, 24 * 5])
    scw = r1("scw", [P, 8 * 3])
    tri = r1("tri", [C, 2, C])
    masks = r1("masks", [C, 2, LEVELS, C])
    sel = r1("sel", [16, 2, NG, GH])
    scum = r1("scum", [16, 2, T])
    tok_g = r1("tok_g", [C, NCH, 16])
    tok_b = r1("tok_b", [C, NCH, 16])
    tok_cum = r1("tok_cum", [C, 2, NCH, 8])
    tok_neg = r1("tok_neg", [C, 2, NCH, 8])
    tok_bk = r1("tok_bk", [C, 2, NCH, 8])
    chunk_decay = r1("chunk_decay", [P, 2, NCH, 8])
    d_at = r1.pos[0]
    assert d_at <= nc.sbuf_usable_end, d_at
    rb = region(b_at)
    cpad = [rb(f"cpad{u}", [P, T + 4]) for u in range(2)]
    cout = [rb(f"cout{u}", [P, T]) for u in range(2)]
    sq = [rb(f"sq{u}", [P, T]) for u in range(2)]
    hroot = rb("hroot", [32, T])
    hinv = rb("hinv", [32, T])
    beta = rb("beta", [16, T])
    gdec = rb("gdec", [16, T])
    sp = [rb(f"sp{i}", [16, T]) for i in range(5)]
    spread = place("spread", [16, 8 * P], F32, b_at)
    assert 4 * 8 * P <= 8 * (T + 4)
    delta = []
    rx = region(b_at)
    ry = region(d_at)

    def dsb(name, shape):
        n = 4
        for s in shape[1:]:
            n *= s
        r = rx if rx.pos[0] + n <= b_at + 2 * KT * F else ry
        return r(name, shape)

    W4 = GH * C
    for u in range(2):
        d = {}
        d["ks"] = dsb(f"ks{u}", [P, W4])
        d["qd"] = dsb(f"qd{u}", [P, W4])
        d["state"] = dsb(f"state{u}", [P, GH * P])
        d["kt"] = dsb(f"kt{u}", [C, GH * P])
        d["vt"] = dsb(f"vt{u}", [C, GH * P])
        d["qkm"] = dsb(f"qkm{u}", [C, W4])
        d["xt"] = dsb(f"xt{u}", [C, W4])
        r = rx if rx.pos[0] + 2 * 4 * W4 <= b_at + 2 * KT * F else ry
        o = r.pos[0]
        d["qs"], d["vs"] = r(f"qs{u}", [P, W4]), r(f"vs{u}", [P, W4])
        d["rr"] = place(f"rr{u}", [C, GH * P], F32, o)
        r = rx if rx.pos[0] + 2 * 4 * W4 <= b_at + 2 * KT * F else ry
        o = r.pos[0]
        d["dec"], d["ob"] = r(f"dec{u}", [C, W4]), r(f"ob{u}", [C, W4])
        d["vn"] = place(f"vn{u}", [C, GH * P], F32, o)
        r = rx if rx.pos[0] + 2 * 4 * W4 <= b_at + 2 * KT * F else ry
        o = r.pos[0]
        d["pp"], d["xx"] = r(f"pp{u}", [C, W4]), r(f"xx{u}", [C, W4])
        d["vk"] = place(f"vk{u}", [C, GH * P], F32, o)
        d["mt"] = dsb(f"mt{u}", [C, W4])
        d["grow"] = dsb(f"grow{u}", [16, W4])
        delta.append(d)
    assert ry.pos[0] <= nc.sbuf_usable_end, (ry.pos[0], nc.sbuf_usable_end)
    scy = place("scy", [P, 8 * T], F32, phase_at)
    gab = place("gab", [P, 16 * T], F32, phase_at + 8 * F)
    rsc = region(d_at)
    pc = rsc("pc", [P, T + 2])
    bst = rsc("bst", [P, T])

    r2 = region(phase_at)
    pf = r2("pf", [P, 24 * T])
    vtok = r2("vtok", [C, NCH, DM])
    causal = r2("causal", [C, C])
    assert r2.pos[0] <= nc.sbuf_usable_end, r2.pos[0]
    rdsa = region(phase_at + 17 * F)
    wi = rdsa("wi", [8, T])
    bias = rdsa("bias", [C, NCH, T])
    assert rdsa.pos[0] <= phase_at + 24 * F
    rv = region(phase_at + 24 * F + NCH * 256 * 4)
    cossin = rv("cossin", [P, 2, T])
    rot = rv("rot", [P, P])
    wit = rv("wit", [C, NCH, 8])
    assert rv.pos[0] <= phase_at + 24 * F + NCH * DM * 4
    rt = region(a_at)
    qz = rt("qz", [P, 2, T])
    score = [rt(f"score{u}", [C, T]) for u in range(2)]
    prob = [rt(f"prob{u}", [C, T]) for u in range(2)]
    ptr = [rt(f"ptr{u}", [C, T]) for u in range(2)]
    otok = rt("otok", [C, NCH * P])
    hbias = [rt(f"hbias{u}", [C, T]) for u in range(2)]
    rowmax = rt("rowmax", [C, 2 * NCH])
    rowsum = rt("rowsum", [C, 2 * NCH])
    rowinv = rt("rowinv", [C, 2 * NCH])
    top8 = rt("top8", [C, NCH * 8])
    lfneg = rt("lfneg", [16, T])
    cneg = rt("cneg", [16, T])
    assert rt.pos[0] <= b_at
    rtk = region(a_at)
    work = rtk("work", [C, NCH * T])
    ps = nc.alloc_psum_tensor("ps", [P, 8, 512], F32)
    SEMS = {}

    def sem(name):
        SEMS[name] = nc.alloc_semaphore(name)
        return SEMS[name]

    raw_full = [sem("raw_full0"), sem("raw_full1")]
    hi_done, lo_done = sem("hi_done"), sem("lo_done")
    block_done = sem("block_done")
    acc_free = sem("acc_free")
    post_done = sem("post_done")
    phase_done = sem("phase_done")
    const_in, const2_in, out_sent = sem("const_in"), sem("const2_in"), sem("out_sent")
    nsq, nused, nsum, nroot, nscaled, nhi, nlo = map(sem, (
        "norm_square", "norm_square_used", "norm_sum", "norm_root", "norm_scaled", "norm_hi", "norm_lo"))
    hsq, hused, hsum, hrt, hiv, hbc, happ = map(sem, (
        "head_square", "head_square_used", "head_sum", "head_root", "head_inverse", "head_spread",
        "head_applied"))
    conv_done, silu_done = sem("conv_done"), sem("silu_done")
    sp_abs, sp_exp = sem("softplus_abs"), sem("softplus_exp")
    prep_pe, prep_act, prep_dve = sem("prep_pe"), sem("prep_act"), sem("prep_dve")
    dpe = [sem("delta_pe0"), sem("delta_pe1")]
    dact = [sem("delta_act0"), sem("delta_act1")]
    ddve = [sem("delta_dve0"), sem("delta_dve1")]
    dpool = [sem("delta_pool0"), sem("delta_pool1")]
    rope_pe, rope_dve = sem("rope_turned"), sem("rope_applied")
    vt_in, vt_pe, vt_out = sem("v_staged"), sem("v_turned"), sem("v_stored")
    ix_q, ix_pe, ix_act, ix_dve = sem("index_q"), sem("index_logits"), sem("index_relu"), sem("index_added")
    wit_pe, prep_dve_ones = sem("index_weights_turned"), sem("ones_ready")
    at_q, at_hb, at_hbe, at_s, at_sc, at_mx = map(sem, (
        "att_q", "att_decay", "att_decay_out", "att_scores", "att_scaled", "att_max"))
    at_p, at_pt, at_pte, at_o, at_oe, at_ot, at_of, at_cn = map(sem, (
        "att_prob", "att_prob_turned", "att_prob_out", "att_value", "att_value_out", "att_turned",
        "att_stored", "att_gate_row"))

    before, total = {}, 0
    for name, seg in SEGS.items():
        before[name] = total
        if name in ("z", "sc", "ya", "yb", "wout", "dsa_out", "fox_out") or name[:2] in ("dn", "up") \
                or name.startswith("down"):
            total += 8 if name == "sc" else seg.n
        elif name.startswith("gu"):
            total += seg.n // 2

    phases = {"pe": 0, "act": 0, "dve": 0, "pool": 0}

    def barrier(e, who):
        phases[who] += 1
        e.drain().then_inc(phase_done, 1)
        e.wait_ge(phase_done, 4 * phases[who])

    def bank(b, rows=P, n=HT, off=0):
        return ps[0:rows, b, off:off + n]

    def pair_of(b, rows=P):
        return ps[0:rows, b:b + 2, 0:HT]

    def two(ap):
        return ap.rearrange("p (h t) -> p h t", h=2)

    def tile_at(buf, m, n=T, off=0):
        return buf[:, bass.ds(m * T + off, n)]

    def load_weights(sp):
        def load(b):
            wait(sp, lo_done, num(b) - 1)
            sp.dma_start(wraw[:, slot(b) * DM:(slot(b) + 1) * DM],
                         w[bass.ds(num(b), 1)].rearrange("a p n -> (a p) n")).then_inc(raw_full[slot(b)], 16)

        load(Blk(0, 0))
        load(Blk(1, 0))
        with sp.Fori(1, nb // 2) as i:
            for u in range(2):
                src = w[bass.ds(sp.snap(i * 2 + u), 1)].rearrange("a p n -> (a p) n")
                sp.wait_ge(lo_done, i * 2 + (u - 1))
                sp.dma_start(wraw[:, u * DM:(u + 1) * DM], src).then_inc(raw_full[u], 16)
        if nb % 2:
            load(Blk(nb - 1, 0))

    def split_hi(act, b):
        if isinstance(b.i, int) and num(b) >= nb:
            return
        s = slot(b)
        wait(act, raw_full[s], 16 * (b.c // 2 + 1 + b.i))
        wait(act, block_done, num(b) - 1)
        act.activation(wh[:, s * DM:(s + 1) * DM], wraw[:, s * DM:(s + 1) * DM], ACT.Copy).then_inc(hi_done, 1)

    def split_lo(pool, b):
        if isinstance(b.i, int) and num(b) >= nb:
            return
        s = slot(b)
        pool.wait_ge(hi_done, num(b) + 1)
        pool.tensor_tensor(wl[:, s * DM:(s + 1) * DM], wraw[:, s * DM:(s + 1) * DM],
                           wh[:, s * DM:(s + 1) * DM].bitcast(F32), ALU.subtract).then_inc(lo_done, 1)

    def products(pe, b, xh, xl, k):
        s = slot(b)
        pe.wait_ge(lo_done, num(b) + 1)
        wait(pe, acc_free, num(b) - 1)
        for h in range(2):
            n = 0
            for ws, x in ((wh, xh), (wl, xh), (wh, xl)):
                for kk in range(k):
                    mm = pe.matmul(ps[:, 2 * s + h, 0:HT], ws[:, s * DM + kk * P:s * DM + (kk + 1) * P],
                                   x[:, kk * T + h * HT:kk * T + (h + 1) * HT],
                                   start=(n == 0), stop=(n == 3 * k - 1))
                    n += 1
        mm.then_inc(block_done, 1)

    def pe_segment(pe, name, xh, xl):
        seg = SEGS[name]
        if name in ("ya", "yb", "wout") or name[:2] in ("dn", "do"):
            pe.wait_ge(post_done, before[name] + 2)
        blocks(pe, seg, lambda j, u, b: products(pe, b, xh, xl, seg.k), first=1 if seg.b0 == 0 else 0)

    def acc(b, rows=P):
        return pair_of(2 * slot(b), rows)

    def stage_at(u):
        return stage[:, u * T:(u + 1) * T]

    def pool_segment(pool, name):
        seg = SEGS[name]
        last = seg.b0 + seg.n == nb
        blocks(pool, seg, lambda j, u, b: split_lo(pool, nxt(b)), first=1 if seg.b0 == 0 else 0,
               last=1 if last else 0)

    def act_segment(act, name, out, func=ACT.Copy, posts=False, **more):
        seg = SEGS[name]
        last = seg.b0 + seg.n == nb
        if posts:
            act.wait_ge(post_done, before[name] + 2)

        def body(j, u, b):
            split_hi(act, nxt(b))
            act.wait_ge(block_done, num(b) + 1)
            if posts:
                act.wait_ge(post_done, before[name] + j + 1)
            act.activation(two(out(j, u)), acc(b), func, **more).then_inc(acc_free, 1)

        blocks(act, seg, body, last=1 if last else 0)

    def dve_segment(dve, name, post):
        seg = SEGS[name]

        def body(j, u, b):
            dve.wait_ge(acc_free, num(b) + 1)
            post(j, u).then_inc(post_done, 1)

        blocks(dve, seg, body)

    def split_store(dve, hi, lo, m, x):
        dve.tensor_scalar(tile_at(hi, m), x, 1.0, None, ALU.mult)
        dve.drain()
        return dve.tensor_tensor(tile_at(lo, m), x, tile_at(hi, m).bitcast(F32), ALU.subtract)

    def add_residual(dve):
        def post(j, u):
            return dve.tensor_tensor(tile_at(res, j), tile_at(res, j), stage_at(u), ALU.add)
        return post

    norms = {"pe": 0, "act": 0, "dve": 0, "pool": 0}
    applied = {"act": 0, "dve": 0, "pool": 0}

    def pe_norm(pe):
        k = norms["pe"]
        norms["pe"] += 1
        for m in range(KT):
            pe.wait_ge(nsq, KT * k + m + 1)
            for h in range(2):
                mm = pe.matmul(ps[:, 4 + h, 0:HT], ones[:, :], sq[m % 2][:, h * HT:(h + 1) * HT],
                               start=(m == 0), stop=(m == KT - 1))
            mm.then_inc(nused, 1)
        pe.drain().then_inc(nsum, 1)

    def act_norm(act):
        k = norms["act"]
        norms["act"] += 1

        def square(m, u):
            act.wait_ge(nused, KT * k + m + 1)
            act.activation(sq[u][:, :], tile_at(res, m), ACT.Square).then_inc(nsq, 1)

        tiles(act, KT, square)
        act.wait_ge(nsum, k + 1)
        act.activation(two(rstd[:, :]), pair_of(4), ACT.Sqrt, bias=eps[:, 0:1],
                       scale=1.0 / DM).then_inc(nroot, 1)

    def dve_norm(dve):
        k = norms["dve"]
        norms["dve"] += 1
        dve.wait_ge(nroot, k + 1)
        dve.reciprocal(rstd[:, :], rstd[:, :])
        dve.drain()

    def dve_norm_apply(dve, gi):
        a = applied["dve"]
        applied["dve"] += 1

        def scale(m, u):
            dve.wait_ge(nlo, KT * a + m + 1)
            dve.scalar_tensor_tensor(stage_at(u), tile_at(res, m), gains[:, bass.ds(m + gi * KT, 1)],
                                     rstd[:, :], ALU.mult, ALU.mult).then_inc(nscaled, 1)

        tiles(dve, KT, scale)

    def act_norm_apply(act, xh):
        a = applied["act"]
        applied["act"] += 1

        def hi(m, u):
            act.wait_ge(nscaled, KT * a + m + 1)
            act.activation(tile_at(xh, m), stage_at(u), ACT.Copy).then_inc(nhi, 1)

        tiles(act, KT, hi)

    def pool_norm_apply(pool, xh, xl):
        a = applied["pool"]
        applied["pool"] += 1

        def lo(m, u):
            pool.wait_ge(nhi, KT * a + m + 1)
            pool.tensor_tensor(tile_at(xl, m), stage_at(u), tile_at(xh, m).bitcast(F32),
                               ALU.subtract).then_inc(nlo, 1)

        tiles(pool, KT, lo)

    heads = {"pe": [0, 0], "act": [0, 0], "dve": [0, 0]}

    def count_heads(who, n):
        at_tile, call = heads[who]
        heads[who] = [at_tile + n, call + 1]
        return at_tile, call

    def pe_headnorm(pe, n, width):
        k, call = count_heads("pe", n)
        rows = 16
        if k:
            pe.wait_ge(happ, k + 2)
        for m in range(n):
            lhs = win128[:, 15 - m:31 - m] if width == P else win64[:, 14 - 2 * m:30 - 2 * m]
            pe.wait_ge(hsq, k + m + 1)
            for h in range(2):
                mm = pe.matmul(ps[0:rows, 4 + h, 0:HT], lhs, sq[m % 2][:, h * HT:(h + 1) * HT],
                               start=(m == 0), stop=(m == n - 1))
            mm.then_inc(hused, 1)
        pe.drain().then_inc(hsum, 1)
        pe.wait_ge(hiv, call + 1)
        for m in range(n):
            if width == P:
                lhs = ident[0:rows, m:m + 1].broadcast_to([rows, P])
            else:
                lhs = spread[:, m * P:(m + 1) * P]
            pe.wait_ge(happ, k + m + 1)
            for h in range(2):
                mm = pe.matmul(ps[:, 4 + 2 * (m % 2) + h, 0:HT], lhs, hinv[0:rows, h * HT:(h + 1) * HT],
                               start=True, stop=True)
            mm.then_inc(hbc, 1)

    def act_headnorm(act, buf, t0, n, width, scale):
        k, call = count_heads("act", n)
        rows = 16

        def square(m, u):
            act.wait_ge(hused, k + m + 1)
            act.activation(sq[u][:, :], tile_at(buf, m + t0), ACT.Square).then_inc(hsq, 1)

        tiles(act, n, square)
        act.wait_ge(hsum, call + 1)
        act.activation(two(hroot[0:rows, :]), pair_of(4, rows), ACT.Sqrt, bias=eps[0:rows, 0:1],
                       scale=scale).then_inc(hrt, 1)

    def dve_headnorm(dve, buf, t0, n, width, gain, rowscale=None):
        k, call = count_heads("dve", n)
        rows = 16
        dve.wait_ge(hrt, call + 1)
        if width != P:
            dve.tensor_copy(spread[:, :].rearrange("p (k n) -> p k n", n=64),
                            ident[0:rows, 0:16].unsqueeze(2).broadcast_to([rows, 16, 64]))
        last = dve.reciprocal(hinv[0:rows, :], hroot[0:rows, :])
        if rowscale is not None:
            dve.drain()
            last = dve.tensor_scalar(hinv[0:rows, :], hinv[0:rows, :], rowscale, None, ALU.mult)
        last.then_inc(hiv, 1)

        def apply(m, u):
            dve.wait_ge(hbc, k + m + 1)
            dve.scalar_tensor_tensor(two(tile_at(buf, m + t0)), two(tile_at(buf, m + t0)), gain,
                                     pair_of(4 + 2 * u), ALU.mult, ALU.mult).then_inc(happ, 1)

        tiles(dve, n, apply)

    softs = {"act": 0, "dve": 0}

    def act_softplus(act, y):
        softs["act"] += 1
        act.wait_ge(sp_abs, softs["act"])
        act.activation(sp[0][:, :], y, ACT.Abs)
        act.drain()
        act.activation(sp[1][:, :], sp[0][:, :], ACT.Exp, scale=-1.0).then_inc(sp_exp, 1)

    def dve_softplus(dve, out_, y):
        softs["dve"] += 1
        _, e, r, p, q = (t[:, :] for t in sp)
        dve.drain().then_inc(sp_abs, 1)
        dve.wait_ge(sp_exp, softs["dve"])
        dve.tensor_scalar(r, e, 2.0, None, ALU.add)
        dve.drain()
        dve.reciprocal(p, r)
        dve.drain()
        dve.tensor_tensor(e, e, p, ALU.mult)
        dve.drain()
        dve.tensor_tensor(q, e, e, ALU.mult)
        dve.drain()
        dve.tensor_scalar(p, q, 1.0 / 17, None, ALU.mult)
        for k in range(7, 0, -1):
            dve.drain()
            dve.scalar_tensor_tensor(p, p, 1.0 / (2 * k + 1), q, ALU.add, ALU.mult)
        dve.drain()
        dve.scalar_tensor_tensor(p, p, 1.0, e, ALU.add, ALU.mult)
        dve.tensor_scalar(r, y, 0.0, None, ALU.max)
        dve.drain()
        dve.scalar_tensor_tensor(out_, p, 2.0, r, ALU.mult, ALU.add)
        dve.drain()

    def act_qkv(act):
        def body(j, u, b):
            split_hi(act, nxt(b))
            act.wait_ge(block_done, num(b) + 1)
            act.wait_ge(conv_done, j + 1)
            act.activation(two(cpad[u][:, 2:2 + T]), acc(b), ACT.Copy).then_inc(acc_free, 1)
            if not isinstance(j, int) or j > 0:
                silu(j - 1, 1 - u)

        def silu(j, u):
            act.wait_ge(conv_done, j + 3)
            act.activation(tile_at(qkv, j), cout[u][:, :], ACT.Silu).then_inc(silu_done, 1)

        blocks(act, SEGS["qkv"], body, first=1)
        silu(23, 1)

    def dve_qkv(dve):
        for u in range(2):
            dve.memset(cpad[u][:, 0:2], 0.0)
            dve.memset(cpad[u][:, T + 2:T + 4], 0.0)
        dve.drain()

        def body(j, u, b):
            dve.wait_ge(acc_free, num(b) + 1)
            dve.wait_ge(silu_done, j + 1)
            o = cout[u][:, :]
            for k in range(5):
                tap = convw[:, bass.ds(j * 5 + k, 1)]
                if k == 0:
                    last = dve.tensor_scalar(o, cpad[u][:, 0:T], tap, None, ALU.mult)
                else:
                    dve.drain()
                    last = dve.scalar_tensor_tensor(o, cpad[u][:, k:k + T], tap, o, ALU.mult, ALU.add)
            last.then_inc(conv_done, 1)

        blocks(dve, SEGS["qkv"], body)

    def act_ba(act):
        b0, b1 = Blk(0, 0), Blk(1, 0)
        split_hi(act, b1)
        act.wait_ge(block_done, 1)
        act.activation(two(beta[:, :]), acc(b0, 16), ACT.Sigmoid).then_inc(acc_free, 1)
        split_hi(act, Blk(2, 0))
        act.wait_ge(block_done, 2)
        act.activation(two(gdec[:, :]), acc(b1, 16), ACT.Identity, bias=rowvec[:, 0:1]).then_inc(acc_free, 1)

    def dve_decay(dve):
        dve.wait_ge(acc_free, 2)
        dve_softplus(dve, gdec[:, :], gdec[:, :])
        dve.wait_ge(prep_act, 1)
        dve.tensor_scalar(gdec[:, :], gdec[:, :], rowvec[:, 4:5], -1.0, ALU.mult, ALU.mult).then_inc(prep_dve, 1)

    def pe_prep(pe):
        pe.wait_ge(prep_dve, 1)
        for c in range(NCH):
            pe.transpose(ps[0:C, 4, c * 16:(c + 1) * 16], gdec[:, c * C:(c + 1) * C], ident[0:16, 0:16])
            mm = pe.transpose(ps[0:C, 5, c * 16:(c + 1) * 16], beta[:, c * C:(c + 1) * C], ident[0:16, 0:16])
        mm.then_inc(prep_pe, 1)
        pe.wait_ge(prep_act, 3)
        for u in range(2):
            g = tok_g[:, :, 8 * u:8 * u + 8]
            pe.matmul(ps[0:C, 6, 48 * u:48 * u + 48].rearrange("p (c h) -> p c h", h=8), tri[:, u, :], g,
                      start=True, stop=True)
            mm = pe.matmul(ps[:, 7, 48 * u:48 * u + 48].rearrange("p (c h) -> p c h", h=8), ones[0:C, :], g,
                           start=True, stop=True)
            for c in range(NCH):
                mm = pe.matmul(ps[0:16, 2 * u + c // 3, (c % 3) * C:(c % 3 + 1) * C], tok_g[:, c, :],
                               tri[:, u, :], start=True, stop=True)
        mm.then_inc(prep_pe, 1)

    def act_prep(act):
        act.wait_ge(prep_pe, 1)
        act.activation(tok_g[:, :, :], ps[0:C, 4, 0:NCH * 16].rearrange("p (c h) -> p c h", h=16),
                       ACT.Copy).then_inc(prep_act, 1)
        act.activation(tok_b[:, :, :], ps[0:C, 5, 0:NCH * 16].rearrange("p (c h) -> p c h", h=16),
                       ACT.Copy).then_inc(prep_act, 1)
        act.wait_ge(prep_pe, 2)
        flat = ps[0:C, 6, 0:96].rearrange("p (u c h) -> p u (c h)", u=2, h=8)
        act.activation(tok_cum[:, :, :, :].rearrange("p u c h -> p u (c h)"), flat, ACT.Copy).then_inc(prep_act, 1)
        act.activation(tok_neg[:, :, :, :].rearrange("p u c h -> p u (c h)"), flat, ACT.Exp).then_inc(prep_act, 1)
        act.activation(chunk_decay[:, :, :, :].rearrange("p u c h -> p u (c h)"),
                       ps[:, 7, 0:96].rearrange("p (u c h) -> p u (c h)", u=2, h=8), ACT.Exp)
        for u in range(2):
            last = act.activation(two(scum[:, u, :]), pair_of(2 * u, 16), ACT.Copy)
        last.then_inc(prep_act, 1)
        act.wait_ge(prep_dve, 2)
        act.activation(tok_bk[:, :, :, :], tok_bk[:, :, :, :], ACT.Exp).then_inc(prep_act, 1)

    def dve_prep(dve):
        dve.wait_ge(prep_act, 6)
        flat = "p u c h -> p u (c h)"
        dve.tensor_scalar(tok_neg[:, :, :, :], tok_neg[:, :, :, :], -1.0, None, ALU.mult)
        dve.scalar_tensor_tensor(tok_bk[:, :, :, :].rearrange(flat), tok_cum[:, :, :, :].rearrange(flat), -1.0,
                                 ps[0:C, 7, 0:96].rearrange("p (u c h) -> p u (c h)", u=2, h=8),
                                 ALU.mult, ALU.add).then_inc(prep_dve, 1)
        dve.wait_ge(prep_act, 7)
        for u in range(2):
            dve.tensor_tensor(tok_bk[:, u, :, :], tok_bk[:, u, :, :], tok_b[:, :, 8 * u:8 * u + 8], ALU.mult)
        dve.memset(oacc[:, :], 0.0)

    NPE, NACT, NDVE, NPOOL = 3 + 2 * LEVELS + 4, 8 + LEVELS, 8 + LEVELS, 6 + LEVELS

    def delta_loop(e, body):
        with e.Fori(0, NG) as g:
            with e.Fori(0, NCH) as c:
                body(g, c, g * NCH + c)

    def chunk_of(u, c):
        return c if u == 0 else c * -1 + (NCH - 1)

    def heads4(t, n):
        return t[:, :].rearrange("p (r n) -> p r n", n=n)

    def pe_delta(pe):
        for u in range(2):
            pe.sem_inc(dpe[u], 1)

        def body(g, c, n):
            def on(u, who, k):
                s, per = {"act": (dact, NACT), "dve": (ddve, NDVE), "pool": (dpool, NPOOL)}[who]
                pe.wait_ge(s[u], n * per + (k + 1))

            def done(mm, u):
                mm.then_inc(dpe[u], 1)

            for u in range(2):
                d = delta[u]
                on(u, "pool", 4)
                on(u, "act", 0)
                for r in range(GH):
                    pe.transpose(ps[0:C, 4 * u, r * P:(r + 1) * P], d["ks"][:, r * C:(r + 1) * C], ident[:, :])
                for r in range(GH):
                    mm = pe.transpose(ps[0:C, 4 * u + 1, r * P:(r + 1) * P], d["vs"][:, r * C:(r + 1) * C],
                                      ident[:, :])
                done(mm, u)
            for u in range(2):
                d = delta[u]
                on(u, "dve", 0)
                for r in range(GH):
                    k = d["ks"][:, r * C:(r + 1) * C]
                    pe.matmul(ps[0:C, 4 * u + 2, r * C:(r + 1) * C], k, k, start=True, stop=True)
                mm = pe.matmul(ps[:, 4 * u + 3, 0:W4], ones[0:16, :], d["grow"][:, :], start=True, stop=True)
                done(mm, u)
            for u in range(2):
                d = delta[u]
                on(u, "act", 1)
                for r in range(GH):
                    mm = pe.matmul(ps[0:C, 4 * u, r * C:(r + 1) * C], d["ks"][:, r * C:(r + 1) * C],
                                   d["qs"][:, r * C:(r + 1) * C], start=True, stop=True)
                done(mm, u)
            for lv in range(LEVELS):
                for u in range(2):
                    d = delta[u]
                    on(u, "pool", 7 + lv)
                    on(u, "dve", 4 + lv)
                    for r in range(GH):
                        mm = pe.matmul(ps[0:C, 4 * u, r * C:(r + 1) * C], d["ob"][:, r * C:(r + 1) * C],
                                       d["xx"][:, r * C:(r + 1) * C], start=True, stop=True)
                    done(mm, u)
                for u in range(2):
                    d = delta[u]
                    on(u, "act", 5 + lv)
                    for r in range(GH):
                        sl = slice(r * C, (r + 1) * C)
                        pe.matmul(ps[0:C, 4 * u + 1, sl], d["xt"][:, sl], d["pp"][:, sl], start=True, stop=True)
                    for r in range(GH):
                        sl = slice(r * C, (r + 1) * C)
                        mm = pe.matmul(ps[0:C, 4 * u + 2, sl], d["pp"][:, sl], d["xt"][:, sl], start=True, stop=True)
                    done(mm, u)
            for u in range(2):
                d = delta[u]
                on(u, "dve", 4 + LEVELS)
                for r in range(GH):
                    mm = pe.matmul(ps[0:C, 4 * u, r * P:(r + 1) * P], d["ks"][:, r * C:(r + 1) * C],
                                   d["state"][:, r * P:(r + 1) * P], start=True, stop=True)
                done(mm, u)
            for u in range(2):
                d = delta[u]
                on(u, "dve", 5 + LEVELS)
                for r in range(GH):
                    mm = pe.matmul(ps[0:C, 4 * u + 1, r * P:(r + 1) * P], d["xt"][:, r * C:(r + 1) * C],
                                   d["rr"][:, r * P:(r + 1) * P], start=True, stop=True)
                done(mm, u)
            for u in range(2):
                d = delta[u]
                on(u, "pool", 6)
                on(u, "act", 8 + LEVELS)
                for r in range(GH):
                    o = ps[:, 4 * u + 2, r * C:(r + 1) * C]
                    pe.matmul(o, d["state"][:, r * P:(r + 1) * P], d["qd"][:, r * C:(r + 1) * C],
                              start=True, stop=False)
                    mm = pe.matmul(o, d["vn"][:, r * P:(r + 1) * P], d["qkm"][:, r * C:(r + 1) * C],
                                   start=False, stop=True)
                done(mm, u)
            for u in range(2):
                d = delta[u]
                on(u, "dve", 6 + LEVELS)
                for r in range(GH):
                    mm = pe.matmul(ps[:, 4 * u + 3, r * P:(r + 1) * P], d["kt"][:, r * P:(r + 1) * P],
                                   d["vk"][:, r * P:(r + 1) * P], start=True, stop=True)
                done(mm, u)

        delta_loop(pe, body)

    def pool_delta(pool):
        for u in range(2):
            pool.sem_inc(dpool[u], 1)
        q3 = qkv[:, :].rearrange("p (h t) -> p h t", t=T)

        def body(g, c, n):
            for u in range(2):
                d = delta[u]
                t0 = pool.snap(chunk_of(u, c) * C)
                h0 = pool.snap(g * GH)
                pool.wait_ge(dpe[u], n * NPE + 1)
                pool.tensor_tensor(heads4(d["grow"], C),
                                   scum[:, u, bass.ds(t0, C)].unsqueeze(1).broadcast_to([16, GH, C]),
                                   sel[:, u, bass.ds(g, 1), :].rearrange("p a r -> p (a r)").unsqueeze(2)
                                   .broadcast_to([16, GH, C]), ALU.mult).then_inc(dpool[u], 1)
                for name, t in (("ks", 8), ("vs", 16), ("qs", 0)):
                    pool.tensor_copy(heads4(d[name], C), q3[:, bass.ds(h0 + t, GH), bass.ds(t0, C)]
                                     ).then_inc(dpool[u], 1)
            for u in range(2):
                d = delta[u]
                pool.drain()
                pool.wait_ge(dact[u], n * NACT + 4)
                pool.tensor_tensor(d["qd"][:, :], d["qd"][:, :], d["qs"][:, :], ALU.mult).then_inc(dpool[u], 1)
            for u in range(2):
                d = delta[u]
                pool.wait_ge(ddve[u], n * NDVE + 3)
                pool.tensor_tensor(heads4(d["qkm"], C), heads4(d["qkm"], C),
                                   tri[:, u, :].unsqueeze(1).broadcast_to([C, GH, C]), ALU.mult
                                   ).then_inc(dpool[u], 1)
            for lv in range(LEVELS):
                for u in range(2):
                    d = delta[u]
                    if lv == 0:
                        pool.wait_ge(ddve[u], n * NDVE + 4)
                    else:
                        pool.wait_ge(dpe[u], n * NPE + (3 + 2 * lv))
                    pool.tensor_tensor(heads4(d["ob"], C), heads4(d["mt"], C),
                                       masks[:, u, lv, :].unsqueeze(1).broadcast_to([C, GH, C]), ALU.mult
                                       ).then_inc(dpool[u], 1)

        delta_loop(pool, body)

    def act_delta(act):
        for u in range(2):
            act.sem_inc(dact[u], 1)

        def body(g, c, n):
            for u in range(2):
                d = delta[u]
                act.wait_ge(dpe[u], n * NPE + 2)
                act.activation(d["kt"][:, :], ps[0:C, 4 * u, :], ACT.Copy).then_inc(dact[u], 1)
                act.activation(d["vt"][:, :], ps[0:C, 4 * u + 1, :], ACT.Copy).then_inc(dact[u], 1)
            for u in range(2):
                d = delta[u]
                act.wait_ge(dpe[u], n * NPE + 3)
                act.activation(d["qd"][:, :], ps[:, 4 * u + 3, 0:W4], ACT.Exp).then_inc(dact[u], 1)
            for u in range(2):
                d = delta[u]
                act.wait_ge(ddve[u], n * NDVE + 2)
                act.activation(d["dec"][:, :], d["dec"][:, :], ACT.Exp).then_inc(dact[u], 1)
            for lv in range(LEVELS):
                for u in range(2):
                    act.wait_ge(dpe[u], n * NPE + (5 + 2 * lv))
                    act.activation(delta[u]["pp"][:, :], ps[0:C, 4 * u, 0:W4], ACT.Copy).then_inc(dact[u], 1)
            for u in range(2):
                d = delta[u]
                act.wait_ge(dpe[u], n * NPE + (6 + 2 * LEVELS))
                cc = chunk_of(u, c)
                for r in range(GH):
                    act.activation(d["vn"][:, r * P:(r + 1) * P], ps[0:C, 4 * u + 1, r * P:(r + 1) * P], ACT.Copy,
                                   scale=tok_b[:, bass.ds(cc, 1), bass.ds(g * GH + (8 * u + r), 1)]
                                   .rearrange("p a b -> p (a b)")).then_inc(dact[u], 1)

        delta_loop(act, body)

    def dve_delta(dve):
        for u in range(2):
            dve.sem_inc(ddve[u], 1)
        o3 = oacc[:, :].rearrange("p (h t) -> p h t", t=T)

        def col(t, u, cc, h):
            return t[:, u, bass.ds(cc, 1), bass.ds(h, 1)].rearrange("p a b -> p (a b)")

        def body(g, c, n):
            ccs = [dve.snap(chunk_of(u, c)) for u in range(2)]
            tok0 = [dve.snap(ccs[u] * C) for u in range(2)]
            h0 = dve.snap(g * GH)
            for u in range(2):
                d = delta[u]
                cc = ccs[u]
                dve.wait_ge(dpe[u], n * NPE + 3)
                dve.wait_ge(dact[u], n * NACT + 4)
                for r in range(GH):
                    sl = slice(r * C, (r + 1) * C)
                    dve.tensor_scalar(d["dec"][:, sl], ps[0:C, 4 * u + 3, sl], col(tok_cum, u, cc, h0 + r),
                                      0.0, ALU.subtract, ALU.min)
                dve.drain().then_inc(ddve[u], 1)
            for u in range(2):
                d = delta[u]
                dve.wait_ge(dact[u], n * NACT + 5)
                dve.wait_ge(dpe[u], n * NPE + 4)
                dve.tensor_tensor(d["qkm"][:, :], ps[0:C, 4 * u, 0:W4], d["dec"][:, :], ALU.mult
                                  ).then_inc(ddve[u], 1)
                cc = ccs[u]
                for r in range(GH):
                    sl = slice(r * C, (r + 1) * C)
                    b = tok_b[:, bass.ds(cc, 1), bass.ds(h0 + (8 * u + r), 1)].rearrange("p a b -> p (a b)")
                    dve.scalar_tensor_tensor(d["mt"][:, sl], ps[0:C, 4 * u + 2, sl], b, d["dec"][:, sl],
                                             ALU.mult, ALU.mult)
                dve.drain().then_inc(ddve[u], 1)
                for x in ("xx", "xt"):
                    dve.tensor_copy(heads4(d[x], C), ident[0:C, 0:C].unsqueeze(1).broadcast_to([C, GH, C]))
                dve.drain().then_inc(ddve[u], 1)
            for lv in range(LEVELS):
                for u in range(2):
                    d = delta[u]
                    dve.wait_ge(dpe[u], n * NPE + (6 + 2 * lv))
                    dve.tensor_tensor(d["xx"][:, :], d["xx"][:, :], ps[0:C, 4 * u + 1, 0:W4], ALU.subtract)
                    dve.tensor_tensor(d["xt"][:, :], d["xt"][:, :], ps[0:C, 4 * u + 2, 0:W4], ALU.subtract)
                    dve.drain().then_inc(ddve[u], 1)
            for u in range(2):
                d = delta[u]
                dve.wait_ge(dpe[u], n * NPE + (5 + 2 * LEVELS))
                for r in range(GH):
                    sl = slice(r * P, (r + 1) * P)
                    dve.scalar_tensor_tensor(d["rr"][:, sl], ps[0:C, 4 * u, sl],
                                             col(tok_neg, u, ccs[u], h0 + r), d["vt"][:, sl],
                                             ALU.mult, ALU.add)
                dve.drain().then_inc(ddve[u], 1)
            for u in range(2):
                d = delta[u]
                dve.wait_ge(dpe[u], n * NPE + (6 + 2 * LEVELS))
                dve.wait_ge(dact[u], n * NACT + (9 + LEVELS))
                for r in range(GH):
                    sl = slice(r * P, (r + 1) * P)
                    dve.tensor_scalar(d["vk"][:, sl], ps[0:C, 4 * u + 1, sl],
                                      col(tok_bk, u, ccs[u], h0 + r), None, ALU.mult)
                dve.drain().then_inc(ddve[u], 1)
            for u in range(2):
                dve.wait_ge(dpe[u], n * NPE + (7 + 2 * LEVELS))
                o = o3[:, bass.ds(h0, GH), bass.ds(tok0[u], C)]
                dve.tensor_tensor(o, o, heads4(ps[:, 4 * u + 2, 0:W4], C), ALU.add)
                dve.drain().then_inc(ddve[u], 1)
            for u in range(2):
                d = delta[u]
                dve.wait_ge(dpe[u], n * NPE + (8 + 2 * LEVELS))
                for r in range(GH):
                    sl = slice(r * P, (r + 1) * P)
                    dve.scalar_tensor_tensor(d["state"][:, sl], d["state"][:, sl],
                                             col(chunk_decay, u, ccs[u], h0 + r),
                                             ps[:, 4 * u + 3, sl], ALU.mult, ALU.add)
                dve.drain().then_inc(ddve[u], 1)

        with dve.Fori(0, NG) as g:
            for u in range(2):
                dve.memset(delta[u]["state"][:, :], 0.0)
            dve.drain()
            with dve.Fori(0, NCH) as c:
                body(g, c, g * NCH + c)

    def act_sc(act):
        b0 = SEGS["sc"].b0
        act.wait_ge(post_done, before["sc"] + 2)
        with act.Fori(0, 4) as i:
            for v in range(6):
                b = Blk(b0 + v, i * 3)
                split_hi(act, nxt(b))
                act.wait_ge(block_done, num(b) + 1)
                if v % 3 == 0:
                    act.wait_ge(post_done, i * 2 + (before["sc"] + v // 3 + 2))
                o = (bst[:, :], stage_at(0), stage_at(1))[v % 3]
                act.activation(two(o), acc(b), ACT.Copy).then_inc(acc_free, 1)

    def dve_sc(dve):
        b0 = SEGS["sc"].b0
        dve.memset(pc[:, 0:1], 0.0)
        dve.memset(pc[:, T + 1:T + 2], 0.0)
        with dve.Fori(0, 4) as i:
            for v in range(2):
                m = i * 2 + v
                dve.drain()
                dve.wait_ge(acc_free, i * 6 + (b0 + 3 * v + 3))
                dve.tensor_tensor(pc[:, 1:T + 1], stage_at(0), stage_at(1), ALU.mult)
                dve.drain()
                o = stage_at(0)
                for k in range(3):
                    tap = scw[:, bass.ds(m * 3 + k, 1)]
                    if k == 0:
                        dve.tensor_scalar(o, pc[:, 0:T], tap, None, ALU.mult)
                    else:
                        dve.scalar_tensor_tensor(o, pc[:, k:k + T], tap, o, ALU.mult, ALU.add)
                    dve.drain()
                dve.tensor_tensor(tile_at(scy, m), o, bst[:, :], ALU.mult).then_inc(post_done, 1)

    def dve_z(dve):
        def post(j, u):
            x = stage_at(u)
            dve.tensor_tensor(x, x, tile_at(oacc, j), ALU.mult)
            dve.drain()
            return split_store(dve, xbh, xbl, j, x)
        dve_segment(dve, "z", post)

    def dve_ya(dve):
        def post(j, u):
            split_store(dve, xah, xal, j, tile_at(scy, j))
            return dve.tensor_tensor(tile_at(gab, j), tile_at(gab, j), stage_at(u), ALU.mult)
        dve_segment(dve, "ya", post)

    def dve_yb(dve):
        def post(j, u):
            x = stage_at(u)
            dve.tensor_tensor(x, x, tile_at(gab, j + 8), ALU.mult)
            dve.drain()
            dve.tensor_tensor(x, x, tile_at(gab, j), ALU.add)
            dve.drain()
            return split_store(dve, xbh, xbl, j, x)
        dve_segment(dve, "yb", post)

    def act_gated(act, name):
        seg = SEGS[name]
        act.wait_ge(post_done, before[name] + 2)
        with act.Fori(0, seg.n // 2) as i:
            for u in range(2):
                b = Blk(seg.b0 + u, i)
                split_hi(act, nxt(b))
                act.wait_ge(block_done, num(b) + 1)
                if u == 0:
                    act.wait_ge(post_done, i + (before[name] + 2))
                act.activation(two(stage_at(u)), acc(b), ACT.Silu if u == 0 else ACT.Copy).then_inc(acc_free, 1)

    def dve_gated(dve, name):
        seg = SEGS[name]
        with dve.Fori(0, seg.n // 2) as m:
            dve.wait_ge(acc_free, m * 2 + (seg.b0 + 2))
            dve.tensor_tensor(stage_at(0), stage_at(0), stage_at(1), ALU.mult)
            dve.drain()
            split_store(dve, xbh, xbl, m, stage_at(0)).then_inc(post_done, 1)

    def dve_relu2(dve, name):
        def post(j, u):
            x = stage_at(u)
            dve.tensor_tensor(x, x, x, ALU.mult)
            dve.drain()
            return split_store(dve, xbh, xbl, j, x)
        dve_segment(dve, name, post)

    ropes = {"pe": 0, "dve": 0}
    vts = {"pe": 0, "act": 0}
    vt2 = place("vtok_dsa", [C, NCH, 256], F32, phase_at + 24 * F)

    def tiles_odd(e, n, body):
        tiles(e, n, body)
        if n % 2:
            body(n - 1, 0)

    def pe_rope(pe, t0, n):
        k = ropes["pe"]
        ropes["pe"] += n

        def turn(m, u):
            pe.wait_ge(rope_dve, k + m + 1)
            for h in range(2):
                mm = pe.matmul(bank(4 + 2 * u + h), rot[:, :], tile_at(pf, m + t0, HT, h * HT),
                               start=True, stop=True)
            mm.then_inc(rope_pe, 1)

        tiles_odd(pe, n, turn)

    def dve_rope(dve, t0, n):
        k = ropes["dve"]
        ropes["dve"] += n

        def apply(m, u):
            x = tile_at(pf, m + t0)
            dve.drain()
            dve.wait_ge(rope_pe, k + m + 1)
            dve.tensor_tensor(x, x, cossin[:, 0, :], ALU.mult)
            dve.tensor_tensor(two(sq[u][:, :]), pair_of(4 + 2 * u), two(cossin[:, 1, :]), ALU.mult)
            dve.drain()
            dve.tensor_tensor(x, x, sq[u][:, :], ALU.add).then_inc(rope_dve, 1)

        tiles_odd(dve, n, apply)

    def act_vtok(act, t0, n, dst):
        k = vts["act"]
        vts["act"] += n

        def move(m, u):
            act.wait_ge(vt_pe, k + m + 1)
            act.activation(stage_at(u), tile_at(pf, m + t0), ACT.Copy).then_inc(vt_in, 1)
            act.wait_ge(vt_pe, k + m + 3)
            for h in range(2):
                last = act.activation(dst[:, 3 * h:3 * h + 3, bass.ds(m * P, P)],
                                      ps[0:C, 4 + 2 * u + h, 0:3 * P].rearrange("p (c n) -> p c n", n=P), ACT.Copy)
            last.then_inc(vt_out, 1)

        tiles(act, n, move)

    def pe_vtok(pe, n):
        k = vts["pe"]
        vts["pe"] += n

        def turn(m, u):
            pe.wait_ge(vt_in, k + m + 1)
            pe.wait_ge(vt_out, k + m + 1)
            for c in range(NCH):
                mm = pe.transpose(ps[0:C, 4 + 2 * u + c // 3, (c % 3) * P:(c % 3 + 1) * P],
                                  stage[:, u * T + c * C:u * T + (c + 1) * C], ident[:, :])
            mm.then_inc(vt_pe, 1)

        tiles(pe, n, turn)

    IX = 2 * (NCH - 1)

    def index_loop(e, body):
        with e.Fori(0, 4) as m:
            body(m)

    def zero_halves(pool):
        pool.memset(qz[64:P, 0, :], 0.0)
        pool.memset(qz[0:64, 1, :], 0.0)

    def heads_apart(pool, x):
        pool.tensor_copy(qz[0:64, 0, :], x[0:64])
        return pool.tensor_copy(qz[64:P, 1, :], x[64:P])

    def pool_index(pool):
        def body(m):
            x = tile_at(pf, pool.snap(m + 12))
            pool.wait_ge(ix_pe, m * IX + 2)
            heads_apart(pool, x).then_inc(ix_q, 1)
        zero_halves(pool)
        index_loop(pool, body)

    def pe_index(pe):
        pe.sem_inc(ix_pe, 2)

        def body(m):
            pe.wait_ge(ix_q, m + 1)
            for k in range(IX):
                hh, t = divmod(k, NCH - 1)
                n = C * (t + 2)
                pe.wait_ge(ix_act, m * IX + (k + 1))
                for x, (o, c) in enumerate(pieces(n)):
                    mm = pe.matmul(ps[0:C, 2 * (k % 2) + x, 0:c],
                                   qz[:, hh, C * (t + 1):C * (t + 2)],
                                   pf[:, 16 * T + o:16 * T + o + c], start=True, stop=True)
                mm.then_inc(ix_pe, 1)
        index_loop(pe, body)

    def psum_cols(b, rows, n):
        return ps[0:rows, b, 0:n] if n <= 512 else pair_of(b, rows)

    def as_psum(ap, n):
        return ap if n <= 512 else two(ap)

    def act_index(act):
        act.sem_inc(ix_act, 2)

        def body(m):
            for k in range(IX):
                n = C * (k % (NCH - 1) + 2)
                act.wait_ge(ix_pe, m * IX + (k + 3))
                act.wait_ge(ix_dve, m * IX + (k + 1))
                act.activation(as_psum(score[k % 2][:, 0:n], n), psum_cols(2 * (k % 2), C, n),
                               ACT.Relu).then_inc(ix_act, 1)
        index_loop(act, body)

    def dve_index(dve):
        for t in range(1, NCH):
            dve.memset(bias[:, t, 0:C * (t + 1)], 0.0)
        dve.sem_inc(ix_dve, 2)

        def body(m):
            for k in range(IX):
                hh, t = divmod(k, NCH - 1)
                t += 1
                n = C * (t + 1)
                if k % (NCH - 1) == 0:
                    dve.drain()
                    head = dve.snap(m * 2 + hh)
                dve.wait_ge(ix_act, m * IX + (k + 3))
                dve.scalar_tensor_tensor(bias[:, t, 0:n], score[k % 2][:, 0:n],
                                         wit[:, t, bass.ds(head, 1)], bias[:, t, 0:n],
                                         ALU.mult, ALU.add).then_inc(ix_dve, 1)
        index_loop(dve, body)

    def dve_topk(dve):
        dve.drain()
        for t in range(1, NCH):
            n = C * (t + 1)
            dve.scalar_tensor_tensor(bias[:, t, n - C:n], causal[:, :], LOWEST / NEG, bias[:, t, n - C:n],
                                     ALU.mult, ALU.add)
        dve.drain()
        for t in range(1, NCH):
            dve.tensor_copy(work[:, t * T:t * T + C * (t + 1)], bias[:, t, 0:C * (t + 1)])
        dve.drain()
        with dve.Fori(0, TOPK // 8):
            for t in range(1, NCH):
                dve.max(top8[:, 8 * t:8 * t + 8], work[:, t * T:t * T + C * (t + 1)])
            dve.drain()
            for t in range(1, NCH):
                x = work[:, t * T:t * T + C * (t + 1)]
                dve.match_replace(x, top8[:, 8 * t:8 * t + 8], x, LOWEST)
            dve.drain()
        for t in range(1, NCH):
            n = C * (t + 1)
            dve.tensor_tensor(bias[:, t, 0:n], work[:, t * T:t * T + n], bias[:, t, 0:n], ALU.is_equal)
        dve.drain()
        for t in range(1, NCH):
            dve.tensor_scalar(bias[:, t, 0:C * (t + 1)], bias[:, t, 0:C * (t + 1)], NEG, None, ALU.mult)
        dve.tensor_copy(bias[:, 0, 0:C], causal[:, :])

    UN = 2 * NCH
    calls = {"pe": 0, "act": 0, "dve": 0, "pool": 0}

    def att_loop(e, who, body):
        call = calls[who]
        calls[who] += 1
        with e.Fori(0, 2) as a:
            with e.Fori(0, 4) as r:
                m = a * 4 + r
                body(a, m, m + 8 * call)

    def pool_attention(pool, fox):
        def body(a, m, g):
            x = tile_at(pf, pool.snap(m + (16 if fox else 0)))
            pool.wait_ge(at_s, g * UN + 2)
            heads_apart(pool, x).then_inc(at_q, 1)
            if fox:
                for hh in range(2):
                    head = pool.snap(m * 2 + hh)
                    pool.wait_ge(at_hb, m * 2 + (hh + 1))
                    pool.tensor_tensor(cneg[:, :], lfneg[:, :], ident[0:16, bass.ds(head, 1)]
                                       .broadcast_to([16, T]), ALU.mult).then_inc(at_cn, 1)
        zero_halves(pool)
        att_loop(pool, "pool", body)

    def pe_attention(pe, fox):
        v = vtok if fox else vt2
        if not fox:
            for ring in (at_s, at_pt, at_o):
                pe.sem_inc(ring, 2)
        else:
            pe.sem_inc(at_hb, 1)

        def body(a, m, g):
            def scores(k):
                hh, t = divmod(k, NCH)
                n = C * (t + 1)
                pe.wait_ge(at_sc, g * UN + (k + 1))
                kt_ = m if fox else a + 8
                for x, (o, c) in enumerate(pieces(n)):
                    mm = pe.matmul(ps[0:C, 2 * (k % 2) + x, 0:c],
                                   qz[:, hh, t * C:(t + 1) * C],
                                   pf[:, bass.ds(kt_ * T + o, c)], start=True, stop=True)
                mm.then_inc(at_s, 1)

            def turn(k):
                t = k % NCH
                pe.wait_ge(at_p, g * UN + (k + 1))
                pe.wait_ge(at_pte, g * UN + (k + 1))
                for kb in range(t + 1):
                    mm = pe.transpose(ps[0:C, 4 + kb // 3, (kb % 3) * C:(kb % 3 + 1) * C],
                                      prob[k % 2][:, kb * C:(kb + 1) * C], ident[0:C, 0:C])
                mm.then_inc(at_pt, 1)

            def values(k):
                hh, t = divmod(k, NCH)
                pe.wait_ge(at_pte, g * UN + (k + 2))
                if k >= 2:
                    pe.wait_ge(at_oe, g * UN + (k - 1))
                for kb in range(t + 1):
                    mm = pe.matmul(ps[0:C, 6 + k % 2, t * 64:(t + 1) * 64], ptr[k % 2][:, kb * C:(kb + 1) * C],
                                   v[:, kb, bass.ds((m if fox else a) * P + 64 * hh, 64)],
                                   start=(kb == 0), stop=(kb == t))
                mm.then_inc(at_o, 1)

            pe.wait_ge(at_of, g + 1)
            if fox:
                for hh in range(2):
                    pe.wait_ge(at_cn, m * 2 + (hh + 1))
                    pe.wait_ge(at_hbe, m * 2 + (hh + 1))
                    for h in range(2):
                        mm = pe.matmul(ps[0:C, 4 + h, 0:HT], ones[0:16, 0:C], cneg[:, h * HT:(h + 1) * HT],
                                       start=True, stop=True)
                    mm.then_inc(at_hb, 1)
                pe.wait_ge(at_hbe, m * 2 + 3)
            pe.wait_ge(at_q, g + 1)
            scores(0)
            scores(1)
            for k in range(UN):
                turn(k)
                if k + 2 < UN:
                    scores(k + 2)
                if k:
                    values(k - 1)
            values(UN - 1)
            pe.wait_ge(at_oe, g * UN + UN)
            for t in range(NCH):
                mm = pe.transpose(ps[:, 4 + t // 3, (t % 3) * C:(t % 3 + 1) * C], otok[:, t * P:(t + 1) * P],
                                  ident[0:C, 0:C])
            mm.then_inc(at_ot, 1)

        att_loop(pe, "pe", body)

    def act_attention(act, fox):
        if not fox:
            act.sem_inc(at_pte, 1)
        else:
            act.sem_inc(at_hbe, 1)

        def body(a, m, g):
            def exp(k):
                n = C * (k % NCH + 1)
                act.wait_ge(at_mx, g * UN + (k + 1))
                act.wait_ge(at_pt, g * UN + (k + 1))
                act.activation(prob[k % 2][:, 0:n], score[k % 2][:, 0:n], ACT.Exp, bias=rowmax[:, k:k + 1],
                               accum_out=rowsum[:, k:k + 1]).then_inc(at_p, 1)

            def out(k):
                t = k % NCH
                n = C * (t + 1)
                act.wait_ge(at_pt, g * UN + (k + 3))
                act.wait_ge(at_o, g * UN + (k + 1))
                if t < 3:
                    act.activation(ptr[k % 2][:, 0:n], ps[0:C, 4, 0:n], ACT.Copy).then_inc(at_pte, 1)
                else:
                    act.activation(ptr[k % 2][:, 0:HT], ps[0:C, 4, 0:HT], ACT.Copy)
                    act.activation(ptr[k % 2][:, HT:n], ps[0:C, 5, 0:n - HT], ACT.Copy).then_inc(at_pte, 1)

            if fox:
                for hh in range(2):
                    act.wait_ge(at_hb, m * 2 + (hh + 2))
                    act.activation(two(hbias[hh][:, :]), pair_of(4, C), ACT.Copy).then_inc(at_hbe, 1)
            for k in range(UN):
                exp(k)
                out(k)

        att_loop(act, "act", body)

    def dve_attention(dve, fox):
        if not fox:
            dve.sem_inc(at_sc, 2)
            dve.sem_inc(at_of, 1)

        def body(a, m, g):
            def soft(k):
                hh, t = divmod(k, NCH)
                n = C * (t + 1)
                dve.wait_ge(at_s, g * UN + (k + 3))
                if k > 1:
                    dve.wait_ge(at_p, g * UN + (k - 1))
                s = score[k % 2][:, 0:n]
                if fox and k % NCH == 0:
                    dve.wait_ge(at_hbe, m * 2 + (hh + 2))
                b = hbias[hh][:, 0:n] if fox else bias[:, t, 0:n]
                dve.scalar_tensor_tensor(as_psum(s, n), psum_cols(2 * (k % 2), C, n), 0.125, as_psum(b, n),
                                         ALU.mult, ALU.add).then_inc(at_sc, 1)
                dve.drain()
                if fox:
                    dve.tensor_tensor(score[k % 2][:, n - C:n], score[k % 2][:, n - C:n], causal[:, :], ALU.add)
                    dve.drain()
                dve.tensor_reduce(rowmax[:, k:k + 1], s, AX.X, ALU.max, negate=True).then_inc(at_mx, 1)

            def out(k):
                hh, t = divmod(k, NCH)
                dve.wait_ge(at_o, g * UN + (k + 3))
                dve.reciprocal(rowinv[:, k:k + 1], rowsum[:, k:k + 1])
                dve.drain()
                dve.tensor_scalar(otok[:, t * P + 64 * hh:t * P + 64 * hh + 64],
                                  ps[0:C, 6 + k % 2, t * 64:(t + 1) * 64], rowinv[:, k:k + 1], None,
                                  ALU.mult).then_inc(at_oe, 1)

            for k in range(UN):
                soft(k)
                if k >= 2:
                    out(k - 2)
            out(UN - 2)
            out(UN - 1)
            dve.wait_ge(at_ot, g + 1)
            dve.tensor_scalar(two(tile_at(xbh, m)), pair_of(4), 1.0, None, ALU.mult)
            dve.drain()
            dve.tensor_tensor(two(tile_at(xbl, m)), pair_of(4), two(tile_at(xbh, m).bitcast(F32)),
                              ALU.subtract)
            dve.drain().then_inc(at_of, 1)

        att_loop(dve, "dve", body)

    def pe_wit(pe):
        for c in range(NCH):
            mm = pe.transpose(ps[0:C, 0, c * 8:(c + 1) * 8], wi[:, c * C:(c + 1) * C], ident[0:8, 0:8])
        mm.then_inc(wit_pe, 1)

    def act_wit(act):
        act.wait_ge(wit_pe, 1)
        act.activation(wit[:, :, :], ps[0:C, 0, 0:NCH * 8].rearrange("p (c h) -> p c h", h=8), ACT.Copy)

    def act_dsa(act):
        def body(j, u, b):
            split_hi(act, nxt(b))
            act.wait_ge(block_done, num(b) + 1)
            if isinstance(j, int) and j == 17:
                act.activation(two(wi[:, :]), acc(b, 8), ACT.Copy, scale=8 ** -0.5 * 64 ** -0.5).then_inc(acc_free, 1)
            else:
                act.activation(two(tile_at(pf, j)), acc(b), ACT.Copy).then_inc(acc_free, 1)
        blocks(act, SEGS["dsa"], body, last=1)

    def act_foxf(act):
        b = Blk(SEGS["foxf"].b0, 0)
        split_hi(act, nxt(b))
        act.wait_ge(block_done, num(b) + 1)
        act.activation(two(lfneg[:, :]), acc(b, 16), ACT.Copy).then_inc(acc_free, 1)

    def dve_forget(dve):
        dve.tensor_scalar(lfneg[:, :], lfneg[:, :], rowvec[:, 2:3], -1.0, ALU.add, ALU.mult)
        dve.drain()
        dve_softplus(dve, cneg[:, :], lfneg[:, :])
        dve.memset(sp[0][:, :], 1.0)
        dve.drain()
        dve.tensor_tensor_scan(lfneg[:, :], sp[0][:, :], cneg[:, :], 0.0, ALU.mult, ALU.add)

    def up(j, u):
        return stage_at(u)

    consts = (
        (res[:, :].rearrange("p (k t) -> p k t", t=T), io["x"].rearrange("k p t -> p k t")),
        (gains[:, :], io["gains"]), (headgain[:, 0:5], io["headgain"]), (rowvec[:, 0:4], io["rowvec"]),
        (ident[:, :], io["ident"]), (win128[:, :], io["win128"]), (win64[:, :], io["win64"]),
        (convw[:, :], io["convw"]), (scw[:, :], io["scw"]), (tri[:, :, :], io["tri"]),
        (masks[:, :, :, :], io["masks"]), (sel[:, :, :, :], io["sel"]))

    def loaded(e):
        e.wait_ge(const_in, 16 * len(consts))

    with nc.Block() as block:
        @block.tensor
        def _(pe):
            loaded(pe)
            for ring in (nused, hused, vt_pe):
                pe.sem_inc(ring, 2)
            pe.wait_ge(prep_dve_ones, 1)
            pe_norm(pe)
            barrier(pe, "pe")
            pe_segment(pe, "ba", xah, xal)
            pe_segment(pe, "qkv", xah, xal)
            pe_headnorm(pe, 16, P)
            barrier(pe, "pe")
            pe_prep(pe)
            barrier(pe, "pe")
            pe_delta(pe)
            barrier(pe, "pe")
            pe_headnorm(pe, 8, P)
            barrier(pe, "pe")
            pe_segment(pe, "z", xah, xal)
            pe_segment(pe, "sc", xah, xal)
            pe_segment(pe, "gates", xah, xal)
            pe_segment(pe, "ya", xbh, xbl)
            pe_segment(pe, "yb", xah, xal)
            pe_segment(pe, "wout", xbh, xbl)
            barrier(pe, "pe")
            pe_norm(pe)
            barrier(pe, "pe")
            for p in range(len(FF1_PARTS)):
                pe_segment(pe, f"gu{p}", xah, xal)
                pe_segment(pe, f"dn{p}", xbh, xbl)
            barrier(pe, "pe")
            pe_norm(pe)
            barrier(pe, "pe")
            barrier(pe, "pe")
            pe_norm(pe)
            barrier(pe, "pe")
            pe_segment(pe, "dsa", xah, xal)
            barrier(pe, "pe")
            pe_headnorm(pe, 8, 64)
            pe_headnorm(pe, 2, 64)
            barrier(pe, "pe")
            pe_rope(pe, 0, 10)
            pe_rope(pe, 12, 5)
            barrier(pe, "pe")
            pe_vtok(pe, 2)
            pe_wit(pe)
            barrier(pe, "pe")
            pe_index(pe)
            barrier(pe, "pe")
            pe_attention(pe, False)
            barrier(pe, "pe")
            pe_segment(pe, "dsa_out", xbh, xbl)
            barrier(pe, "pe")
            pe_norm(pe)
            barrier(pe, "pe")
            for p in range(len(FF2_PARTS)):
                pe_segment(pe, f"up0_{p}", xah, xal)
                pe_segment(pe, f"down0_{p}", xbh, xbl)
            barrier(pe, "pe")
            pe_norm(pe)
            barrier(pe, "pe")
            pe_segment(pe, "foxkv", xah, xal)
            pe_segment(pe, "foxf", xah, xal)
            pe_segment(pe, "foxq", xbh, xbl)
            barrier(pe, "pe")
            pe_headnorm(pe, 8, 64)
            pe_headnorm(pe, 8, 64)
            barrier(pe, "pe")
            pe_vtok(pe, 8)
            barrier(pe, "pe")
            pe_attention(pe, True)
            barrier(pe, "pe")
            pe_segment(pe, "fox_out", xbh, xbl)
            barrier(pe, "pe")
            pe_norm(pe)
            barrier(pe, "pe")
            for p in range(len(FF2_PARTS)):
                pe_segment(pe, f"up1_{p}", xah, xal)
                pe_segment(pe, f"down1_{p}", xbh, xbl)
            barrier(pe, "pe")

        @block.scalar
        def _(act):
            loaded(act)
            for ring in (silu_done, vt_out):
                act.sem_inc(ring, 2)
            act.wait_ge(prep_dve_ones, 1)
            act_norm(act)
            act_norm_apply(act, xah)
            split_hi(act, Blk(0, 0))
            barrier(act, "act")
            act_ba(act)
            act_qkv(act)
            act.activation(rowvec[:, 4:5], rowvec[:, 1:2], ACT.Exp).then_inc(prep_act, 1)
            act_softplus(act, gdec[:, :])
            act_headnorm(act, qkv, 0, 16, P, 1.0)
            barrier(act, "act")
            act_prep(act)
            barrier(act, "act")
            act_delta(act)
            barrier(act, "act")
            act_headnorm(act, oacc, 0, 8, P, 1.0 / P)
            barrier(act, "act")
            act_segment(act, "z", up, ACT.Silu, posts=True)
            act_sc(act)
            act_segment(act, "gates", lambda j, u: tile_at(gab, j), ACT.Sigmoid)
            for name in ("ya", "yb", "wout"):
                act_segment(act, name, up, posts=True)
            barrier(act, "act")
            act_norm(act)
            act_norm_apply(act, xah)
            barrier(act, "act")
            for p in range(len(FF1_PARTS)):
                act_gated(act, f"gu{p}")
                act_segment(act, f"dn{p}", up, posts=True)
            barrier(act, "act")
            act_norm(act)
            barrier(act, "act")
            for dst, src in ((res[:, :].rearrange("p (k t) -> p k t", t=T)[:, :, 0:NMETA],
                              io["meta2"].rearrange("k p t -> p k t")),
                             (causal[:, :], io["causal"]), (cossin[:, :, :], io["cossin"]), (rot[:, :], io["rot"])):
                act.dma_start(dst, src).then_inc(const2_in, 16)
            act.wait_ge(const2_in, 64)
            barrier(act, "act")
            act_norm(act)
            act_norm_apply(act, xah)
            barrier(act, "act")
            act_dsa(act)
            barrier(act, "act")
            act_headnorm(act, pf, 0, 8, 64, 1.0 / 64)
            act_headnorm(act, pf, 8, 2, 64, 1.0 / 64)
            barrier(act, "act")
            barrier(act, "act")
            act_vtok(act, 10, 2, vt2)
            act_wit(act)
            barrier(act, "act")
            act_index(act)
            barrier(act, "act")
            act_attention(act, False)
            barrier(act, "act")
            act_segment(act, "dsa_out", up, posts=True)
            barrier(act, "act")
            act_norm(act)
            act_norm_apply(act, xah)
            barrier(act, "act")
            for p in range(len(FF2_PARTS)):
                act_segment(act, f"up0_{p}", up, ACT.Relu, posts=True)
                act_segment(act, f"down0_{p}", up, posts=True)
            barrier(act, "act")
            act_norm(act)
            act_norm_apply(act, xah)
            act_norm_apply(act, xbh)
            barrier(act, "act")
            act_segment(act, "foxkv", lambda j, u: tile_at(pf, j))
            act_foxf(act)
            act_segment(act, "foxq", lambda j, u: tile_at(pf, j + 16))
            barrier(act, "act")
            act_softplus(act, lfneg[:, :])
            act_headnorm(act, pf, 0, 8, 64, 1.0 / 64)
            act_headnorm(act, pf, 16, 8, 64, 1.0 / 64)
            barrier(act, "act")
            act_vtok(act, 8, 8, vtok)
            barrier(act, "act")
            act_attention(act, True)
            barrier(act, "act")
            act_segment(act, "fox_out", up, posts=True)
            barrier(act, "act")
            act_norm(act)
            act_norm_apply(act, xah)
            barrier(act, "act")
            for p in range(len(FF2_PARTS)):
                act_segment(act, f"up1_{p}", up, ACT.Relu, posts=True)
                act_segment(act, f"down1_{p}", up, posts=True)
            barrier(act, "act")

        @block.vector
        def _(dve):
            for ring in (post_done, conv_done, happ, rope_dve):
                dve.sem_inc(ring, 2)
            dve.memset(ones[:, :], 1.0)
            dve.memset(eps[:, :], EPS)
            dve.drain().then_inc(prep_dve_ones, 1)
            loaded(dve)
            dve_norm(dve)
            dve_norm_apply(dve, 0)
            barrier(dve, "dve")
            dve_qkv(dve)
            dve_decay(dve)
            dve_headnorm(dve, qkv, 0, 16, P, 1.0, rowvec[:, 3:4])
            barrier(dve, "dve")
            dve_prep(dve)
            barrier(dve, "dve")
            dve_delta(dve)
            barrier(dve, "dve")
            dve_headnorm(dve, oacc, 0, 8, P, headgain[:, 0:1])
            barrier(dve, "dve")
            dve_z(dve)
            dve_sc(dve)
            dve_ya(dve)
            dve_yb(dve)
            dve_segment(dve, "wout", add_residual(dve))
            barrier(dve, "dve")
            dve_norm(dve)
            dve_norm_apply(dve, 1)
            barrier(dve, "dve")
            for p in range(len(FF1_PARTS)):
                dve_gated(dve, f"gu{p}")
                dve_segment(dve, f"dn{p}", add_residual(dve))
            barrier(dve, "dve")
            dve_norm(dve)
            tiles(dve, KT, lambda m, u: dve.scalar_tensor_tensor(
                tile_at(res, m), tile_at(res, m), gains[:, bass.ds(m + 2 * KT, 1)], rstd[:, :],
                ALU.mult, ALU.mult))
            barrier(dve, "dve")
            barrier(dve, "dve")
            dve_norm(dve)
            dve_norm_apply(dve, 3)
            barrier(dve, "dve")
            barrier(dve, "dve")
            dve_headnorm(dve, pf, 0, 8, 64, headgain[:, 1:2])
            dve_headnorm(dve, pf, 8, 2, 64, headgain[:, 2:3])
            barrier(dve, "dve")
            dve_rope(dve, 0, 10)
            dve_rope(dve, 12, 5)
            barrier(dve, "dve")
            barrier(dve, "dve")
            dve_index(dve)
            dve_topk(dve)
            barrier(dve, "dve")
            dve_attention(dve, False)
            barrier(dve, "dve")
            dve_segment(dve, "dsa_out", add_residual(dve))
            barrier(dve, "dve")
            dve_norm(dve)
            dve_norm_apply(dve, 4)
            barrier(dve, "dve")
            for p in range(len(FF2_PARTS)):
                dve_relu2(dve, f"up0_{p}")
                dve_segment(dve, f"down0_{p}", add_residual(dve))
            barrier(dve, "dve")
            dve_norm(dve)
            dve_norm_apply(dve, 5)
            dve_norm_apply(dve, 6)
            barrier(dve, "dve")
            barrier(dve, "dve")
            dve_forget(dve)
            dve_headnorm(dve, pf, 0, 8, 64, headgain[:, 3:4])
            dve_headnorm(dve, pf, 16, 8, 64, headgain[:, 4:5])
            barrier(dve, "dve")
            barrier(dve, "dve")
            dve_attention(dve, True)
            barrier(dve, "dve")
            dve_segment(dve, "fox_out", add_residual(dve))
            barrier(dve, "dve")
            dve_norm(dve)
            dve_norm_apply(dve, 7)
            barrier(dve, "dve")
            for p in range(len(FF2_PARTS)):
                dve_relu2(dve, f"up1_{p}")
                dve_segment(dve, f"down1_{p}", add_residual(dve))
            barrier(dve, "dve")

        @block.gpsimd
        def _(pool):
            pool.sem_inc(nlo, 2)
            pool_norm_apply(pool, xah, xal)
            split_lo(pool, Blk(0, 0))
            barrier(pool, "pool")
            pool_segment(pool, "ba")
            pool_segment(pool, "qkv")
            barrier(pool, "pool")
            barrier(pool, "pool")
            pool_delta(pool)
            barrier(pool, "pool")
            barrier(pool, "pool")
            for name in ("z", "sc", "gates", "ya", "yb", "wout"):
                pool_segment(pool, name)
            barrier(pool, "pool")
            pool_norm_apply(pool, xah, xal)
            barrier(pool, "pool")
            for p in range(len(FF1_PARTS)):
                pool_segment(pool, f"gu{p}")
                pool_segment(pool, f"dn{p}")
            barrier(pool, "pool")
            barrier(pool, "pool")
            barrier(pool, "pool")
            pool_norm_apply(pool, xah, xal)
            barrier(pool, "pool")
            pool_segment(pool, "dsa")
            barrier(pool, "pool")
            barrier(pool, "pool")
            barrier(pool, "pool")
            barrier(pool, "pool")
            pool_index(pool)
            barrier(pool, "pool")
            pool_attention(pool, False)
            barrier(pool, "pool")
            pool_segment(pool, "dsa_out")
            barrier(pool, "pool")
            pool_norm_apply(pool, xah, xal)
            barrier(pool, "pool")
            for p in range(len(FF2_PARTS)):
                pool_segment(pool, f"up0_{p}")
                pool_segment(pool, f"down0_{p}")
            barrier(pool, "pool")
            pool_norm_apply(pool, xah, xal)
            pool_norm_apply(pool, xbh, xbl)
            barrier(pool, "pool")
            pool_segment(pool, "foxkv")
            pool_segment(pool, "foxf")
            pool_segment(pool, "foxq")
            barrier(pool, "pool")
            barrier(pool, "pool")
            barrier(pool, "pool")
            pool_attention(pool, True)
            barrier(pool, "pool")
            pool_segment(pool, "fox_out")
            barrier(pool, "pool")
            pool_norm_apply(pool, xah, xal)
            barrier(pool, "pool")
            for p in range(len(FF2_PARTS)):
                pool_segment(pool, f"up1_{p}")
                pool_segment(pool, f"down1_{p}")
            barrier(pool, "pool")

        @block.sync
        def _(sp):
            for dst, src in consts:
                sp.dma_start(dst, src).then_inc(const_in, 16)
            load_weights(sp)
            sp.wait_ge(phase_done, 4 * phases["pe"])
            sp.dma_start(out.rearrange("k p t -> p k t"),
                         res[:, :].rearrange("p (k t) -> p k t", t=T)[:, :, NMETA:T]).then_inc(out_sent, 16)
            sp.wait_ge(out_sent, 16)


def constants():
    f = np.float32
    ident = np.eye(P, dtype=f)
    win128 = np.zeros((P, 31), f)
    win128[:, 15] = 1
    win64 = np.zeros((P, 30), f)
    win64[0:64, 14] = 1
    win64[64:128, 15] = 1
    s, i = np.arange(C)[:, None], np.arange(C)[None, :]
    tri = np.stack([s <= i, s >= i], 1).astype(f)
    masks = np.zeros((C, 2, LEVELS, C), f)
    for lv in range(LEVELS):
        b = 2 ** lv
        same = (s // (2 * b)) == (i // (2 * b))
        lo, hi = (s // b) % 2 == 0, (i // b) % 2 == 1
        masks[:, 0, lv, :] = same & lo & hi
        masks[:, 1, lv, :] = same & ~lo & ~hi
    sel = np.zeros((16, 2, NG, GH), f)
    for u in range(2):
        for g in range(NG):
            for r in range(GH):
                sel[8 * u + GH * g + r, u, g, r] = 1
    causal = np.where(s >= i, 0.0, NEG).astype(f)
    inv = (1.0 / (np.float32(10000.0) ** (np.arange(0, 64, 2, dtype=f) / f(64)))).astype(f)
    ang = np.arange(T, dtype=f)[:, None] * inv[None, :]
    cossin = np.stack([np.tile(np.cos(ang).T, (4, 1)), np.tile(np.sin(ang).T, (4, 1))], 1).astype(f)
    rot = np.zeros((P, P), f)
    for h in range(2):
        for d in range(32):
            rot[64 * h + 32 + d, 64 * h + d] = -1
            rot[64 * h + d, 64 * h + 32 + d] = 1
    return dict(ident=ident, win128=win128, win64=win64, tri=tri, masks=masks, sel=sel, causal=causal,
                cossin=np.ascontiguousarray(cossin), rot=rot)


def columns(m):
    k, n = m.shape
    x = m.reshape(k // P, P, n // P, P).transpose(2, 1, 0, 3).reshape(n // P, P, k)
    return x if k == DM else np.concatenate([x, np.zeros((n // P, P, DM - k), x.dtype)], 2)


def widened(m):
    return np.concatenate([m, np.zeros((m.shape[0], P - m.shape[1]), m.dtype)], 1)


def lay_weights(a):
    wi_ = a["w_in"][0]
    cuts = np.cumsum([1024, 1024, 1024, 1024, 16, 16, 1024, 1024, 1024, 1024, 1024])
    q, k, v, z, b, aa, scb, scc, scx, ga, gb = np.split(wi_, cuts[:-1], axis=1)
    out = [columns(widened(b)), columns(widened(aa)), columns(q), columns(k), columns(v), columns(z)]
    out.append(np.stack([columns(scb), columns(scc), columns(scx)], 1).reshape(24, P, DM))
    out += [columns(ga), columns(gb), columns(a["w_branch_dn"][0]), columns(a["w_branch_sc"][0]),
            columns(a["w_out"][0])]
    gu, dn = a["w_gate_up"][0], a["w_down"][0]
    at = 0
    for n in FF1_PARTS:
        g = columns(gu[:, at:at + n * P])
        u = columns(gu[:, FF1 + at:FF1 + at + n * P])
        out.append(np.stack([g, u], 1).reshape(2 * n, P, DM))
        out.append(columns(dn[at:at + n * P]))
        at += n * P
    w = a["a_w_in_2"][0]
    q, k, v, qi, ki, wt = np.split(w, np.cumsum([1024, 256, 256, 512, 64]), axis=1)
    order = dsa_heads()
    q = q.reshape(DM, 16, 64)[:, order].reshape(DM, DM)
    out += [columns(q), columns(k), columns(v), columns(qi), columns(np.concatenate([ki, ki], 1)),
            columns(widened(wt)), columns(a["a_w_out_2"][0].reshape(16, 64, DM)[order].reshape(DM, DM))]

    def mlp(i):
        for p in range(4):
            out.append(columns(a["mlp_w1_2"][i][:, p * DM:(p + 1) * DM]))
            out.append(columns(a["mlp_w2_2"][i][p * DM:(p + 1) * DM]))

    mlp(0)
    kv = a["kv_w_2"]
    out += [columns(kv[:, :2 * DM]), columns(widened(kv[:, 2 * DM:])), columns(a["b_w_q_2"][0]),
            columns(a["b_w_out_2"][0])]
    mlp(1)
    out = np.concatenate(out, 0)
    assert out.shape == (NB, P, DM)
    return out


def dsa_heads():
    return [(2 * (m // 4) + h) * 4 + m % 4 for m in range(8) for h in range(2)]


def lay_inputs(inputs):
    a = {k: np.asarray(v) for k, v in inputs.items()}
    f = np.float32
    x = np.concatenate([a["meta_tokens"], a["x"][0]], 0)
    per = lambda v: v.reshape(KT, P).T
    gains = [a["norm1_w"][0], a["norm2_w"][0], a["final_norm_w"], a["attn_norm_2"][0], a["mlp_norm_2"][0],
             a["kv_norm_2"], a["attn_norm_2"][1], a["mlp_norm_2"][1]]
    twice = lambda v: np.concatenate([v, v])
    qscale = np.array([P ** -0.5] * 8 + [1.0] * 8, f)
    lay = dict(
        w=lay_weights(a),
        x=x.T.reshape(KT, P, T),
        meta2=a["meta_tokens_2"].T.reshape(KT, P, NMETA),
        gains=np.concatenate([per(g) for g in gains], 1),
        headgain=np.stack([a["dn_norm_w"][0], twice(a["a_q_gain_2"][0]), twice(a["a_k_gain_2"][0]),
                           twice(a["kv_k_gain_2"]), twice(a["b_q_gain_2"][0])], 1),
        rowvec=np.stack([a["dt_bias"][0].reshape(16), a["A_log"][0].reshape(16), a["kv_f_bias_2"], qscale], 1),
        convw=a["dn_conv_w"][0].reshape(5, 24, P).transpose(2, 1, 0).reshape(P, 120),
        scw=a["sc_conv_w"][0].reshape(3, 8, P).transpose(2, 1, 0).reshape(P, 24),
        **constants())
    return {k: np.ascontiguousarray(v) for k, v in lay.items()}


def kernel(**inputs):
    import concourse.bacc as bacc
    from concourse.bass_utils import run_bass_kernel_spmd

    nc = bacc.Bacc("TRN2", target_bir_lowering=False, num_devices=1)
    arrays, io = {}, {}
    for name, v in lay_inputs(inputs).items():
        arrays[f"in_{name}"] = v
        io[name] = nc.dram_tensor(f"in_{name}", v.shape, mybir.dt.from_np(v.dtype), kind="ExternalInput").ap()
    io["out"] = nc.dram_tensor("out", (KT, P, SEQ), F32, kind="ExternalOutput").ap()
    build_program(nc, io)
    got = run_bass_kernel_spmd(nc, [arrays], core_ids=[0]).results[0]["out"]
    return np.ascontiguousarray(got.reshape(DM, SEQ).T).reshape(1, SEQ, DM)
```

```python
from collections import namedtuple

import numpy as np

import concourse.bass as bass
from concourse import mybir

F32 = mybir.dt.float32
F32R = mybir.dt.float32r
BF16 = mybir.dt.bfloat16
ALU = mybir.AluOpType
ACT = mybir.ActivationFunctionType
AX = mybir.AxisListType

P = 128
DM = 1024
KT = DM // P
NMETA, SEQ = 16, 512
T = NMETA + SEQ
HT = T // 2
C = 106
NCH = -(-T // C)
TS = NCH * C
ROWS = [min(C, T - t * C) for t in range(NCH)]
ENDS = [min(C * (t + 1), T) for t in range(NCH)]
H1, NG, GH = 8, 2, 4
FF1 = 2816
FF1_PARTS = [8, 8, 6]
FF2_PARTS = [8, 8, 8, 8]
PARTS = 80
LEVELS = 7
TOPK = 128
NEG = -1.0e30
LOWEST = -3.0e38
EPS = 1.0e-6

Blk = namedtuple("Blk", "c i")


def num(b):
    return b.c + 2 * b.i


def slot(b):
    return b.c % 2


def nxt(b, n=1):
    return Blk(b.c + n, b.i)


Seg = namedtuple("Seg", "b0 n k")


def plan_segments():
    segs, at = {}, 0

    def add(name, n, k=KT):
        nonlocal at
        segs[name] = Seg(at, n, k)
        at += n

    add("ba", 2)
    add("qkv", 24)
    add("z", 8)
    add("sc", 24)
    add("gates", 16)
    add("ya", 8)
    add("yb", 8)
    add("wout", 8)
    for p, n in enumerate(FF1_PARTS):
        add(f"gu{p}", 2 * n)
        add(f"dn{p}", 8, n)
    add("dsa", 18)
    add("dsa_out", 8)
    for p, n in enumerate(FF2_PARTS):
        add(f"up0_{p}", n)
        add(f"down0_{p}", 8, n)
    add("foxkv", 16)
    add("foxf", 1)
    add("foxq", 8)
    add("fox_out", 8)
    for p, n in enumerate(FF2_PARTS):
        add(f"up1_{p}", n)
        add(f"down1_{p}", 8, n)
    return segs, at


SEGS, NB = plan_segments()


def wait(e, sem, value):
    if isinstance(value, int) and value <= 0:
        return
    e.wait_ge(sem, value)


def blocks(e, seg, body, first=0, last=0):
    pairs = seg.n // 2
    for i in range(first):
        for u in range(2):
            body(2 * i + u, u, Blk(seg.b0 + 2 * i + u, 0))
    if pairs - last > first:
        with e.Fori(first, pairs - last) as i:
            for u in range(2):
                body(i * 2 + u, u, Blk(seg.b0 + u, i))
    for i in range(pairs - last, pairs):
        for u in range(2):
            body(2 * i + u, u, Blk(seg.b0 + 2 * i + u, 0))
    if seg.n % 2:
        body(seg.n - 1, 0, Blk(seg.b0 + seg.n - 1, 0))


def tiles(e, n, body):
    with e.Fori(0, n // 2) as i:
        for u in range(2):
            body(i * 2 + u, u)


def pieces(n):
    return [(0, n)] if n <= 512 else [(0, HT), (HT, HT)]


def build_program(nc, io):
    w, out, nb = io["w"], io["out"], NB

    base = 16512
    F = 4 * T

    def place(name, shape, dt, offset):
        return nc.alloc_sbuf_tensor_at(name, shape, dt, offset=offset)

    def region(start):
        pos = [start]

        def sb(name, shape, dt=F32):
            n = 2 if dt == BF16 else 4
            for s in shape[1:]:
                n *= s
            n = -(-n // 32) * 32
            off = pos[0]
            pos[0] += n
            return place(name, shape, dt, off)

        sb.pos = pos
        return sb

    keep = region(base)
    res = keep("res", [P, KT * T])
    a_at = keep.pos[0]
    xah, xal = keep("xah", [P, KT * T], F32R), keep("xal", [P, KT * T], F32R)
    b_at = keep.pos[0]
    xbh, xbl = keep("xbh", [P, KT * T], F32R), keep("xbl", [P, KT * T], F32R)
    wraw = keep("wraw", [P, 2 * DM])
    wh, wl = keep("wh", [P, 2 * DM], F32R), keep("wl", [P, 2 * DM], F32R)
    stage_pos = keep.pos[0]
    stage = keep("stage", [P, 2 * T])
    ident = keep("ident", [P, P])
    ones = keep("ones", [P, P])
    win128 = keep("win128", [P, 31])
    win64 = keep("win64", [P, 30])
    gains = keep("gains", [P, 8 * KT])
    headgain = keep("headgain", [P, 8])
    rowvec = keep("rowvec", [16, 8])
    eps = keep("eps", [P, 1])
    rstd = keep("rstd", [P, T])
    phase_at = keep.pos[0]

    r1 = region(phase_at)
    qkv = r1("qkv", [P, 24 * TS])
    oacc = r1("oacc", [P, 8 * TS])
    convw = r1("convw", [P, 24 * 5])
    scw = r1("scw", [P, 8 * 3])
    tri = r1("tri", [C, 2, C])
    masks = r1("masks", [C, 2, LEVELS, C])
    sel = r1("sel", [16, 2, NG, GH])
    scum = r1("scum", [16, 2, TS])
    tok_g = r1("tok_g", [C, NCH, 16])
    tok_b = r1("tok_b", [C, NCH, 16])
    tok_cum = r1("tok_cum", [C, 2, NCH, 8])
    tok_neg = r1("tok_neg", [C, 2, NCH, 8])
    tok_bk = r1("tok_bk", [C, 2, NCH, 8])
    chunk_decay = r1("chunk_decay", [P, 2, NCH, 8])
    d_at = r1.pos[0]
    assert d_at <= nc.sbuf_usable_end, d_at
    rb = region(b_at)
    cpad = [rb(f"cpad{u}", [P, T + 4]) for u in range(2)]
    cout = [rb(f"cout{u}", [P, T]) for u in range(2)]
    sq = [rb(f"sq{u}", [P, T]) for u in range(2)]
    hroot = rb("hroot", [32, T])
    hinv = rb("hinv", [32, T])
    beta = rb("beta", [16, TS])
    gdec = rb("gdec", [16, TS])
    sp = [rb(f"sp{i}", [16, T]) for i in range(5)]
    spread = place("spread", [16, 8 * P], F32, b_at)
    assert 4 * 8 * P <= 8 * (T + 4)
    delta = []
    rx = region(b_at)
    ry = region(d_at)

    def dsb(name, shape):
        n = 4
        for s in shape[1:]:
            n *= s
        r = rx if rx.pos[0] + n <= b_at + 2 * KT * F else ry
        return r(name, shape)

    W4 = GH * C
    for u in range(2):
        d = {}
        d["ks"] = dsb(f"ks{u}", [P, W4])
        d["qd"] = dsb(f"qd{u}", [P, W4])
        d["state"] = dsb(f"state{u}", [P, GH * P])
        d["kt"] = dsb(f"kt{u}", [C, GH * P])
        d["vt"] = dsb(f"vt{u}", [C, GH * P])
        d["qkm"] = dsb(f"qkm{u}", [C, W4])
        r = rx if rx.pos[0] + 4 * W4 <= b_at + 2 * KT * F else ry
        o = r.pos[0]
        d["xt"] = r(f"xt{u}", [C, W4])
        d["grow"] = place(f"grow{u}", [16, W4], F32, o)
        r = rx if rx.pos[0] + 2 * 4 * W4 <= b_at + 2 * KT * F else ry
        o = r.pos[0]
        d["qs"], d["vs"] = r(f"qs{u}", [P, W4]), r(f"vs{u}", [P, W4])
        d["rr"] = place(f"rr{u}", [C, GH * P], F32, o)
        r = rx if rx.pos[0] + 2 * 4 * W4 <= b_at + 2 * KT * F else ry
        o = r.pos[0]
        d["dec"], d["ob"] = r(f"dec{u}", [C, W4]), r(f"ob{u}", [C, W4])
        d["vn"] = place(f"vn{u}", [C, GH * P], F32, o)
        r = rx if rx.pos[0] + 2 * 4 * W4 <= b_at + 2 * KT * F else ry
        o = r.pos[0]
        d["pp"], d["xx"] = r(f"pp{u}", [C, W4]), r(f"xx{u}", [C, W4])
        d["vk"] = place(f"vk{u}", [C, GH * P], F32, o)
        d["mt"] = place(f"mt{u}", [C, W4], F32, stage_pos + u * 4 * W4)
        delta.append(d)
    assert ry.pos[0] <= nc.sbuf_usable_end, (ry.pos[0], nc.sbuf_usable_end)
    scy = place("scy", [P, 8 * T], F32, phase_at)
    gab = place("gab", [P, 16 * T], F32, phase_at + 8 * F)
    rsc = region(d_at)
    pc = rsc("pc", [P, T + 2])
    bst = rsc("bst", [P, T])

    r2 = region(phase_at)
    pf = r2("pf", [P, 24 * T])
    vtok = r2("vtok", [C, NCH, DM])
    causal = r2("causal", [C, C])
    mask16 = r2("mask16", [C, NCH, T], BF16)
    ident16 = r2("ident16", [P, C], BF16)
    assert r2.pos[0] <= nc.sbuf_usable_end, r2.pos[0]
    rdsa = region(phase_at + 17 * F)
    wi = rdsa("wi", [8, T])
    bias = rdsa("bias", [C, NCH, T])
    assert rdsa.pos[0] <= phase_at + 24 * F
    rv = region(phase_at + 24 * F + NCH * 256 * 4)
    cossin = rv("cossin", [P, 2, T])
    rot = rv("rot", [P, P])
    wit = rv("wit", [C, NCH, 8])
    assert rv.pos[0] <= phase_at + 24 * F + NCH * DM * 4
    rt = region(a_at)
    qz = rt("qz", [P, 2, T])
    score = [rt(f"score{u}", [C, T]) for u in range(2)]
    prob = [rt(f"prob{u}", [C, T]) for u in range(2)]
    ptr = [rt(f"ptr{u}", [C, T]) for u in range(2)]
    otok = rt("otok", [C, NCH * P])
    headrow = rt("headrow", [PARTS, 2, C], BF16)
    decay_row = rt("decay_row", [PARTS, T], BF16)
    rowmax = rt("rowmax", [C, 2 * NCH])
    rowsum = rt("rowsum", [C, 2 * NCH])
    rowinv = rt("rowinv", [C, 2 * NCH])
    top8 = rt("top8", [C, NCH * 8])
    lfneg = rt("lfneg", [16, T])
    cneg = rt("cneg", [16, T])
    assert rt.pos[0] <= b_at
    rtk = region(a_at)
    work = rtk("work", [C, NCH, T])
    ps = nc.alloc_psum_tensor("ps", [P, 8, 512], F32)
    SEMS = {}

    def sem(name):
        SEMS[name] = nc.alloc_semaphore(name)
        return SEMS[name]

    raw_full = [sem("raw_full0"), sem("raw_full1")]
    hi_done, lo_done = sem("hi_done"), sem("lo_done")
    block_done = sem("block_done")
    acc_free = sem("acc_free")
    post_done = sem("post_done")
    phase_done = sem("phase_done")
    const_in, const2_in, out_sent = sem("const_in"), sem("const2_in"), sem("out_sent")
    nsq, nused, nsum, nroot, nscaled, nhi, nlo = map(sem, (
        "norm_square", "norm_square_used", "norm_sum", "norm_root", "norm_scaled", "norm_hi", "norm_lo"))
    hsq, hused, hsum, hrt, hiv, hbc, happ = map(sem, (
        "head_square", "head_square_used", "head_sum", "head_root", "head_inverse", "head_spread",
        "head_applied"))
    conv_done, silu_done = sem("conv_done"), sem("silu_done")
    sp_abs, sp_exp = sem("softplus_abs"), sem("softplus_exp")
    prep_pe, prep_act, prep_dve = sem("prep_pe"), sem("prep_act"), sem("prep_dve")
    dpe = [sem("delta_pe0"), sem("delta_pe1")]
    dact = [sem("delta_act0"), sem("delta_act1")]
    ddve = [sem("delta_dve0"), sem("delta_dve1")]
    dpool = [sem("delta_pool0"), sem("delta_pool1")]
    rope_pe, rope_dve = sem("rope_turned"), sem("rope_applied")
    vt_in, vt_pe, vt_out = sem("v_staged"), sem("v_turned"), sem("v_stored")
    ix_q, ix_pe, ix_act, ix_dve = sem("index_q"), sem("index_logits"), sem("index_relu"), sem("index_added")
    wit_pe, prep_dve_ones = sem("index_weights_turned"), sem("ones_ready")
    at_zero, at_row, at_q, at_s, at_mx = map(sem, (
        "att_zeroed", "att_head_row", "att_q", "att_scores", "att_max"))
    at_p, at_pt, at_pte, at_o, at_oe, at_ot, at_of = map(sem, (
        "att_prob", "att_prob_turned", "att_prob_out", "att_value", "att_value_out", "att_turned",
        "att_stored"))

    before, total = {}, 0
    for name, seg in SEGS.items():
        before[name] = total
        if name in ("z", "sc", "ya", "yb", "wout", "dsa_out", "fox_out") or name[:2] in ("dn", "up") \
                or name.startswith("down"):
            total += 8 if name == "sc" else seg.n
        elif name.startswith("gu"):
            total += seg.n // 2

    phases = {"pe": 0, "act": 0, "dve": 0, "pool": 0}

    def barrier(e, who):
        phases[who] += 1
        e.drain().then_inc(phase_done, 1)
        e.wait_ge(phase_done, 4 * phases[who])

    def bank(b, rows=P, n=HT, off=0):
        return ps[0:rows, b, off:off + n]

    def pair_of(b, rows=P):
        return ps[0:rows, b:b + 2, 0:HT]

    def two(ap):
        return ap.rearrange("p (h t) -> p h t", h=2)

    def tile_at(buf, m, n=T, off=0):
        step = TS if buf is qkv or buf is oacc else T
        return buf[:, bass.ds(m * step + off, n)]

    def load_weights(sp):
        def load(b):
            wait(sp, lo_done, num(b) - 1)
            sp.dma_start(wraw[:, slot(b) * DM:(slot(b) + 1) * DM],
                         w[bass.ds(num(b), 1)].rearrange("a p n -> (a p) n")).then_inc(raw_full[slot(b)], 16)

        load(Blk(0, 0))
        load(Blk(1, 0))
        with sp.Fori(1, nb // 2) as i:
            for u in range(2):
                src = w[bass.ds(sp.snap(i * 2 + u), 1)].rearrange("a p n -> (a p) n")
                sp.wait_ge(lo_done, i * 2 + (u - 1))
                sp.dma_start(wraw[:, u * DM:(u + 1) * DM], src).then_inc(raw_full[u], 16)
        if nb % 2:
            load(Blk(nb - 1, 0))

    def split_hi(act, b):
        if isinstance(b.i, int) and num(b) >= nb:
            return
        s = slot(b)
        wait(act, raw_full[s], 16 * (b.c // 2 + 1 + b.i))
        wait(act, block_done, num(b) - 1)
        act.activation(wh[:, s * DM:(s + 1) * DM], wraw[:, s * DM:(s + 1) * DM], ACT.Copy).then_inc(hi_done, 1)

    def split_lo(pool, b):
        if isinstance(b.i, int) and num(b) >= nb:
            return
        s = slot(b)
        pool.wait_ge(hi_done, num(b) + 1)
        pool.tensor_tensor(wl[:, s * DM:(s + 1) * DM], wraw[:, s * DM:(s + 1) * DM],
                           wh[:, s * DM:(s + 1) * DM].bitcast(F32), ALU.subtract).then_inc(lo_done, 1)

    def products(pe, b, xh, xl, k):
        s = slot(b)
        pe.wait_ge(lo_done, num(b) + 1)
        wait(pe, acc_free, num(b) - 1)
        for h in range(2):
            n = 0
            for ws, x in ((wh, xh), (wl, xh), (wh, xl)):
                for kk in range(k):
                    mm = pe.matmul(ps[:, 2 * s + h, 0:HT], ws[:, s * DM + kk * P:s * DM + (kk + 1) * P],
                                   x[:, kk * T + h * HT:kk * T + (h + 1) * HT],
                                   start=(n == 0), stop=(n == 3 * k - 1))
                    n += 1
        mm.then_inc(block_done, 1)

    def pe_segment(pe, name, xh, xl):
        seg = SEGS[name]
        if name in ("ya", "yb", "wout") or name[:2] in ("dn", "do"):
            pe.wait_ge(post_done, before[name] + 2)
        blocks(pe, seg, lambda j, u, b: products(pe, b, xh, xl, seg.k), first=1 if seg.b0 == 0 else 0)

    def acc(b, rows=P):
        return pair_of(2 * slot(b), rows)

    def stage_at(u):
        return stage[:, u * T:(u + 1) * T]

    def pool_segment(pool, name):
        seg = SEGS[name]
        last = seg.b0 + seg.n == nb
        blocks(pool, seg, lambda j, u, b: split_lo(pool, nxt(b)), first=1 if seg.b0 == 0 else 0,
               last=1 if last else 0)

    def act_segment(act, name, out, func=ACT.Copy, posts=False, **more):
        seg = SEGS[name]
        last = seg.b0 + seg.n == nb
        if posts:
            act.wait_ge(post_done, before[name] + 2)

        def body(j, u, b):
            split_hi(act, nxt(b))
            act.wait_ge(block_done, num(b) + 1)
            if posts:
                act.wait_ge(post_done, before[name] + j + 1)
            act.activation(two(out(j, u)), acc(b), func, **more).then_inc(acc_free, 1)

        blocks(act, seg, body, last=1 if last else 0)

    def dve_segment(dve, name, post):
        seg = SEGS[name]

        def body(j, u, b):
            dve.wait_ge(acc_free, num(b) + 1)
            post(j, u).then_inc(post_done, 1)

        blocks(dve, seg, body)

    def split_store(dve, hi, lo, m, x):
        dve.tensor_scalar(tile_at(hi, m), x, 1.0, None, ALU.mult)
        dve.drain()
        return dve.tensor_tensor(tile_at(lo, m), x, tile_at(hi, m).bitcast(F32), ALU.subtract)

    def add_residual(dve):
        def post(j, u):
            return dve.tensor_tensor(tile_at(res, j), tile_at(res, j), stage_at(u), ALU.add)
        return post

    norms = {"pe": 0, "act": 0, "dve": 0, "pool": 0}
    applied = {"act": 0, "dve": 0, "pool": 0}

    def pe_norm(pe):
        k = norms["pe"]
        norms["pe"] += 1
        for m in range(KT):
            pe.wait_ge(nsq, KT * k + m + 1)
            for h in range(2):
                mm = pe.matmul(ps[:, 4 + h, 0:HT], ones[:, :], sq[m % 2][:, h * HT:(h + 1) * HT],
                               start=(m == 0), stop=(m == KT - 1))
            mm.then_inc(nused, 1)
        pe.drain().then_inc(nsum, 1)

    def act_norm(act):
        k = norms["act"]
        norms["act"] += 1

        def square(m, u):
            act.wait_ge(nused, KT * k + m + 1)
            act.activation(sq[u][:, :], tile_at(res, m), ACT.Square).then_inc(nsq, 1)

        tiles(act, KT, square)
        act.wait_ge(nsum, k + 1)
        act.activation(two(rstd[:, :]), pair_of(4), ACT.Sqrt, bias=eps[:, 0:1],
                       scale=1.0 / DM).then_inc(nroot, 1)

    def dve_norm(dve):
        k = norms["dve"]
        norms["dve"] += 1
        dve.wait_ge(nroot, k + 1)
        dve.reciprocal(rstd[:, :], rstd[:, :])
        dve.drain()

    def dve_norm_apply(dve, gi):
        a = applied["dve"]
        applied["dve"] += 1

        def scale(m, u):
            dve.wait_ge(nlo, KT * a + m + 1)
            dve.scalar_tensor_tensor(stage_at(u), tile_at(res, m), gains[:, bass.ds(m + gi * KT, 1)],
                                     rstd[:, :], ALU.mult, ALU.mult).then_inc(nscaled, 1)

        tiles(dve, KT, scale)

    def act_norm_apply(act, xh):
        a = applied["act"]
        applied["act"] += 1

        def hi(m, u):
            act.wait_ge(nscaled, KT * a + m + 1)
            act.activation(tile_at(xh, m), stage_at(u), ACT.Copy).then_inc(nhi, 1)

        tiles(act, KT, hi)

    def pool_norm_apply(pool, xh, xl):
        a = applied["pool"]
        applied["pool"] += 1

        def lo(m, u):
            pool.wait_ge(nhi, KT * a + m + 1)
            pool.tensor_tensor(tile_at(xl, m), stage_at(u), tile_at(xh, m).bitcast(F32),
                               ALU.subtract).then_inc(nlo, 1)

        tiles(pool, KT, lo)

    heads = {"pe": [0, 0], "act": [0, 0], "dve": [0, 0]}

    def count_heads(who, n):
        at_tile, call = heads[who]
        heads[who] = [at_tile + n, call + 1]
        return at_tile, call

    def pe_headnorm(pe, n, width):
        k, call = count_heads("pe", n)
        rows = 16
        if k:
            pe.wait_ge(happ, k + 2)
        for m in range(n):
            lhs = win128[:, 15 - m:31 - m] if width == P else win64[:, 14 - 2 * m:30 - 2 * m]
            pe.wait_ge(hsq, k + m + 1)
            for h in range(2):
                mm = pe.matmul(ps[0:rows, 4 + h, 0:HT], lhs, sq[m % 2][:, h * HT:(h + 1) * HT],
                               start=(m == 0), stop=(m == n - 1))
            mm.then_inc(hused, 1)
        pe.drain().then_inc(hsum, 1)
        pe.wait_ge(hiv, call + 1)
        for m in range(n):
            if width == P:
                lhs = ident[0:rows, m:m + 1].broadcast_to([rows, P])
            else:
                lhs = spread[:, m * P:(m + 1) * P]
            pe.wait_ge(happ, k + m + 1)
            for h in range(2):
                mm = pe.matmul(ps[:, 4 + 2 * (m % 2) + h, 0:HT], lhs, hinv[0:rows, h * HT:(h + 1) * HT],
                               start=True, stop=True)
            mm.then_inc(hbc, 1)

    def act_headnorm(act, buf, t0, n, width, scale):
        k, call = count_heads("act", n)
        rows = 16

        def square(m, u):
            act.wait_ge(hused, k + m + 1)
            act.activation(sq[u][:, :], tile_at(buf, m + t0), ACT.Square).then_inc(hsq, 1)

        tiles(act, n, square)
        act.wait_ge(hsum, call + 1)
        act.activation(two(hroot[0:rows, :]), pair_of(4, rows), ACT.Sqrt, bias=eps[0:rows, 0:1],
                       scale=scale).then_inc(hrt, 1)

    def dve_headnorm(dve, buf, t0, n, width, gain, rowscale=None):
        k, call = count_heads("dve", n)
        rows = 16
        dve.wait_ge(hrt, call + 1)
        if width != P:
            dve.tensor_copy(spread[:, :].rearrange("p (k n) -> p k n", n=64),
                            ident[0:rows, 0:16].unsqueeze(2).broadcast_to([rows, 16, 64]))
        last = dve.reciprocal(hinv[0:rows, :], hroot[0:rows, :])
        if rowscale is not None:
            dve.drain()
            last = dve.tensor_scalar(hinv[0:rows, :], hinv[0:rows, :], rowscale, None, ALU.mult)
        last.then_inc(hiv, 1)

        def apply(m, u):
            dve.wait_ge(hbc, k + m + 1)
            dve.scalar_tensor_tensor(two(tile_at(buf, m + t0)), two(tile_at(buf, m + t0)), gain,
                                     pair_of(4 + 2 * u), ALU.mult, ALU.mult).then_inc(happ, 1)

        tiles(dve, n, apply)

    softs = {"act": 0, "dve": 0}

    def act_softplus(act, y):
        softs["act"] += 1
        act.wait_ge(sp_abs, softs["act"])
        act.activation(sp[0][:, :], y, ACT.Abs)
        act.drain()
        act.activation(sp[1][:, :], sp[0][:, :], ACT.Exp, scale=-1.0).then_inc(sp_exp, 1)

    def dve_softplus(dve, out_, y):
        softs["dve"] += 1
        _, e, r, p, q = (t[:, :] for t in sp)
        dve.drain().then_inc(sp_abs, 1)
        dve.wait_ge(sp_exp, softs["dve"])
        dve.tensor_scalar(r, e, 2.0, None, ALU.add)
        dve.drain()
        dve.reciprocal(p, r)
        dve.drain()
        dve.tensor_tensor(e, e, p, ALU.mult)
        dve.drain()
        dve.tensor_tensor(q, e, e, ALU.mult)
        dve.drain()
        dve.tensor_scalar(p, q, 1.0 / 17, None, ALU.mult)
        for k in range(7, 0, -1):
            dve.drain()
            dve.scalar_tensor_tensor(p, p, 1.0 / (2 * k + 1), q, ALU.add, ALU.mult)
        dve.drain()
        dve.scalar_tensor_tensor(p, p, 1.0, e, ALU.add, ALU.mult)
        dve.tensor_scalar(r, y, 0.0, None, ALU.max)
        dve.drain()
        dve.scalar_tensor_tensor(out_, p, 2.0, r, ALU.mult, ALU.add)
        dve.drain()

    def act_qkv(act):
        def body(j, u, b):
            split_hi(act, nxt(b))
            act.wait_ge(block_done, num(b) + 1)
            act.wait_ge(conv_done, j + 1)
            act.activation(two(cpad[u][:, 2:2 + T]), acc(b), ACT.Copy).then_inc(acc_free, 1)
            if not isinstance(j, int) or j > 0:
                silu(j - 1, 1 - u)

        def silu(j, u):
            act.wait_ge(conv_done, j + 3)
            act.activation(tile_at(qkv, j), cout[u][:, :], ACT.Silu).then_inc(silu_done, 1)

        blocks(act, SEGS["qkv"], body, first=1)
        silu(23, 1)

    def dve_qkv(dve):
        for u in range(2):
            dve.memset(cpad[u][:, 0:2], 0.0)
            dve.memset(cpad[u][:, T + 2:T + 4], 0.0)
        dve.memset(qkv[:, :].rearrange("p (k t) -> p k t", t=TS)[:, :, T:TS], 0.0)
        dve.drain()

        def body(j, u, b):
            dve.wait_ge(acc_free, num(b) + 1)
            dve.wait_ge(silu_done, j + 1)
            o = cout[u][:, :]
            for k in range(5):
                tap = convw[:, bass.ds(j * 5 + k, 1)]
                if k == 0:
                    last = dve.tensor_scalar(o, cpad[u][:, 0:T], tap, None, ALU.mult)
                else:
                    dve.drain()
                    last = dve.scalar_tensor_tensor(o, cpad[u][:, k:k + T], tap, o, ALU.mult, ALU.add)
            last.then_inc(conv_done, 1)

        blocks(dve, SEGS["qkv"], body)

    def act_ba(act):
        b0, b1 = Blk(0, 0), Blk(1, 0)
        split_hi(act, b1)
        act.wait_ge(block_done, 1)
        act.activation(two(beta[:, 0:T]), acc(b0, 16), ACT.Sigmoid).then_inc(acc_free, 1)
        split_hi(act, Blk(2, 0))
        act.wait_ge(block_done, 2)
        act.activation(two(gdec[:, 0:T]), acc(b1, 16), ACT.Identity, bias=rowvec[:, 0:1]).then_inc(acc_free, 1)

    def dve_decay(dve):
        dve.memset(gdec[:, T:TS], 0.0)
        dve.memset(beta[:, T:TS], 0.0)
        dve.wait_ge(acc_free, 2)
        dve_softplus(dve, gdec[:, 0:T], gdec[:, 0:T])
        dve.wait_ge(prep_act, 1)
        dve.tensor_scalar(gdec[:, 0:T], gdec[:, 0:T], rowvec[:, 4:5], -1.0, ALU.mult, ALU.mult).then_inc(prep_dve, 1)

    CW = NCH * 8

    def pe_prep(pe):
        pe.wait_ge(prep_dve, 1)
        for c in range(NCH):
            pe.transpose(ps[0:C, 4, c * 16:(c + 1) * 16], gdec[:, c * C:(c + 1) * C], ident[0:16, 0:16])
            mm = pe.transpose(ps[0:C, 5, c * 16:(c + 1) * 16], beta[:, c * C:(c + 1) * C], ident[0:16, 0:16])
        mm.then_inc(prep_pe, 1)
        pe.wait_ge(prep_act, 3)
        for u in range(2):
            g = tok_g[:, :, 8 * u:8 * u + 8]
            pe.matmul(ps[0:C, 6, CW * u:CW * (u + 1)].rearrange("p (c h) -> p c h", h=8), tri[:, u, :], g,
                      start=True, stop=True)
            mm = pe.matmul(ps[:, 7, CW * u:CW * (u + 1)].rearrange("p (c h) -> p c h", h=8), ones[0:C, :], g,
                           start=True, stop=True)
            for c in range(NCH):
                mm = pe.matmul(ps[0:16, 2 * u + c // 4, (c % 4) * C:(c % 4 + 1) * C], tok_g[:, c, :],
                               tri[:, u, :], start=True, stop=True)
        mm.then_inc(prep_pe, 1)

    def act_prep(act):
        act.wait_ge(prep_pe, 1)
        act.activation(tok_g[:, :, :], ps[0:C, 4, 0:NCH * 16].rearrange("p (c h) -> p c h", h=16),
                       ACT.Copy).then_inc(prep_act, 1)
        act.activation(tok_b[:, :, :], ps[0:C, 5, 0:NCH * 16].rearrange("p (c h) -> p c h", h=16),
                       ACT.Copy).then_inc(prep_act, 1)
        act.wait_ge(prep_pe, 2)
        flat = ps[0:C, 6, 0:2 * CW].rearrange("p (u c h) -> p u (c h)", u=2, h=8)
        act.activation(tok_cum[:, :, :, :].rearrange("p u c h -> p u (c h)"), flat, ACT.Copy).then_inc(prep_act, 1)
        act.activation(tok_neg[:, :, :, :].rearrange("p u c h -> p u (c h)"), flat, ACT.Exp).then_inc(prep_act, 1)
        act.activation(chunk_decay[:, :, :, :].rearrange("p u c h -> p u (c h)"),
                       ps[:, 7, 0:2 * CW].rearrange("p (u c h) -> p u (c h)", u=2, h=8), ACT.Exp)
        for u in range(2):
            act.activation(scum[:, u, 0:4 * C], ps[0:16, 2 * u, 0:4 * C], ACT.Copy)
            last = act.activation(scum[:, u, 4 * C:TS], ps[0:16, 2 * u + 1, 0:TS - 4 * C], ACT.Copy)
        last.then_inc(prep_act, 1)
        act.wait_ge(prep_dve, 2)
        act.activation(tok_bk[:, :, :, :], tok_bk[:, :, :, :], ACT.Exp).then_inc(prep_act, 1)

    def dve_prep(dve):
        dve.wait_ge(prep_act, 6)
        flat = "p u c h -> p u (c h)"
        dve.tensor_scalar(tok_neg[:, :, :, :], tok_neg[:, :, :, :], -1.0, None, ALU.mult)
        dve.scalar_tensor_tensor(tok_bk[:, :, :, :].rearrange(flat), tok_cum[:, :, :, :].rearrange(flat), -1.0,
                                 ps[0:C, 7, 0:2 * CW].rearrange("p (u c h) -> p u (c h)", u=2, h=8),
                                 ALU.mult, ALU.add).then_inc(prep_dve, 1)
        dve.wait_ge(prep_act, 7)
        for u in range(2):
            dve.tensor_tensor(tok_bk[:, u, :, :], tok_bk[:, u, :, :], tok_b[:, :, 8 * u:8 * u + 8], ALU.mult)
        dve.memset(oacc[:, :], 0.0)

    L = LEVELS
    NPE, NACT, NDVE, NPOOL = 6 + 3 * L, 9 + L, 7 + 2 * L, 4 + L

    def delta_loop(e, body):
        with e.Fori(0, NG) as g:
            with e.Fori(0, NCH) as c:
                body(g, c, g * NCH + c)

    def chunk_of(u, c):
        return c if u == 0 else c * -1 + (NCH - 1)

    def heads4(t, n):
        return t[:, :].rearrange("p (r n) -> p r n", n=n)

    def head_slices(n):
        return [slice(r * n, (r + 1) * n) for r in range(GH)]

    def pe_delta(pe):
        for u in range(2):
            pe.sem_inc(dpe[u], 1)

        def body(g, c, n):
            def on(u, who, k):
                s, per = {"act": (dact, NACT), "dve": (ddve, NDVE), "pool": (dpool, NPOOL)}[who]
                pe.wait_ge(s[u], n * per + (k + 1))

            def products4(out_, u, lhs, rhs, width=C, rows=C):
                for sl in head_slices(width):
                    mm = pe.matmul(ps[0:rows, 4 * u + out_, sl], lhs(sl), rhs(sl), start=True, stop=True)
                return mm

            for u in range(2):
                on(u, "pool", 1)
                on(u, "dve", 0)
                pe.matmul(ps[:, 4 * u + 3, 0:W4], ones[0:16, :], delta[u]["grow"][:, :], start=True,
                          stop=True).then_inc(dpe[u], 1)
            for u in range(2):
                d = delta[u]
                on(u, "act", 2)
                for r in range(GH):
                    pe.transpose(ps[0:C, 4 * u, r * P:(r + 1) * P], d["ks"][:, r * C:(r + 1) * C], ident[:, :])
                for r in range(GH):
                    mm = pe.transpose(ps[0:C, 4 * u + 1, r * P:(r + 1) * P], d["vs"][:, r * C:(r + 1) * C],
                                      ident[:, :])
                mm.then_inc(dpe[u], 1)
            for u in range(2):
                k = delta[u]["ks"]
                products4(2, u, lambda sl: k[:, sl], lambda sl: k[:, sl]).then_inc(dpe[u], 1)
            for u in range(2):
                d = delta[u]
                on(u, "pool", 2)
                on(u, "act", 4)
                products4(0, u, lambda sl: d["ks"][:, sl], lambda sl: d["qs"][:, sl]).then_inc(dpe[u], 1)
            for u in range(2):
                d = delta[u]
                on(u, "pool", 4)
                on(u, "act", 5)
                products4(1, u, lambda sl: d["ob"][:, sl], lambda sl: ident[0:C, 0:C]).then_inc(dpe[u], 1)
            for lv in range(1, L):
                for u in range(2):
                    d = delta[u]
                    on(u, "pool", 5 + lv)
                    on(u, "dve", 2 + 2 * lv)
                    products4(0, u, lambda sl: d["ob"][:, sl], lambda sl: d["xx"][:, sl]).then_inc(dpe[u], 1)
                for u in range(2):
                    d = delta[u]
                    on(u, "act", 6 + lv)
                    on(u, "dve", 3 + 2 * lv)
                    last = lv == L - 1
                    if not last:
                        products4(1, u, lambda sl: d["xt"][:, sl], lambda sl: d["pp"][:, sl]).then_inc(dpe[u], 1)
                    products4(2, u, lambda sl: d["pp"][:, sl], lambda sl: d["xt"][:, sl]
                              ).then_inc(dpe[u], 2 if last else 1)
            for u in range(2):
                d = delta[u]
                for r in range(GH):
                    mm = pe.matmul(ps[0:C, 4 * u, r * P:(r + 1) * P], d["ks"][:, r * C:(r + 1) * C],
                                   d["state"][:, r * P:(r + 1) * P], start=True, stop=True)
                mm.then_inc(dpe[u], 1)
            for u in range(2):
                d = delta[u]
                on(u, "dve", 4 + 2 * L)
                for r in range(GH):
                    mm = pe.matmul(ps[0:C, 4 * u + 1, r * P:(r + 1) * P], d["xt"][:, r * C:(r + 1) * C],
                                   d["rr"][:, r * P:(r + 1) * P], start=True, stop=True)
                mm.then_inc(dpe[u], 1)
            for u in range(2):
                d = delta[u]
                on(u, "pool", 5)
                on(u, "act", 9 + L)
                for r in range(GH):
                    o = ps[:, 4 * u + 2, r * C:(r + 1) * C]
                    pe.matmul(o, d["state"][:, r * P:(r + 1) * P], d["qd"][:, r * C:(r + 1) * C],
                              start=True, stop=False)
                    mm = pe.matmul(o, d["vn"][:, r * P:(r + 1) * P], d["qkm"][:, r * C:(r + 1) * C],
                                   start=False, stop=True)
                mm.then_inc(dpe[u], 1)
            for u in range(2):
                d = delta[u]
                on(u, "dve", 5 + 2 * L)
                for r in range(GH):
                    mm = pe.matmul(ps[:, 4 * u + 3, r * P:(r + 1) * P], d["kt"][:, r * P:(r + 1) * P],
                                   d["vk"][:, r * P:(r + 1) * P], start=True, stop=True)
                mm.then_inc(dpe[u], 1)

        delta_loop(pe, body)

    def pool_delta(pool):
        for u in range(2):
            pool.sem_inc(dpool[u], 1)
        q3 = qkv[:, :].rearrange("p (h t) -> p h t", t=TS)

        def body(g, c, n):
            t0 = [pool.snap(chunk_of(u, c) * C) for u in range(2)]
            h0 = pool.snap(g * GH)
            for u in range(2):
                d = delta[u]
                pool.wait_ge(dact[u], n * NACT + 1)
                pool.tensor_tensor(heads4(d["grow"], C),
                                   scum[:, u, bass.ds(t0[u], C)].unsqueeze(1).broadcast_to([16, GH, C]),
                                   sel[:, u, bass.ds(g, 1), :].rearrange("p a r -> p (a r)").unsqueeze(2)
                                   .broadcast_to([16, GH, C]), ALU.mult).then_inc(dpool[u], 1)
            for u in range(2):
                pool.tensor_copy(heads4(delta[u]["qs"], C), q3[:, bass.ds(h0, GH), bass.ds(t0[u], C)]
                                 ).then_inc(dpool[u], 1)
            for u in range(2):
                d = delta[u]
                pool.drain()
                pool.wait_ge(dact[u], n * NACT + 4)
                pool.tensor_tensor(d["qd"][:, :], d["qd"][:, :], d["qs"][:, :], ALU.mult).then_inc(dpool[u], 1)

            def masked(u, lv):
                d = delta[u]
                pool.tensor_tensor(heads4(d["ob"], C), heads4(d["mt"], C),
                                   masks[:, u, lv, :].unsqueeze(1).broadcast_to([C, GH, C]), ALU.mult
                                   ).then_inc(dpool[u], 1)

            for u in range(2):
                pool.wait_ge(ddve[u], n * NDVE + 3)
                masked(u, 0)
            for u in range(2):
                d = delta[u]
                pool.wait_ge(ddve[u], n * NDVE + 4)
                pool.tensor_tensor(heads4(d["qkm"], C), heads4(d["qkm"], C),
                                   tri[:, u, :].unsqueeze(1).broadcast_to([C, GH, C]), ALU.mult
                                   ).then_inc(dpool[u], 1)
            for lv in range(1, L):
                for u in range(2):
                    if lv == 1:
                        pool.wait_ge(ddve[u], n * NDVE + 6)
                    else:
                        pool.wait_ge(dpe[u], n * NPE + (3 * lv + 1))
                    masked(u, lv)

        delta_loop(pool, body)

    def act_delta(act):
        for u in range(2):
            act.sem_inc(dact[u], 1)
        q3 = qkv[:, :].rearrange("p (h t) -> p h t", t=TS)

        def body(g, c, n):
            h0 = act.snap(g * GH)
            ccs = [act.snap(chunk_of(u, c)) for u in range(2)]
            t0 = [act.snap(ccs[u] * C) for u in range(2)]
            for u in range(2):
                for name, t in (("ks", 8), ("vs", 16)):
                    act.activation(heads4(delta[u][name], C), q3[:, bass.ds(h0 + t, GH), bass.ds(t0[u], C)],
                                   ACT.Copy).then_inc(dact[u], 1)
            for u in range(2):
                d = delta[u]
                act.wait_ge(dpe[u], n * NPE + 2)
                act.activation(d["qd"][:, :], ps[:, 4 * u + 3, 0:W4], ACT.Exp).then_inc(dact[u], 1)
            for u in range(2):
                d = delta[u]
                act.wait_ge(dpe[u], n * NPE + 3)
                act.activation(d["kt"][:, :], ps[0:C, 4 * u, :], ACT.Copy).then_inc(dact[u], 1)
                act.activation(d["vt"][:, :], ps[0:C, 4 * u + 1, :], ACT.Copy).then_inc(dact[u], 1)
            for u in range(2):
                d = delta[u]
                act.wait_ge(ddve[u], n * NDVE + 2)
                act.activation(d["dec"][:, :], d["dec"][:, :], ACT.Exp).then_inc(dact[u], 1)
            for lv in range(1, L):
                for u in range(2):
                    act.wait_ge(dpe[u], n * NPE + (4 + 3 * lv))
                    act.activation(delta[u]["pp"][:, :], ps[0:C, 4 * u, 0:W4], ACT.Copy).then_inc(dact[u], 1)
            for u in range(2):
                d = delta[u]
                act.wait_ge(dpe[u], n * NPE + (5 + 3 * L))
                for r in range(GH):
                    act.activation(d["vn"][:, r * P:(r + 1) * P], ps[0:C, 4 * u + 1, r * P:(r + 1) * P], ACT.Copy,
                                   scale=tok_b[:, bass.ds(ccs[u], 1), bass.ds(h0 + (8 * u + r), 1)]
                                   .rearrange("p a b -> p (a b)")).then_inc(dact[u], 1)

        delta_loop(act, body)

    def dve_delta(dve):
        for u in range(2):
            dve.sem_inc(ddve[u], 1)
        o3 = oacc[:, :].rearrange("p (h t) -> p h t", t=TS)
        one = ident[0:C, 0:C].unsqueeze(1).broadcast_to([C, GH, C])

        def col(t, u, cc, h):
            return t[:, u, bass.ds(cc, 1), bass.ds(h, 1)].rearrange("p a b -> p (a b)")

        def body(g, c, n):
            ccs = [dve.snap(chunk_of(u, c)) for u in range(2)]
            tok0 = [dve.snap(ccs[u] * C) for u in range(2)]
            h0 = dve.snap(g * GH)
            for u in range(2):
                d = delta[u]
                dve.wait_ge(dact[u], n * NACT + 4)
                for r, sl in enumerate(head_slices(C)):
                    last = dve.tensor_scalar(d["dec"][:, sl], ps[0:C, 4 * u + 3, sl],
                                             col(tok_cum, u, ccs[u], h0 + r), 0.0, ALU.subtract, ALU.min)
                last.then_inc(ddve[u], 1)
            for u in range(2):
                d = delta[u]
                dve.wait_ge(dpe[u], n * NPE + 4)
                dve.wait_ge(dact[u], n * NACT + 7)
                for r, sl in enumerate(head_slices(C)):
                    b = tok_b[:, bass.ds(ccs[u], 1), bass.ds(h0 + (8 * u + r), 1)].rearrange("p a b -> p (a b)")
                    last = dve.scalar_tensor_tensor(d["mt"][:, sl], ps[0:C, 4 * u + 2, sl], b, d["dec"][:, sl],
                                                    ALU.mult, ALU.mult)
                last.then_inc(ddve[u], 1)
            for u in range(2):
                d = delta[u]
                dve.wait_ge(dpe[u], n * NPE + 5)
                dve.tensor_tensor(d["qkm"][:, :], ps[0:C, 4 * u, 0:W4], d["dec"][:, :], ALU.mult
                                  ).then_inc(ddve[u], 1)
            for u in range(2):
                d = delta[u]
                dve.wait_ge(dpe[u], n * NPE + 6)
                dve.tensor_tensor(heads4(d["xx"], C), one, heads4(ps[0:C, 4 * u + 1, 0:W4], C), ALU.subtract
                                  ).then_inc(ddve[u], 1)
                dve.tensor_tensor(heads4(d["xt"], C), one, heads4(d["ob"], C), ALU.subtract
                                  ).then_inc(ddve[u], 1)
            for lv in range(1, L):
                for u in range(2):
                    d = delta[u]
                    if lv < L - 1:
                        dve.wait_ge(dpe[u], n * NPE + (5 + 3 * lv))
                        dve.tensor_tensor(d["xx"][:, :], d["xx"][:, :], ps[0:C, 4 * u + 1, 0:W4], ALU.subtract
                                          ).then_inc(ddve[u], 1)
                    dve.wait_ge(dpe[u], n * NPE + (6 + 3 * lv))
                    dve.tensor_tensor(d["xt"][:, :], d["xt"][:, :], ps[0:C, 4 * u + 2, 0:W4], ALU.subtract
                                      ).then_inc(ddve[u], 1 if lv < L - 1 else 2)
            for u in range(2):
                d = delta[u]
                dve.wait_ge(dpe[u], n * NPE + (4 + 3 * L))
                for r, sl in enumerate(head_slices(P)):
                    last = dve.scalar_tensor_tensor(d["rr"][:, sl], ps[0:C, 4 * u, sl],
                                                    col(tok_neg, u, ccs[u], h0 + r), d["vt"][:, sl],
                                                    ALU.mult, ALU.add)
                last.then_inc(ddve[u], 1)
            for u in range(2):
                d = delta[u]
                dve.wait_ge(dact[u], n * NACT + (10 + L))
                for r, sl in enumerate(head_slices(P)):
                    last = dve.tensor_scalar(d["vk"][:, sl], ps[0:C, 4 * u + 1, sl],
                                             col(tok_bk, u, ccs[u], h0 + r), None, ALU.mult)
                last.then_inc(ddve[u], 1)
            for u in range(2):
                dve.drain()
                dve.wait_ge(dpe[u], n * NPE + (6 + 3 * L))
                o = o3[:, bass.ds(h0, GH), bass.ds(tok0[u], C)]
                dve.tensor_tensor(o, o, heads4(ps[:, 4 * u + 2, 0:W4], C), ALU.add).then_inc(ddve[u], 1)
            for u in range(2):
                d = delta[u]
                dve.wait_ge(dpe[u], n * NPE + (7 + 3 * L))
                for r, sl in enumerate(head_slices(P)):
                    last = dve.scalar_tensor_tensor(d["state"][:, sl], d["state"][:, sl],
                                                    col(chunk_decay, u, ccs[u], h0 + r),
                                                    ps[:, 4 * u + 3, sl], ALU.mult, ALU.add)
                last.then_inc(ddve[u], 1)

        with dve.Fori(0, NG) as g:
            dve.drain()
            for u in range(2):
                dve.memset(delta[u]["state"][:, :], 0.0)
            dve.drain()
            with dve.Fori(0, NCH) as c:
                body(g, c, g * NCH + c)

    def act_sc(act):
        b0 = SEGS["sc"].b0
        act.wait_ge(post_done, before["sc"] + 2)
        with act.Fori(0, 4) as i:
            for v in range(6):
                b = Blk(b0 + v, i * 3)
                split_hi(act, nxt(b))
                act.wait_ge(block_done, num(b) + 1)
                if v % 3 == 0:
                    act.wait_ge(post_done, i * 2 + (before["sc"] + v // 3 + 2))
                o = (bst[:, :], stage_at(0), stage_at(1))[v % 3]
                act.activation(two(o), acc(b), ACT.Copy).then_inc(acc_free, 1)

    def dve_sc(dve):
        b0 = SEGS["sc"].b0
        dve.memset(pc[:, 0:1], 0.0)
        dve.memset(pc[:, T + 1:T + 2], 0.0)
        with dve.Fori(0, 4) as i:
            for v in range(2):
                m = i * 2 + v
                dve.drain()
                dve.wait_ge(acc_free, i * 6 + (b0 + 3 * v + 3))
                dve.tensor_tensor(pc[:, 1:T + 1], stage_at(0), stage_at(1), ALU.mult)
                dve.drain()
                o = stage_at(0)
                for k in range(3):
                    tap = scw[:, bass.ds(m * 3 + k, 1)]
                    if k == 0:
                        dve.tensor_scalar(o, pc[:, 0:T], tap, None, ALU.mult)
                    else:
                        dve.scalar_tensor_tensor(o, pc[:, k:k + T], tap, o, ALU.mult, ALU.add)
                    dve.drain()
                dve.tensor_tensor(tile_at(scy, m), o, bst[:, :], ALU.mult).then_inc(post_done, 1)

    def dve_z(dve):
        def post(j, u):
            x = stage_at(u)
            dve.tensor_tensor(x, x, tile_at(oacc, j), ALU.mult)
            dve.drain()
            return split_store(dve, xbh, xbl, j, x)
        dve_segment(dve, "z", post)

    def dve_ya(dve):
        def post(j, u):
            split_store(dve, xah, xal, j, tile_at(scy, j))
            return dve.tensor_tensor(tile_at(gab, j), tile_at(gab, j), stage_at(u), ALU.mult)
        dve_segment(dve, "ya", post)

    def dve_yb(dve):
        def post(j, u):
            x = stage_at(u)
            dve.tensor_tensor(x, x, tile_at(gab, j + 8), ALU.mult)
            dve.drain()
            dve.tensor_tensor(x, x, tile_at(gab, j), ALU.add)
            dve.drain()
            return split_store(dve, xbh, xbl, j, x)
        dve_segment(dve, "yb", post)

    def act_gated(act, name):
        seg = SEGS[name]
        act.wait_ge(post_done, before[name] + 2)
        with act.Fori(0, seg.n // 2) as i:
            for u in range(2):
                b = Blk(seg.b0 + u, i)
                split_hi(act, nxt(b))
                act.wait_ge(block_done, num(b) + 1)
                if u == 0:
                    act.wait_ge(post_done, i + (before[name] + 2))
                act.activation(two(stage_at(u)), acc(b), ACT.Silu if u == 0 else ACT.Copy).then_inc(acc_free, 1)

    def dve_gated(dve, name):
        seg = SEGS[name]
        with dve.Fori(0, seg.n // 2) as m:
            dve.wait_ge(acc_free, m * 2 + (seg.b0 + 2))
            dve.tensor_tensor(stage_at(0), stage_at(0), stage_at(1), ALU.mult)
            dve.drain()
            split_store(dve, xbh, xbl, m, stage_at(0)).then_inc(post_done, 1)

    def dve_relu2(dve, name):
        def post(j, u):
            x = stage_at(u)
            dve.tensor_tensor(x, x, x, ALU.mult)
            dve.drain()
            return split_store(dve, xbh, xbl, j, x)
        dve_segment(dve, name, post)

    ropes = {"pe": 0, "dve": 0}
    vts = {"pe": 0, "act": 0}
    vt2 = place("vtok_dsa", [C, NCH, 256], F32, phase_at + 24 * F)

    def tiles_odd(e, n, body):
        tiles(e, n, body)
        if n % 2:
            body(n - 1, 0)

    def pe_rope(pe, t0, n):
        k = ropes["pe"]
        ropes["pe"] += n

        def turn(m, u):
            pe.wait_ge(rope_dve, k + m + 1)
            for h in range(2):
                mm = pe.matmul(bank(4 + 2 * u + h), rot[:, :], tile_at(pf, m + t0, HT, h * HT),
                               start=True, stop=True)
            mm.then_inc(rope_pe, 1)

        tiles_odd(pe, n, turn)

    def dve_rope(dve, t0, n):
        k = ropes["dve"]
        ropes["dve"] += n

        def apply(m, u):
            x = tile_at(pf, m + t0)
            dve.drain()
            dve.wait_ge(rope_pe, k + m + 1)
            dve.tensor_tensor(x, x, cossin[:, 0, :], ALU.mult)
            dve.tensor_tensor(two(sq[u][:, :]), pair_of(4 + 2 * u), two(cossin[:, 1, :]), ALU.mult)
            dve.drain()
            dve.tensor_tensor(x, x, sq[u][:, :], ALU.add).then_inc(rope_dve, 1)

        tiles_odd(dve, n, apply)

    def act_vtok(act, t0, n, dst):
        k = vts["act"]
        vts["act"] += n

        def move(m, u):
            act.wait_ge(vt_pe, k + m + 1)
            act.activation(stage_at(u), tile_at(pf, m + t0), ACT.Copy).then_inc(vt_in, 1)
            act.wait_ge(vt_pe, k + m + 3)
            act.activation(dst[:, 0:4, bass.ds(m * P, P)],
                           ps[0:C, 4 + 2 * u, :].rearrange("p (c n) -> p c n", n=P), ACT.Copy)
            last = act.activation(dst[0:ROWS[4], 4, bass.ds(m * P, P)], ps[0:ROWS[4], 5 + 2 * u, 0:P], ACT.Copy)
            last.then_inc(vt_out, 1)

        tiles(act, n, move)

    def pe_vtok(pe, n):
        k = vts["pe"]
        vts["pe"] += n

        def turn(m, u):
            pe.wait_ge(vt_in, k + m + 1)
            pe.wait_ge(vt_out, k + m + 1)
            for c in range(NCH):
                mm = pe.transpose(ps[0:ROWS[c], 4 + 2 * u + c // 4, (c % 4) * P:(c % 4 + 1) * P],
                                  stage[:, u * T + c * C:u * T + ENDS[c]], ident[:, :])
            mm.then_inc(vt_pe, 1)

        tiles(pe, n, turn)

    IX = 2 * (NCH - 1)

    def index_loop(e, body):
        with e.Fori(0, 4) as m:
            body(m)

    def zero_halves(pool):
        pool.memset(qz[64:P, 0, :], 0.0)
        pool.memset(qz[0:64, 1, :], 0.0)

    def heads_apart(pool, x):
        pool.tensor_copy(qz[0:64, 0, :], x[0:64])
        return pool.tensor_copy(qz[64:P, 1, :], x[64:P])

    def pool_index(pool):
        def body(m):
            x = tile_at(pf, pool.snap(m + 12))
            pool.wait_ge(ix_pe, m * IX + 2)
            heads_apart(pool, x).then_inc(ix_q, 1)
        zero_halves(pool)
        index_loop(pool, body)

    def pe_index(pe):
        pe.sem_inc(ix_pe, 2)

        def body(m):
            pe.wait_ge(ix_q, m + 1)
            for k in range(IX):
                hh, t = divmod(k, NCH - 1)
                t += 1
                pe.wait_ge(ix_act, m * IX + (k + 1))
                for x, (o, c) in enumerate(pieces(ENDS[t])):
                    mm = pe.matmul(ps[0:ROWS[t], 2 * (k % 2) + x, 0:c], qz[:, hh, C * t:ENDS[t]],
                                   pf[:, 16 * T + o:16 * T + o + c], start=True, stop=True)
                mm.then_inc(ix_pe, 1)
        index_loop(pe, body)

    def psum_cols(b, rows, n):
        return ps[0:rows, b, 0:n] if n <= 512 else pair_of(b, rows)

    def as_psum(ap, n):
        return ap if n <= 512 else two(ap)

    def act_index(act):
        act.sem_inc(ix_act, 2)

        def body(m):
            for k in range(IX):
                n, rows = ENDS[k % (NCH - 1) + 1], ROWS[k % (NCH - 1) + 1]
                act.wait_ge(ix_pe, m * IX + (k + 3))
                act.wait_ge(ix_dve, m * IX + (k + 1))
                act.activation(as_psum(score[k % 2][0:rows, 0:n], n), psum_cols(2 * (k % 2), rows, n),
                               ACT.Relu).then_inc(ix_act, 1)
        index_loop(act, body)

    def rows_of(buf, t):
        return buf[0:ROWS[t], t, 0:ENDS[t]]

    def dve_index(dve):
        for t in range(1, NCH):
            dve.memset(rows_of(bias, t), 0.0)
        dve.sem_inc(ix_dve, 2)

        def body(m):
            for k in range(IX):
                hh, t = divmod(k, NCH - 1)
                t += 1
                if k % (NCH - 1) == 0:
                    dve.drain()
                    head = dve.snap(m * 2 + hh)
                dve.wait_ge(ix_act, m * IX + (k + 3))
                dve.scalar_tensor_tensor(rows_of(bias, t), score[k % 2][0:ROWS[t], 0:ENDS[t]],
                                         wit[0:ROWS[t], t, bass.ds(head, 1)], rows_of(bias, t),
                                         ALU.mult, ALU.add).then_inc(ix_dve, 1)
        index_loop(dve, body)

    def dve_topk(dve):
        dve.drain()
        for t in range(1, NCH):
            x = bias[0:ROWS[t], t, C * t:ENDS[t]]
            dve.scalar_tensor_tensor(x, causal[0:ROWS[t], 0:ROWS[t]], LOWEST / NEG, x, ALU.mult, ALU.add)
        dve.drain()
        for t in range(1, NCH):
            dve.tensor_copy(rows_of(work, t), rows_of(bias, t))
        dve.drain()
        with dve.Fori(0, TOPK // 8):
            for t in range(1, NCH):
                dve.max(top8[0:ROWS[t], 8 * t:8 * t + 8], rows_of(work, t))
            dve.drain()
            for t in range(1, NCH):
                dve.match_replace(rows_of(work, t), top8[0:ROWS[t], 8 * t:8 * t + 8], rows_of(work, t), LOWEST)
            dve.drain()
        for t in range(1, NCH):
            dve.tensor_tensor(rows_of(bias, t), rows_of(work, t), rows_of(bias, t), ALU.is_equal)
        dve.drain()
        for t in range(1, NCH):
            dve.tensor_scalar(rows_of(mask16, t), rows_of(bias, t), NEG, None, ALU.mult)
        dve.tensor_copy(mask16[:, 0, 0:C], causal[:, :])
        dve.tensor_copy(ident16[:, :], ident[:, 0:C])

    UN = 2 * NCH
    calls = {"pe": 0, "act": 0, "dve": 0, "pool": 0}

    def att_loop(e, who, body):
        call = calls[who]
        calls[who] += 1
        with e.Fori(0, 2) as a:
            with e.Fori(0, 4) as r:
                m = a * 4 + r
                body(a, m, m + 8 * call)

    def pool_attention(pool):
        zero_halves(pool)
        pool.drain().then_inc(at_zero, 1)

    def pe_attention(pe, fox):
        v = vtok if fox else vt2
        if not fox:
            for ring in (at_s, at_pt, at_o):
                pe.sem_inc(ring, 2)

        def body(a, m, g):
            def scores(k):
                hh, t = divmod(k, NCH)
                rows = ROWS[t]
                if k >= 2:
                    pe.wait_ge(at_p, g * UN + (k - 1))
                kt_ = m if fox else a + 8
                for x, (o, c) in enumerate(pieces(ENDS[t])):
                    s = ps[0:rows, 2 * (k % 2) + x, 0:c]
                    pe.matmul(s, qz[:, hh, t * C:ENDS[t]], pf[:, bass.ds(kt_ * T + o, c)], start=True, stop=False)
                    if fox:
                        diagonal = o + c == ENDS[t]
                        mm = pe.matmul(s, headrow[:, hh, 0:rows], decay_row[:, o:o + c], start=False,
                                       stop=not diagonal)
                        if diagonal:
                            mm = pe.matmul(ps[0:rows, 2 * (k % 2) + x, c - rows:c], ident16[0:rows, 0:rows],
                                           mask16[0:rows, 0, 0:rows], start=False, stop=True)
                    else:
                        mm = pe.matmul(s, ident16[0:rows, 0:rows], mask16[0:rows, t, o:o + c], start=False,
                                       stop=True)
                mm.then_inc(at_s, 1)

            def turn(k):
                t = k % NCH
                pe.wait_ge(at_p, g * UN + (k + 1))
                pe.wait_ge(at_pte, g * UN + (k + 1))
                rows = ROWS[t]
                for kb in range(t + 1):
                    mm = pe.transpose(ps[0:ROWS[kb], 4 + kb // 4, (kb % 4) * rows:(kb % 4 + 1) * rows],
                                      prob[k % 2][0:rows, kb * C:ENDS[kb]], ident[0:rows, 0:rows])
                mm.then_inc(at_pt, 1)

            def values(k):
                hh, t = divmod(k, NCH)
                pe.wait_ge(at_pte, g * UN + (k + 2))
                if k >= 2:
                    pe.wait_ge(at_oe, g * UN + (k - 1))
                rows = ROWS[t]
                for kb in range(t + 1):
                    mm = pe.matmul(ps[0:rows, 6 + k % 2, t * 64:(t + 1) * 64],
                                   ptr[k % 2][0:ROWS[kb], kb * rows:(kb + 1) * rows],
                                   v[0:ROWS[kb], kb, bass.ds((m if fox else a) * P + 64 * hh, 64)],
                                   start=(kb == 0), stop=(kb == t))
                mm.then_inc(at_o, 1)

            if fox:
                pe.wait_ge(at_row, m + 1)
            pe.wait_ge(at_q, g + 1)
            scores(0)
            scores(1)
            pe.wait_ge(at_of, g + 1)
            for k in range(UN):
                if k + 2 < UN:
                    scores(k + 2)
                turn(k)
                if k:
                    values(k - 1)
            values(UN - 1)
            pe.wait_ge(at_oe, g * UN + UN)
            for t in range(NCH):
                for x in range(2):
                    lo, hi = max(t * C, x * HT), min(ENDS[t], (x + 1) * HT)
                    if lo < hi:
                        rows = slice(lo - t * C, hi - t * C)
                        mm = pe.matmul(ps[:, 4 + x, lo - x * HT:hi - x * HT], otok[0:ROWS[t], t * P:(t + 1) * P],
                                       ident[0:ROWS[t], rows], start=True, stop=True)
            mm.then_inc(at_ot, 1)

        att_loop(pe, "pe", body)

    def act_attention(act, fox):
        if not fox:
            act.sem_inc(at_pte, 1)
        act.wait_ge(at_zero, 2 if fox else 1)

        def body(a, m, g):
            def exp(k):
                n, rows = ENDS[k % NCH], ROWS[k % NCH]
                act.wait_ge(at_mx, g * UN + (k + 1))
                act.wait_ge(at_pt, g * UN + (k + 1))
                act.activation(as_psum(prob[k % 2][0:rows, 0:n], n), psum_cols(2 * (k % 2), rows, n), ACT.Exp,
                               bias=rowmax[0:rows, k:k + 1], accum_out=rowsum[0:rows, k:k + 1]).then_inc(at_p, 1)

            def out(k):
                t = k % NCH
                n, rows = min(t + 1, 4) * ROWS[t], ROWS[t]
                act.wait_ge(at_pt, g * UN + (k + 3))
                act.wait_ge(at_o, g * UN + (k + 1))
                last = act.activation(ptr[k % 2][:, 0:n], ps[0:C, 4, 0:n], ACT.Copy)
                if t == 4:
                    last = act.activation(ptr[k % 2][0:rows, n:n + rows], ps[0:rows, 5, 0:rows], ACT.Copy)
                last.then_inc(at_pte, 1)

            x = tile_at(pf, act.snap(m + (16 if fox else 0)))
            act.wait_ge(at_s, g * UN + 2)
            act.activation(qz[0:64, 0, :], x[0:64], ACT.Copy)
            act.activation(qz[64:P, 1, :], x[64:P], ACT.Copy).then_inc(at_q, 1)
            exp(0)
            for k in range(UN):
                if k + 1 < UN:
                    exp(k + 1)
                out(k)

        att_loop(act, "act", body)

    def dve_attention(dve, fox):
        if not fox:
            dve.sem_inc(at_of, 1)
        else:
            dve.memset(headrow[:, :, :], 0.0)
            dve.drain()

        def body(a, m, g):
            def top(k):
                n, rows = ENDS[k % NCH], ROWS[k % NCH]
                dve.wait_ge(at_s, g * UN + (k + 3))
                dve.tensor_reduce(rowmax[0:rows, k:k + 1], psum_cols(2 * (k % 2), rows, n),
                                  AX.X if n <= 512 else AX.XY, ALU.max, negate=True).then_inc(at_mx, 1)

            def out(k):
                hh, t = divmod(k, NCH)
                rows = ROWS[t]
                dve.wait_ge(at_o, g * UN + (k + 3))
                dve.reciprocal(rowinv[0:rows, k:k + 1], rowsum[0:rows, k:k + 1])
                dve.drain()
                dve.tensor_scalar(otok[0:rows, t * P + 64 * hh:t * P + 64 * hh + 64],
                                  ps[0:rows, 6 + k % 2, t * 64:(t + 1) * 64], rowinv[0:rows, k:k + 1], None,
                                  ALU.mult).then_inc(at_oe, 1)

            if fox:
                heads_ = [dve.snap(m * 2 + hh) for hh in range(2)]
                dve.wait_ge(at_s, g * UN + 2)
                for hh in range(2):
                    for part in range(3):
                        last = dve.tensor_copy(headrow[32 * part:32 * part + 16, hh, :],
                                               ident[0:16, bass.ds(heads_[hh], 1)].broadcast_to([16, C]))
                last.then_inc(at_row, 1)
            for k in range(UN):
                top(k)
                if k >= 2:
                    out(k - 2)
            out(UN - 2)
            out(UN - 1)
            dve.wait_ge(at_ot, g + 1)
            dve.tensor_scalar(two(tile_at(xbh, m)), pair_of(4), 1.0, None, ALU.mult)
            dve.drain()
            dve.tensor_tensor(two(tile_at(xbl, m)), pair_of(4), two(tile_at(xbh, m).bitcast(F32)),
                              ALU.subtract)
            dve.drain().then_inc(at_of, 1)

        att_loop(dve, "dve", body)

    def pe_wit(pe):
        for c in range(NCH):
            mm = pe.transpose(ps[0:ROWS[c], 0, c * 8:(c + 1) * 8], wi[:, c * C:ENDS[c]], ident[0:8, 0:8])
        mm.then_inc(wit_pe, 1)

    def act_wit(act):
        act.wait_ge(wit_pe, 1)
        for c in range(NCH):
            act.activation(wit[0:ROWS[c], c, :], ps[0:ROWS[c], 0, c * 8:(c + 1) * 8], ACT.Copy)

    def act_dsa(act):
        def body(j, u, b):
            split_hi(act, nxt(b))
            act.wait_ge(block_done, num(b) + 1)
            if isinstance(j, int) and j == 17:
                act.activation(two(wi[:, :]), acc(b, 8), ACT.Copy, scale=8 ** -0.5 * 64 ** -0.5).then_inc(acc_free, 1)
            else:
                act.activation(two(tile_at(pf, j)), acc(b), ACT.Copy).then_inc(acc_free, 1)
        blocks(act, SEGS["dsa"], body, last=1)

    def act_foxf(act):
        b = Blk(SEGS["foxf"].b0, 0)
        split_hi(act, nxt(b))
        act.wait_ge(block_done, num(b) + 1)
        act.activation(two(lfneg[:, :]), acc(b, 16), ACT.Copy).then_inc(acc_free, 1)

    def dve_forget(dve):
        dve.tensor_scalar(lfneg[:, :], lfneg[:, :], rowvec[:, 2:3], -1.0, ALU.add, ALU.mult)
        dve.drain()
        dve_softplus(dve, cneg[:, :], lfneg[:, :])
        dve.memset(sp[0][:, :], 1.0)
        dve.drain()
        dve.tensor_tensor_scan(lfneg[:, :], sp[0][:, :], cneg[:, :], 0.0, ALU.mult, ALU.add)
        dve.memset(decay_row[:, :], 0.0)
        for part in range(3):
            dve.drain()
            rows = slice(32 * part, 32 * part + 16)
            dve.tensor_copy(decay_row[rows, :], lfneg[:, :])
            dve.drain()
            if part < 2:
                dve.tensor_tensor(lfneg[:, :], lfneg[:, :], decay_row[rows, :], ALU.subtract)

    def up(j, u):
        return stage_at(u)

    consts = (
        (res[:, :].rearrange("p (k t) -> p k t", t=T), io["x"].rearrange("k p t -> p k t")),
        (gains[:, :], io["gains"]), (headgain[:, 0:5], io["headgain"]), (rowvec[:, 0:4], io["rowvec"]),
        (ident[:, :], io["ident"]), (win128[:, :], io["win128"]), (win64[:, :], io["win64"]),
        (convw[:, :], io["convw"]), (scw[:, :], io["scw"]), (tri[:, :, :], io["tri"]),
        (masks[:, :, :, :], io["masks"]), (sel[:, :, :, :], io["sel"]))

    def loaded(e):
        e.wait_ge(const_in, 16 * len(consts))

    with nc.Block() as block:
        @block.tensor
        def _(pe):
            loaded(pe)
            for ring in (nused, hused, vt_pe):
                pe.sem_inc(ring, 2)
            pe.wait_ge(prep_dve_ones, 1)
            pe_norm(pe)
            barrier(pe, "pe")
            pe_segment(pe, "ba", xah, xal)
            pe_segment(pe, "qkv", xah, xal)
            pe_headnorm(pe, 16, P)
            barrier(pe, "pe")
            pe_prep(pe)
            barrier(pe, "pe")
            pe_delta(pe)
            barrier(pe, "pe")
            pe_headnorm(pe, 8, P)
            barrier(pe, "pe")
            pe_segment(pe, "z", xah, xal)
            pe_segment(pe, "sc", xah, xal)
            pe_segment(pe, "gates", xah, xal)
            pe_segment(pe, "ya", xbh, xbl)
            pe_segment(pe, "yb", xah, xal)
            pe_segment(pe, "wout", xbh, xbl)
            barrier(pe, "pe")
            pe_norm(pe)
            barrier(pe, "pe")
            for p in range(len(FF1_PARTS)):
                pe_segment(pe, f"gu{p}", xah, xal)
                pe_segment(pe, f"dn{p}", xbh, xbl)
            barrier(pe, "pe")
            pe_norm(pe)
            barrier(pe, "pe")
            barrier(pe, "pe")
            pe_norm(pe)
            barrier(pe, "pe")
            pe_segment(pe, "dsa", xah, xal)
            barrier(pe, "pe")
            pe_headnorm(pe, 8, 64)
            pe_headnorm(pe, 2, 64)
            barrier(pe, "pe")
            pe_rope(pe, 0, 10)
            pe_rope(pe, 12, 5)
            barrier(pe, "pe")
            pe_vtok(pe, 2)
            pe_wit(pe)
            barrier(pe, "pe")
            pe_index(pe)
            barrier(pe, "pe")
            pe_attention(pe, False)
            barrier(pe, "pe")
            pe_segment(pe, "dsa_out", xbh, xbl)
            barrier(pe, "pe")
            pe_norm(pe)
            barrier(pe, "pe")
            for p in range(len(FF2_PARTS)):
                pe_segment(pe, f"up0_{p}", xah, xal)
                pe_segment(pe, f"down0_{p}", xbh, xbl)
            barrier(pe, "pe")
            pe_norm(pe)
            barrier(pe, "pe")
            pe_segment(pe, "foxkv", xah, xal)
            pe_segment(pe, "foxf", xah, xal)
            pe_segment(pe, "foxq", xbh, xbl)
            barrier(pe, "pe")
            pe_headnorm(pe, 8, 64)
            pe_headnorm(pe, 8, 64)
            barrier(pe, "pe")
            pe_vtok(pe, 8)
            barrier(pe, "pe")
            pe_attention(pe, True)
            barrier(pe, "pe")
            pe_segment(pe, "fox_out", xbh, xbl)
            barrier(pe, "pe")
            pe_norm(pe)
            barrier(pe, "pe")
            for p in range(len(FF2_PARTS)):
                pe_segment(pe, f"up1_{p}", xah, xal)
                pe_segment(pe, f"down1_{p}", xbh, xbl)
            barrier(pe, "pe")

        @block.scalar
        def _(act):
            loaded(act)
            for ring in (silu_done, vt_out):
                act.sem_inc(ring, 2)
            act.wait_ge(prep_dve_ones, 1)
            act_norm(act)
            act_norm_apply(act, xah)
            split_hi(act, Blk(0, 0))
            barrier(act, "act")
            act_ba(act)
            act_qkv(act)
            act.activation(rowvec[:, 4:5], rowvec[:, 1:2], ACT.Exp).then_inc(prep_act, 1)
            act_softplus(act, gdec[:, 0:T])
            act_headnorm(act, qkv, 0, 16, P, 1.0)
            barrier(act, "act")
            act_prep(act)
            barrier(act, "act")
            act_delta(act)
            barrier(act, "act")
            act_headnorm(act, oacc, 0, 8, P, 1.0 / P)
            barrier(act, "act")
            act_segment(act, "z", up, ACT.Silu, posts=True)
            act_sc(act)
            act_segment(act, "gates", lambda j, u: tile_at(gab, j), ACT.Sigmoid)
            for name in ("ya", "yb", "wout"):
                act_segment(act, name, up, posts=True)
            barrier(act, "act")
            act_norm(act)
            act_norm_apply(act, xah)
            barrier(act, "act")
            for p in range(len(FF1_PARTS)):
                act_gated(act, f"gu{p}")
                act_segment(act, f"dn{p}", up, posts=True)
            barrier(act, "act")
            act_norm(act)
            barrier(act, "act")
            for dst, src in ((res[:, :].rearrange("p (k t) -> p k t", t=T)[:, :, 0:NMETA],
                              io["meta2"].rearrange("k p t -> p k t")),
                             (causal[:, :], io["causal"]), (cossin[:, :, :], io["cossin"]), (rot[:, :], io["rot"])):
                act.dma_start(dst, src).then_inc(const2_in, 16)
            act.wait_ge(const2_in, 64)
            barrier(act, "act")
            act_norm(act)
            act_norm_apply(act, xah)
            barrier(act, "act")
            act_dsa(act)
            barrier(act, "act")
            act_headnorm(act, pf, 0, 8, 64, 1.0 / 64)
            act_headnorm(act, pf, 8, 2, 64, 1.0 / 64)
            barrier(act, "act")
            barrier(act, "act")
            act_vtok(act, 10, 2, vt2)
            act_wit(act)
            barrier(act, "act")
            act_index(act)
            barrier(act, "act")
            act_attention(act, False)
            barrier(act, "act")
            act_segment(act, "dsa_out", up, posts=True)
            barrier(act, "act")
            act_norm(act)
            act_norm_apply(act, xah)
            barrier(act, "act")
            for p in range(len(FF2_PARTS)):
                act_segment(act, f"up0_{p}", up, ACT.Relu, posts=True)
                act_segment(act, f"down0_{p}", up, posts=True)
            barrier(act, "act")
            act_norm(act)
            act_norm_apply(act, xah)
            act_norm_apply(act, xbh)
            barrier(act, "act")
            act_segment(act, "foxkv", lambda j, u: tile_at(pf, j))
            act_foxf(act)
            act_segment(act, "foxq", lambda j, u: tile_at(pf, j + 16))
            barrier(act, "act")
            act_softplus(act, lfneg[:, :])
            act_headnorm(act, pf, 0, 8, 64, 1.0 / 64)
            act_headnorm(act, pf, 16, 8, 64, 1.0 / 64)
            barrier(act, "act")
            act_vtok(act, 8, 8, vtok)
            barrier(act, "act")
            act_attention(act, True)
            barrier(act, "act")
            act_segment(act, "fox_out", up, posts=True)
            barrier(act, "act")
            act_norm(act)
            act_norm_apply(act, xah)
            barrier(act, "act")
            for p in range(len(FF2_PARTS)):
                act_segment(act, f"up1_{p}", up, ACT.Relu, posts=True)
                act_segment(act, f"down1_{p}", up, posts=True)
            barrier(act, "act")

        @block.vector
        def _(dve):
            for ring in (post_done, conv_done, happ, rope_dve):
                dve.sem_inc(ring, 2)
            dve.memset(ones[:, :], 1.0)
            dve.memset(eps[:, :], EPS)
            dve.drain().then_inc(prep_dve_ones, 1)
            loaded(dve)
            for k in (1, 4):
                dve.tensor_scalar(headgain[:, k:k + 1], headgain[:, k:k + 1], 64 ** -0.5, None, ALU.mult)
            dve_norm(dve)
            dve_norm_apply(dve, 0)
            barrier(dve, "dve")
            dve_qkv(dve)
            dve_decay(dve)
            dve_headnorm(dve, qkv, 0, 16, P, 1.0, rowvec[:, 3:4])
            barrier(dve, "dve")
            dve_prep(dve)
            barrier(dve, "dve")
            dve_delta(dve)
            barrier(dve, "dve")
            dve_headnorm(dve, oacc, 0, 8, P, headgain[:, 0:1])
            barrier(dve, "dve")
            dve_z(dve)
            dve_sc(dve)
            dve_ya(dve)
            dve_yb(dve)
            dve_segment(dve, "wout", add_residual(dve))
            barrier(dve, "dve")
            dve_norm(dve)
            dve_norm_apply(dve, 1)
            barrier(dve, "dve")
            for p in range(len(FF1_PARTS)):
                dve_gated(dve, f"gu{p}")
                dve_segment(dve, f"dn{p}", add_residual(dve))
            barrier(dve, "dve")
            dve_norm(dve)
            tiles(dve, KT, lambda m, u: dve.scalar_tensor_tensor(
                tile_at(res, m), tile_at(res, m), gains[:, bass.ds(m + 2 * KT, 1)], rstd[:, :],
                ALU.mult, ALU.mult))
            barrier(dve, "dve")
            barrier(dve, "dve")
            dve_norm(dve)
            dve_norm_apply(dve, 3)
            barrier(dve, "dve")
            barrier(dve, "dve")
            dve_headnorm(dve, pf, 0, 8, 64, headgain[:, 1:2])
            dve_headnorm(dve, pf, 8, 2, 64, headgain[:, 2:3])
            barrier(dve, "dve")
            dve_rope(dve, 0, 10)
            dve_rope(dve, 12, 5)
            barrier(dve, "dve")
            barrier(dve, "dve")
            dve_index(dve)
            dve_topk(dve)
            barrier(dve, "dve")
            dve_attention(dve, False)
            barrier(dve, "dve")
            dve_segment(dve, "dsa_out", add_residual(dve))
            barrier(dve, "dve")
            dve_norm(dve)
            dve_norm_apply(dve, 4)
            barrier(dve, "dve")
            for p in range(len(FF2_PARTS)):
                dve_relu2(dve, f"up0_{p}")
                dve_segment(dve, f"down0_{p}", add_residual(dve))
            barrier(dve, "dve")
            dve_norm(dve)
            dve_norm_apply(dve, 5)
            dve_norm_apply(dve, 6)
            barrier(dve, "dve")
            barrier(dve, "dve")
            dve_forget(dve)
            dve_headnorm(dve, pf, 0, 8, 64, headgain[:, 3:4])
            dve_headnorm(dve, pf, 16, 8, 64, headgain[:, 4:5])
            barrier(dve, "dve")
            barrier(dve, "dve")
            dve_attention(dve, True)
            barrier(dve, "dve")
            dve_segment(dve, "fox_out", add_residual(dve))
            barrier(dve, "dve")
            dve_norm(dve)
            dve_norm_apply(dve, 7)
            barrier(dve, "dve")
            for p in range(len(FF2_PARTS)):
                dve_relu2(dve, f"up1_{p}")
                dve_segment(dve, f"down1_{p}", add_residual(dve))
            barrier(dve, "dve")

        @block.gpsimd
        def _(pool):
            pool.sem_inc(nlo, 2)
            pool_norm_apply(pool, xah, xal)
            split_lo(pool, Blk(0, 0))
            barrier(pool, "pool")
            pool_segment(pool, "ba")
            pool_segment(pool, "qkv")
            barrier(pool, "pool")
            barrier(pool, "pool")
            pool_delta(pool)
            barrier(pool, "pool")
            barrier(pool, "pool")
            for name in ("z", "sc", "gates", "ya", "yb", "wout"):
                pool_segment(pool, name)
            barrier(pool, "pool")
            pool_norm_apply(pool, xah, xal)
            barrier(pool, "pool")
            for p in range(len(FF1_PARTS)):
                pool_segment(pool, f"gu{p}")
                pool_segment(pool, f"dn{p}")
            barrier(pool, "pool")
            barrier(pool, "pool")
            barrier(pool, "pool")
            pool_norm_apply(pool, xah, xal)
            barrier(pool, "pool")
            pool_segment(pool, "dsa")
            barrier(pool, "pool")
            barrier(pool, "pool")
            barrier(pool, "pool")
            barrier(pool, "pool")
            pool_index(pool)
            barrier(pool, "pool")
            pool_attention(pool)
            barrier(pool, "pool")
            pool_segment(pool, "dsa_out")
            barrier(pool, "pool")
            pool_norm_apply(pool, xah, xal)
            barrier(pool, "pool")
            for p in range(len(FF2_PARTS)):
                pool_segment(pool, f"up0_{p}")
                pool_segment(pool, f"down0_{p}")
            barrier(pool, "pool")
            pool_norm_apply(pool, xah, xal)
            pool_norm_apply(pool, xbh, xbl)
            barrier(pool, "pool")
            pool_segment(pool, "foxkv")
            pool_segment(pool, "foxf")
            pool_segment(pool, "foxq")
            barrier(pool, "pool")
            barrier(pool, "pool")
            barrier(pool, "pool")
            pool_attention(pool)
            barrier(pool, "pool")
            pool_segment(pool, "fox_out")
            barrier(pool, "pool")
            pool_norm_apply(pool, xah, xal)
            barrier(pool, "pool")
            for p in range(len(FF2_PARTS)):
                pool_segment(pool, f"up1_{p}")
                pool_segment(pool, f"down1_{p}")
            barrier(pool, "pool")

        @block.sync
        def _(sp):
            for dst, src in consts:
                sp.dma_start(dst, src).then_inc(const_in, 16)
            load_weights(sp)
            sp.wait_ge(phase_done, 4 * phases["pe"])
            sp.dma_start(out.rearrange("k p t -> p k t"),
                         res[:, :].rearrange("p (k t) -> p k t", t=T)[:, :, NMETA:T]).then_inc(out_sent, 16)
            sp.wait_ge(out_sent, 16)


def constants():
    f = np.float32
    ident = np.eye(P, dtype=f)
    win128 = np.zeros((P, 31), f)
    win128[:, 15] = 1
    win64 = np.zeros((P, 30), f)
    win64[0:64, 14] = 1
    win64[64:128, 15] = 1
    s, i = np.arange(C)[:, None], np.arange(C)[None, :]
    tri = np.stack([s <= i, s >= i], 1).astype(f)
    masks = np.zeros((C, 2, LEVELS, C), f)
    for lv in range(LEVELS):
        b = 2 ** lv
        same = (s // (2 * b)) == (i // (2 * b))
        lo, hi = (s // b) % 2 == 0, (i // b) % 2 == 1
        masks[:, 0, lv, :] = same & lo & hi
        masks[:, 1, lv, :] = same & ~lo & ~hi
    sel = np.zeros((16, 2, NG, GH), f)
    for u in range(2):
        for g in range(NG):
            for r in range(GH):
                sel[8 * u + GH * g + r, u, g, r] = 1
    causal = np.where(s >= i, 0.0, NEG).astype(f)
    inv = (1.0 / (np.float32(10000.0) ** (np.arange(0, 64, 2, dtype=f) / f(64)))).astype(f)
    ang = np.arange(T, dtype=f)[:, None] * inv[None, :]
    cossin = np.stack([np.tile(np.cos(ang).T, (4, 1)), np.tile(np.sin(ang).T, (4, 1))], 1).astype(f)
    rot = np.zeros((P, P), f)
    for h in range(2):
        for d in range(32):
            rot[64 * h + 32 + d, 64 * h + d] = -1
            rot[64 * h + d, 64 * h + 32 + d] = 1
    return dict(ident=ident, win128=win128, win64=win64, tri=tri, masks=masks, sel=sel, causal=causal,
                cossin=np.ascontiguousarray(cossin), rot=rot)


def columns(m):
    k, n = m.shape
    x = m.reshape(k // P, P, n // P, P).transpose(2, 1, 0, 3).reshape(n // P, P, k)
    return x if k == DM else np.concatenate([x, np.zeros((n // P, P, DM - k), x.dtype)], 2)


def widened(m):
    return np.concatenate([m, np.zeros((m.shape[0], P - m.shape[1]), m.dtype)], 1)


def lay_weights(a):
    wi_ = a["w_in"][0]
    cuts = np.cumsum([1024, 1024, 1024, 1024, 16, 16, 1024, 1024, 1024, 1024, 1024])
    q, k, v, z, b, aa, scb, scc, scx, ga, gb = np.split(wi_, cuts[:-1], axis=1)
    out = [columns(widened(b)), columns(widened(aa)), columns(q), columns(k), columns(v), columns(z)]
    out.append(np.stack([columns(scb), columns(scc), columns(scx)], 1).reshape(24, P, DM))
    out += [columns(ga), columns(gb), columns(a["w_branch_dn"][0]), columns(a["w_branch_sc"][0]),
            columns(a["w_out"][0])]
    gu, dn = a["w_gate_up"][0], a["w_down"][0]
    at = 0
    for n in FF1_PARTS:
        g = columns(gu[:, at:at + n * P])
        u = columns(gu[:, FF1 + at:FF1 + at + n * P])
        out.append(np.stack([g, u], 1).reshape(2 * n, P, DM))
        out.append(columns(dn[at:at + n * P]))
        at += n * P
    w = a["a_w_in_2"][0]
    q, k, v, qi, ki, wt = np.split(w, np.cumsum([1024, 256, 256, 512, 64]), axis=1)
    order = dsa_heads()
    q = q.reshape(DM, 16, 64)[:, order].reshape(DM, DM)
    out += [columns(q), columns(k), columns(v), columns(qi), columns(np.concatenate([ki, ki], 1)),
            columns(widened(wt)), columns(a["a_w_out_2"][0].reshape(16, 64, DM)[order].reshape(DM, DM))]

    def mlp(i):
        for p in range(4):
            out.append(columns(a["mlp_w1_2"][i][:, p * DM:(p + 1) * DM]))
            out.append(columns(a["mlp_w2_2"][i][p * DM:(p + 1) * DM]))

    mlp(0)
    kv = a["kv_w_2"]
    out += [columns(kv[:, :2 * DM]), columns(widened(kv[:, 2 * DM:])), columns(a["b_w_q_2"][0]),
            columns(a["b_w_out_2"][0])]
    mlp(1)
    out = np.concatenate(out, 0)
    assert out.shape == (NB, P, DM)
    return out


def dsa_heads():
    return [(2 * (m // 4) + h) * 4 + m % 4 for m in range(8) for h in range(2)]


def lay_inputs(inputs):
    a = {k: np.asarray(v) for k, v in inputs.items()}
    f = np.float32
    x = np.concatenate([a["meta_tokens"], a["x"][0]], 0)
    per = lambda v: v.reshape(KT, P).T
    gains = [a["norm1_w"][0], a["norm2_w"][0], a["final_norm_w"], a["attn_norm_2"][0], a["mlp_norm_2"][0],
             a["kv_norm_2"], a["attn_norm_2"][1], a["mlp_norm_2"][1]]
    twice = lambda v: np.concatenate([v, v])
    qscale = np.array([P ** -0.5] * 8 + [1.0] * 8, f)
    lay = dict(
        w=lay_weights(a),
        x=x.T.reshape(KT, P, T),
        meta2=a["meta_tokens_2"].T.reshape(KT, P, NMETA),
        gains=np.concatenate([per(g) for g in gains], 1),
        headgain=np.stack([a["dn_norm_w"][0], twice(a["a_q_gain_2"][0]), twice(a["a_k_gain_2"][0]),
                           twice(a["kv_k_gain_2"]), twice(a["b_q_gain_2"][0])], 1),
        rowvec=np.stack([a["dt_bias"][0].reshape(16), a["A_log"][0].reshape(16), a["kv_f_bias_2"], qscale], 1),
        convw=a["dn_conv_w"][0].reshape(5, 24, P).transpose(2, 1, 0).reshape(P, 120),
        scw=a["sc_conv_w"][0].reshape(3, 8, P).transpose(2, 1, 0).reshape(P, 24),
        **constants())
    return {k: np.ascontiguousarray(v) for k, v in lay.items()}


def kernel(**inputs):
    import concourse.bacc as bacc
    from concourse.bass_utils import run_bass_kernel_spmd

    nc = bacc.Bacc("TRN2", target_bir_lowering=False, num_devices=1)
    arrays, io = {}, {}
    for name, v in lay_inputs(inputs).items():
        arrays[f"in_{name}"] = v
        io[name] = nc.dram_tensor(f"in_{name}", v.shape, mybir.dt.from_np(v.dtype), kind="ExternalInput").ap()
    io["out"] = nc.dram_tensor("out", (KT, P, SEQ), F32, kind="ExternalOutput").ap()
    build_program(nc, io)
    got = run_bass_kernel_spmd(nc, [arrays], core_ids=[0]).results[0]["out"]
    return np.ascontiguousarray(got.reshape(DM, SEQ).T).reshape(1, SEQ, DM)
```

```python
from collections import namedtuple

import numpy as np

import concourse.bass as bass
from concourse import mybir

F32 = mybir.dt.float32
F32R = mybir.dt.float32r
BF16 = mybir.dt.bfloat16
ALU = mybir.AluOpType
ACT = mybir.ActivationFunctionType
AX = mybir.AxisListType

P = 128
DM = 1024
KT = DM // P
NMETA, SEQ = 16, 512
T = NMETA + SEQ
HT = T // 2
C = 106
NCH = -(-T // C)
TS = NCH * C
ROWS = [min(C, T - t * C) for t in range(NCH)]
ENDS = [min(C * (t + 1), T) for t in range(NCH)]
H1, NG, GH = 8, 2, 4
FF1 = 2816
FF1_PARTS = [8, 8, 6]
FF2_PARTS = [8, 8, 8, 8]
PARTS = 80
LEVELS = 7
TOPK = 128
NEG = -1.0e30
LOWEST = -3.0e38
EPS = 1.0e-6

Blk = namedtuple("Blk", "c i")


def num(b):
    return b.c + 2 * b.i


def slot(b):
    return b.c % 2


def nxt(b, n=1):
    return Blk(b.c + n, b.i)


Seg = namedtuple("Seg", "b0 n k")


def plan_segments():
    segs, at = {}, 0

    def add(name, n, k=KT):
        nonlocal at
        segs[name] = Seg(at, n, k)
        at += n

    add("ba", 2)
    add("qkv", 24)
    add("z", 8)
    add("sc", 24)
    add("gates", 16)
    add("ya", 8)
    add("yb", 8)
    add("wout", 8)
    for p, n in enumerate(FF1_PARTS):
        add(f"gu{p}", 2 * n)
        add(f"dn{p}", 8, n)
    add("dsa", 18)
    add("dsa_out", 8)
    for p, n in enumerate(FF2_PARTS):
        add(f"up0_{p}", n)
        add(f"down0_{p}", 8, n)
    add("foxkv", 16)
    add("foxf", 1)
    add("foxq", 8)
    add("fox_out", 8)
    for p, n in enumerate(FF2_PARTS):
        add(f"up1_{p}", n)
        add(f"down1_{p}", 8, n)
    return segs, at


SEGS, NB = plan_segments()


def wait(e, sem, value):
    if isinstance(value, int) and value <= 0:
        return
    e.wait_ge(sem, value)


def blocks(e, seg, body, first=0, last=0):
    pairs = seg.n // 2
    for i in range(first):
        for u in range(2):
            body(2 * i + u, u, Blk(seg.b0 + 2 * i + u, 0))
    if pairs - last > first:
        with e.Fori(first, pairs - last) as i:
            for u in range(2):
                body(i * 2 + u, u, Blk(seg.b0 + u, i))
    for i in range(pairs - last, pairs):
        for u in range(2):
            body(2 * i + u, u, Blk(seg.b0 + 2 * i + u, 0))
    if seg.n % 2:
        body(seg.n - 1, 0, Blk(seg.b0 + seg.n - 1, 0))


def tiles(e, n, body):
    with e.Fori(0, n // 2) as i:
        for u in range(2):
            body(i * 2 + u, u)


def pieces(n):
    return [(0, n)] if n <= 512 else [(0, HT), (HT, HT)]


def build_program(nc, io):
    w, out, nb = io["w"], io["out"], NB

    base = 16512
    F = 4 * T

    def place(name, shape, dt, offset):
        return nc.alloc_sbuf_tensor_at(name, shape, dt, offset=offset)

    def region(start):
        pos = [start]

        def sb(name, shape, dt=F32):
            n = 2 if dt == BF16 else 4
            for s in shape[1:]:
                n *= s
            n = -(-n // 32) * 32
            off = pos[0]
            pos[0] += n
            return place(name, shape, dt, off)

        sb.pos = pos
        return sb

    keep = region(base)
    res = keep("res", [P, KT * T])
    a_at = keep.pos[0]
    xah, xal = keep("xah", [P, KT * T], F32R), keep("xal", [P, KT * T], F32R)
    b_at = keep.pos[0]
    xbh, xbl = keep("xbh", [P, KT * T], F32R), keep("xbl", [P, KT * T], F32R)
    wraw = keep("wraw", [P, 2 * DM])
    wh, wl = keep("wh", [P, 2 * DM], F32R), keep("wl", [P, 2 * DM], F32R)
    stage_pos = keep.pos[0]
    stage = keep("stage", [P, 2 * T])
    ident = keep("ident", [P, P])
    ones = keep("ones", [P, P])
    win128 = keep("win128", [P, 31])
    win64 = keep("win64", [P, 30])
    gains = keep("gains", [P, 8 * KT])
    headgain = keep("headgain", [P, 8])
    rowvec = keep("rowvec", [16, 8])
    eps = keep("eps", [P, 1])
    rstd = keep("rstd", [P, T])
    phase_at = keep.pos[0]

    r1 = region(phase_at)
    qkv = r1("qkv", [P, 24 * TS])
    oacc = r1("oacc", [P, 8 * TS])
    convw = r1("convw", [P, 24 * 5])
    scw = r1("scw", [P, 8 * 3])
    tri = r1("tri", [C, 2, C])
    masks = r1("masks", [C, 2, LEVELS, C])
    sel = r1("sel", [16, 2, NG, GH])
    scum = r1("scum", [16, 2, TS])
    tok_g = r1("tok_g", [C, NCH, 16])
    tok_b = r1("tok_b", [C, NCH, 16])
    tok_cum = r1("tok_cum", [C, 2, NCH, 8])
    tok_neg = r1("tok_neg", [C, 2, NCH, 8])
    tok_bk = r1("tok_bk", [C, 2, NCH, 8])
    chunk_decay = r1("chunk_decay", [P, 2, NCH, 8])
    d_at = r1.pos[0]
    assert d_at <= nc.sbuf_usable_end, d_at
    rb = region(b_at)
    cpad = [rb(f"cpad{u}", [P, T + 4]) for u in range(2)]
    cout = [rb(f"cout{u}", [P, T]) for u in range(2)]
    sq = [rb(f"sq{u}", [P, T]) for u in range(2)]
    hroot = rb("hroot", [32, T])
    hinv = rb("hinv", [P, T])
    beta = rb("beta", [16, TS])
    gdec = rb("gdec", [16, TS])
    sp = [rb(f"sp{i}", [16, T]) for i in range(5)]
    spread = place("spread", [P, 8 * P], F32, b_at)
    assert 4 * 8 * P <= 8 * (T + 4)
    delta = []
    rx = region(b_at)
    ry = region(d_at)

    def dsb(name, shape):
        n = 4
        for s in shape[1:]:
            n *= s
        r = rx if rx.pos[0] + n <= b_at + 2 * KT * F else ry
        return r(name, shape)

    W4 = GH * C
    for u in range(2):
        d = {}
        d["ks"] = dsb(f"ks{u}", [P, W4])
        d["qd"] = dsb(f"qd{u}", [P, W4])
        d["state"] = dsb(f"state{u}", [P, GH * P])
        d["kt"] = dsb(f"kt{u}", [C, GH * P])
        d["vt"] = dsb(f"vt{u}", [C, GH * P])
        d["qkm"] = dsb(f"qkm{u}", [C, W4])
        r = rx if rx.pos[0] + 4 * W4 <= b_at + 2 * KT * F else ry
        o = r.pos[0]
        d["xt"] = r(f"xt{u}", [C, W4])
        d["grow"] = place(f"grow{u}", [16, W4], F32, o)
        r = rx if rx.pos[0] + 2 * 4 * W4 <= b_at + 2 * KT * F else ry
        o = r.pos[0]
        d["qs"], d["vs"] = r(f"qs{u}", [P, W4]), r(f"vs{u}", [P, W4])
        d["rr"] = place(f"rr{u}", [C, GH * P], F32, o)
        r = rx if rx.pos[0] + 2 * 4 * W4 <= b_at + 2 * KT * F else ry
        o = r.pos[0]
        d["dec"], d["ob"] = r(f"dec{u}", [C, W4]), r(f"ob{u}", [C, W4])
        d["vn"] = place(f"vn{u}", [C, GH * P], F32, o)
        r = rx if rx.pos[0] + 2 * 4 * W4 <= b_at + 2 * KT * F else ry
        o = r.pos[0]
        d["pp"], d["xx"] = r(f"pp{u}", [C, W4]), r(f"xx{u}", [C, W4])
        d["vk"] = place(f"vk{u}", [C, GH * P], F32, o)
        d["mt"] = place(f"mt{u}", [C, W4], F32, stage_pos + u * 4 * W4)
        delta.append(d)
    assert ry.pos[0] <= nc.sbuf_usable_end, (ry.pos[0], nc.sbuf_usable_end)
    scy = place("scy", [P, 8 * T], F32, phase_at)
    gab = place("gab", [P, 16 * T], F32, phase_at + 8 * F)
    rsc = region(d_at)
    pc = rsc("pc", [P, T + 2])
    bst = rsc("bst", [P, T])

    r2 = region(phase_at)
    pf = r2("pf", [P, 24 * T])
    vtok = r2("vtok", [C, NCH, DM])
    causal = r2("causal", [C, C])
    mask16 = r2("mask16", [C, NCH, T], BF16)
    ident16 = r2("ident16", [P, C], BF16)
    assert r2.pos[0] <= nc.sbuf_usable_end, r2.pos[0]
    rdsa = region(phase_at + 17 * F)
    wi = rdsa("wi", [8, T])
    bias = rdsa("bias", [C, NCH, T])
    assert rdsa.pos[0] <= phase_at + 24 * F
    rv = region(phase_at + 24 * F + NCH * 256 * 4)
    cossin = rv("cossin", [P, 2, T])
    rot = rv("rot", [P, P])
    wit = rv("wit", [C, NCH, 8])
    assert rv.pos[0] <= phase_at + 24 * F + NCH * DM * 4
    rt = region(a_at)
    qz = rt("qz", [P, 4, T])
    score = [rt(f"score{u}", [C, T]) for u in range(2)]
    prob = [rt(f"prob{u}", [C, T]) for u in range(2)]
    ptr = [rt(f"ptr{u}", [C, T]) for u in range(2)]
    otok = rt("otok", [C, 2, NCH * P])
    headrow = rt("headrow", [PARTS, 4, C], BF16)
    decay_row = rt("decay_row", [PARTS, T], BF16)
    rowmax = rt("rowmax", [C, 4 * NCH])
    rowsum = rt("rowsum", [C, 4 * NCH])
    rowinv = rt("rowinv", [C, 4 * NCH])
    top8 = rt("top8", [C, NCH * 8])
    lfneg = rt("lfneg", [16, T])
    cneg = rt("cneg", [16, T])
    assert rt.pos[0] <= b_at
    rtk = region(a_at)
    work = rtk("work", [C, NCH, T])
    nsqr = [place(f"nsqr{u}", [P, T], F32, a_at + u * F) for u in range(2)]
    ps = nc.alloc_psum_tensor("ps", [P, 8, 512], F32)

    def sem(name):
        return nc.alloc_semaphore(name)

    raw_full = [sem("raw_full0"), sem("raw_full1")]
    hi_done, lo_done = sem("hi_done"), sem("lo_done")
    block_done = sem("block_done")
    acc_free = sem("acc_free")
    post_done = sem("post_done")
    phase_done = sem("phase_done")
    const_in, const2_in, out_sent = sem("const_in"), sem("const2_in"), sem("out_sent")
    nsq, nused, nsum, nroot, nscaled, nhi, nlo = map(sem, (
        "norm_square", "norm_square_used", "norm_sum", "norm_root", "norm_scaled", "norm_hi", "norm_lo"))
    hsq, hused, hsum, hrt, hiv, hbc, happ = map(sem, (
        "head_square", "head_square_used", "head_sum", "head_root", "head_inverse", "head_spread",
        "head_applied"))
    conv_done, silu_done = sem("conv_done"), sem("silu_done")
    sp_abs, sp_exp = sem("softplus_abs"), sem("softplus_exp")
    prep_pe, prep_act, prep_dve = sem("prep_pe"), sem("prep_act"), sem("prep_dve")
    dpe = [sem("delta_pe0"), sem("delta_pe1")]
    dact = [sem("delta_act0"), sem("delta_act1")]
    ddve = [sem("delta_dve0"), sem("delta_dve1")]
    dpool = [sem("delta_pool0"), sem("delta_pool1")]
    rope_pe, rope_cos, rope_dve = sem("rope_turned"), sem("rope_cosine"), sem("rope_applied")
    vt_in, vt_pe, vt_out = sem("v_staged"), sem("v_turned"), sem("v_stored")
    ix_q, ix_pe, ix_act, ix_dve = sem("index_q"), sem("index_logits"), sem("index_relu"), sem("index_added")
    wit_pe, prep_dve_ones = sem("index_weights_turned"), sem("ones_ready")
    at_zero, at_row, at_q, at_s, at_mx = map(sem, (
        "att_zeroed", "att_head_row", "att_q", "att_scores", "att_max"))
    at_p, at_pt, at_pte, at_o, at_oe, at_ot, at_of = map(sem, (
        "att_prob", "att_prob_turned", "att_prob_out", "att_value", "att_value_out", "att_turned",
        "att_stored"))

    before, total = {}, 0
    for name, seg in SEGS.items():
        before[name] = total
        if name in ("z", "sc", "ya", "yb", "wout", "dsa_out", "fox_out") or name[:2] in ("dn", "up") \
                or name.startswith("down"):
            total += 8 if name == "sc" else seg.n
        elif name.startswith("gu"):
            total += seg.n // 2

    norms = {"pe": 0, "act": 0, "dve": 0}
    applied = {"act": 0, "dve": 0, "pool": 0}
    phases = {"pe": 0, "act": 0, "dve": 0, "pool": 0}

    def barrier(e, who):
        phases[who] += 1
        e.drain().then_inc(phase_done, 1)
        e.wait_ge(phase_done, 4 * phases[who])

    def bank(b, rows=P, n=HT, off=0):
        return ps[0:rows, b, off:off + n]

    def pair_of(b, rows=P):
        return ps[0:rows, b:b + 2, 0:HT]

    def two(ap):
        return ap.rearrange("p (h t) -> p h t", h=2)

    def tile_at(buf, m, n=T, off=0):
        step = TS if buf is qkv or buf is oacc else T
        return buf[:, bass.ds(m * step + off, n)]

    def load_weights(sp):
        def load(b):
            wait(sp, lo_done, num(b) - 1)
            sp.dma_start(wraw[:, slot(b) * DM:(slot(b) + 1) * DM],
                         w[bass.ds(num(b), 1)].rearrange("a p n -> (a p) n")).then_inc(raw_full[slot(b)], 16)

        load(Blk(0, 0))
        load(Blk(1, 0))
        with sp.Fori(1, nb // 2) as i:
            for u in range(2):
                src = w[bass.ds(sp.snap(i * 2 + u), 1)].rearrange("a p n -> (a p) n")
                sp.wait_ge(lo_done, i * 2 + (u - 1))
                sp.dma_start(wraw[:, u * DM:(u + 1) * DM], src).then_inc(raw_full[u], 16)
        if nb % 2:
            load(Blk(nb - 1, 0))

    def split_hi(act, b):
        if isinstance(b.i, int) and num(b) >= nb:
            return
        s = slot(b)
        wait(act, raw_full[s], 16 * (b.c // 2 + 1 + b.i))
        wait(act, block_done, num(b) - 1)
        act.activation(wh[:, s * DM:(s + 1) * DM], wraw[:, s * DM:(s + 1) * DM], ACT.Copy).then_inc(hi_done, 1)

    def split_lo(pool, b):
        if isinstance(b.i, int) and num(b) >= nb:
            return
        s = slot(b)
        pool.wait_ge(hi_done, num(b) + 1)
        pool.tensor_tensor(wl[:, s * DM:(s + 1) * DM], wraw[:, s * DM:(s + 1) * DM],
                           wh[:, s * DM:(s + 1) * DM].bitcast(F32), ALU.subtract).then_inc(lo_done, 1)

    def products(pe, b, xh, xl, k, fresh=None, late=None):
        s = slot(b)
        pe.wait_ge(lo_done, num(b) + 1)
        wait(pe, acc_free, num(b) - 1)
        passes = [(ws, x, kk) for ws, x in ((wh, xh), (wl, xh), (wh, xl)) for kk in range(k)]
        order = [(h, n) for h in range(2) for n in range(3 * k)]
        if fresh is not None:
            order = [(h, n) for n in range(3 * k) for h in range(2)]
        if late is not None:
            order = [(h, n) for h in range(2) for n in range(3 * k) if passes[n][2] < k - 1] + \
                    [(h, n) for h in range(2) for n in range(3 * k) if passes[n][2] == k - 1]
        waited = False
        for i, (h, n) in enumerate(order):
            ws, x, kk = passes[n]
            if fresh is not None and h == 0 and n < k:
                pe.wait_ge(nhi, KT * fresh + kk + 1)
            if fresh is not None and h == 0 and n >= 2 * k:
                pe.wait_ge(nlo, KT * fresh + kk + 3)
            if late is not None and kk == k - 1 and not waited:
                pe.wait_ge(post_done, late)
                waited = True
            mm = pe.matmul(ps[:, 2 * s + h, 0:HT], ws[:, s * DM + kk * P:s * DM + (kk + 1) * P],
                           x[:, kk * T + h * HT:kk * T + (h + 1) * HT],
                           start=(h not in [o[0] for o in order[:i]]), stop=(h not in [o[0] for o in order[i + 1:]]))
        mm.then_inc(block_done, 1)

    def pe_segment(pe, name, xh, xl, fresh=None, norm=False):
        seg = SEGS[name]

        def body(j, u, b):
            first_block = isinstance(j, int) and j == 0
            products(pe, b, xh, xl, seg.k, fresh if first_block else None, late if first_block else None)
            if norm and (not isinstance(j, int) or j >= 2):
                norm_sum(pe, j - 2, u)

        late = None
        if name in ("ya", "yb", "wout") or name[:2] in ("dn", "do"):
            late = before[name] + 2
            pe.wait_ge(post_done, late - 1)
        blocks(pe, seg, body, first=2 if norm else 1 if seg.b0 == 0 or fresh is not None or late is not None else 0)
        if norm:
            norm_sum(pe, KT - 2, 0)
            norm_sum(pe, KT - 1, 1)
            norms["pe"] += 1
            pe.drain().then_inc(nsum, 1)

    def acc(b, rows=P):
        return pair_of(2 * slot(b), rows)

    def stage_at(u):
        return stage[:, u * T:(u + 1) * T]

    def pool_segment(pool, name):
        seg = SEGS[name]
        last = seg.b0 + seg.n == nb
        blocks(pool, seg, lambda j, u, b: split_lo(pool, nxt(b)), first=1 if seg.b0 == 0 else 0,
               last=1 if last else 0)

    def act_segment(act, name, out, func=ACT.Copy, posts=False, norm=False, **more):
        seg = SEGS[name]
        last = seg.b0 + seg.n == nb
        if posts:
            act.wait_ge(post_done, before[name] + 2)

        def body(j, u, b):
            split_hi(act, nxt(b))
            act.wait_ge(block_done, num(b) + 1)
            if posts:
                act.wait_ge(post_done, before[name] + j + 1)
            act.activation(two(out(j, u)), acc(b), func, **more).then_inc(acc_free, 1)
            if norm and (not isinstance(j, int) or j > 0):
                squared(j - 1, 1 - u)

        def squared(m, u):
            act.wait_ge(post_done, m + (before[name] + 3))
            norm_square(act, m, u)

        blocks(act, seg, body, first=1 if norm else 0, last=1 if last else 0)
        if norm:
            squared(KT - 1, 1)

    def dve_segment(dve, name, post):
        seg = SEGS[name]

        def body(j, u, b):
            dve.wait_ge(acc_free, num(b) + 1)
            post(j, u).then_inc(post_done, 1)

        blocks(dve, seg, body)

    def split_store(dve, hi, lo, m, x):
        dve.tensor_scalar(tile_at(hi, m), x, 1.0, None, ALU.mult)
        dve.drain()
        return dve.tensor_tensor(tile_at(lo, m), x, tile_at(hi, m).bitcast(F32), ALU.subtract)

    def add_residual(dve):
        def post(j, u):
            return dve.tensor_tensor(tile_at(res, j), tile_at(res, j), stage_at(u), ALU.add)
        return post


    def norm_sum(pe, m, u):
        static = isinstance(m, int)
        pe.wait_ge(nsq, m + (KT * norms["pe"] + 1))
        for h in range(2):
            mm = pe.matmul(ps[:, 4 + h, 0:HT], ones[:, :], nsqr[u][:, h * HT:(h + 1) * HT],
                           start=static and m == 0, stop=static and m == KT - 1)
        mm.then_inc(nused, 1)

    def pe_norm(pe):
        for m in range(KT):
            norm_sum(pe, m, m % 2)
        norms["pe"] += 1
        pe.drain().then_inc(nsum, 1)

    def norm_square(act, m, u):
        act.wait_ge(nused, m + (KT * norms["act"] + 1))
        act.activation(nsqr[u][:, :], tile_at(res, m), ACT.Square).then_inc(nsq, 1)

    def act_norm(act, squares=True):
        if squares:
            tiles(act, KT, lambda m, u: norm_square(act, m, u))
        norms["act"] += 1
        act.wait_ge(nsum, norms["act"])
        act.activation(two(rstd[:, :]), pair_of(4), ACT.Sqrt, bias=eps[:, 0:1],
                       scale=1.0 / DM).then_inc(nroot, 1)

    def dve_norm(dve):
        k = norms["dve"]
        norms["dve"] += 1
        dve.wait_ge(nroot, k + 1)
        dve.reciprocal(rstd[:, :], rstd[:, :])
        dve.drain()

    slots = [place(f"scaled{v}", [P, T], F32, b_at + (2 * KT - 2 + v) * F) for v in range(2)]

    def ring_of(a):
        return 2 if a in (0, 5) else 4

    def scaled(v):
        return stage_at(v) if v < 2 else slots[v - 2][:, :]

    def quads(e, a, body):
        n = ring_of(a)
        with e.Fori(0, KT // n) as i:
            for v in range(n):
                body(i * n + v, v)

    def dve_norm_apply(dve, gi):
        a = applied["dve"]
        applied["dve"] += 1

        def scale(m, u):
            dve.wait_ge(nlo, m + (KT * a + 3 - ring_of(a)))
            dve.scalar_tensor_tensor(scaled(u), tile_at(res, m), gains[:, bass.ds(m + gi * KT, 1)],
                                     rstd[:, :], ALU.mult, ALU.mult).then_inc(nscaled, 1)

        quads(dve, a, scale)

    def act_norm_apply(act, xh):
        a = applied["act"]
        applied["act"] += 1

        def hi(m, u):
            act.wait_ge(nscaled, KT * a + m + 1)
            act.activation(tile_at(xh, m), scaled(u), ACT.Copy).then_inc(nhi, 1)

        quads(act, a, hi)

    def pool_norm_apply(pool, xh, xl):
        a = applied["pool"]
        applied["pool"] += 1

        def lo(m, u):
            pool.wait_ge(nhi, KT * a + m + 1)
            pool.tensor_tensor(tile_at(xl, m), scaled(u), tile_at(xh, m).bitcast(F32),
                               ALU.subtract).then_inc(nlo, 1)

        quads(pool, a, lo)

    heads = {"pe": [0, 0], "act": [0, 0], "dve": [0, 0]}

    def count_heads(who, n):
        at_tile, call = heads[who]
        heads[who] = [at_tile + n, call + 1]
        return at_tile, call

    def pe_headnorm(pe, n, width):
        k, call = count_heads("pe", n)
        rows = 16
        if k:
            pe.wait_ge(happ, k + 2)
        for m in range(n):
            lhs = win128[:, 15 - m:31 - m] if width == P else win64[:, 14 - 2 * m:30 - 2 * m]
            pe.wait_ge(hsq, k + m + 1)
            for h in range(2):
                mm = pe.matmul(ps[0:rows, 4 + h, 0:HT], lhs, sq[m % 2][:, h * HT:(h + 1) * HT],
                               start=(m == 0), stop=(m == n - 1))
            mm.then_inc(hused, 1)
        pe.drain().then_inc(hsum, 1)
        pe.wait_ge(hiv, call + 1)
        for m in range(n):
            if width == P:
                lhs = ident[:, m:m + 1].broadcast_to([P, P])
            else:
                lhs = spread[:, m * P:(m + 1) * P]
            pe.wait_ge(happ, k + m + 1)
            for h in range(2):
                mm = pe.matmul(ps[:, 4 + 2 * (m % 2) + h, 0:HT], lhs, hinv[:, h * HT:(h + 1) * HT],
                               start=True, stop=True)
            mm.then_inc(hbc, 1)

    def act_headnorm(act, buf, t0, n, width, scale):
        k, call = count_heads("act", n)
        rows = 16

        def square(m, u):
            act.wait_ge(hused, k + m + 1)
            act.activation(sq[u][:, :], tile_at(buf, m + t0), ACT.Square).then_inc(hsq, 1)

        tiles(act, n, square)
        act.wait_ge(hsum, call + 1)
        act.activation(two(hroot[0:rows, :]), pair_of(4, rows), ACT.Sqrt, bias=eps[0:rows, 0:1],
                       scale=scale).then_inc(hrt, 1)

    def dve_headnorm(dve, buf, t0, n, width, gain, rowscale=None):
        k, call = count_heads("dve", n)
        rows = 16
        dve.memset(hinv[:, :], 0.0)
        dve.drain()
        dve.wait_ge(hrt, call + 1)
        if width != P:
            dve.tensor_copy(spread[:, :].rearrange("p (k n) -> p k n", n=64),
                            ident[:, 0:16].unsqueeze(2).broadcast_to([P, 16, 64]))
        last = dve.reciprocal(hinv[0:rows, :], hroot[0:rows, :])
        if rowscale is not None:
            dve.drain()
            last = dve.tensor_scalar(hinv[0:rows, :], hinv[0:rows, :], rowscale, None, ALU.mult)
        last.then_inc(hiv, 1)

        def apply(m, u):
            dve.wait_ge(hbc, k + m + 1)
            dve.scalar_tensor_tensor(two(tile_at(buf, m + t0)), two(tile_at(buf, m + t0)), gain,
                                     pair_of(4 + 2 * u), ALU.mult, ALU.mult).then_inc(happ, 1)

        tiles(dve, n, apply)

    softs = {"act": 0, "dve": 0}

    def act_softplus(act, y):
        softs["act"] += 1
        act.wait_ge(sp_abs, softs["act"])
        act.activation(sp[0][:, :], y, ACT.Abs)
        act.drain()
        act.activation(sp[1][:, :], sp[0][:, :], ACT.Exp, scale=-1.0).then_inc(sp_exp, 1)

    def dve_softplus(dve, out_, y):
        softs["dve"] += 1
        _, e, r, p, q = (t[:, :] for t in sp)
        dve.drain().then_inc(sp_abs, 1)
        dve.wait_ge(sp_exp, softs["dve"])
        dve.tensor_scalar(r, e, 2.0, None, ALU.add)
        dve.drain()
        dve.reciprocal(p, r)
        dve.drain()
        dve.tensor_tensor(e, e, p, ALU.mult)
        dve.drain()
        dve.tensor_tensor(q, e, e, ALU.mult)
        dve.drain()
        dve.tensor_scalar(p, q, 1.0 / 17, None, ALU.mult)
        for k in range(7, 0, -1):
            dve.drain()
            dve.scalar_tensor_tensor(p, p, 1.0 / (2 * k + 1), q, ALU.add, ALU.mult)
        dve.drain()
        dve.scalar_tensor_tensor(p, p, 1.0, e, ALU.add, ALU.mult)
        dve.tensor_scalar(r, y, 0.0, None, ALU.max)
        dve.drain()
        dve.scalar_tensor_tensor(out_, p, 2.0, r, ALU.mult, ALU.add)
        dve.drain()

    def act_qkv(act):
        def body(j, u, b):
            split_hi(act, nxt(b))
            act.wait_ge(block_done, num(b) + 1)
            act.wait_ge(conv_done, j + 1)
            act.activation(two(cpad[u][:, 2:2 + T]), acc(b), ACT.Copy).then_inc(acc_free, 1)
            if not isinstance(j, int) or j > 0:
                silu(j - 1, 1 - u)

        def silu(j, u):
            act.wait_ge(conv_done, j + 3)
            act.activation(tile_at(qkv, j), cout[u][:, :], ACT.Silu).then_inc(silu_done, 1)

        blocks(act, SEGS["qkv"], body, first=1)
        silu(23, 1)

    def dve_qkv(dve):
        for u in range(2):
            dve.memset(cpad[u][:, 0:2], 0.0)
            dve.memset(cpad[u][:, T + 2:T + 4], 0.0)
        dve.memset(qkv[:, :].rearrange("p (k t) -> p k t", t=TS)[:, :, T:TS], 0.0)
        dve.drain()

        def body(j, u, b):
            dve.wait_ge(acc_free, num(b) + 1)
            dve.wait_ge(silu_done, j + 1)
            o = cout[u][:, :]
            for k in range(5):
                tap = convw[:, bass.ds(j * 5 + k, 1)]
                if k == 0:
                    last = dve.tensor_scalar(o, cpad[u][:, 0:T], tap, None, ALU.mult)
                else:
                    dve.drain()
                    last = dve.scalar_tensor_tensor(o, cpad[u][:, k:k + T], tap, o, ALU.mult, ALU.add)
            last.then_inc(conv_done, 1)

        blocks(dve, SEGS["qkv"], body)

    def act_ba(act):
        b0, b1 = Blk(0, 0), Blk(1, 0)
        split_hi(act, b1)
        act.wait_ge(block_done, 1)
        act.activation(two(beta[:, 0:T]), acc(b0, 16), ACT.Sigmoid).then_inc(acc_free, 1)
        split_hi(act, Blk(2, 0))
        act.wait_ge(block_done, 2)
        act.activation(two(gdec[:, 0:T]), acc(b1, 16), ACT.Identity, bias=rowvec[:, 0:1]).then_inc(acc_free, 1)

    def dve_decay(dve):
        dve.memset(gdec[:, T:TS], 0.0)
        dve.memset(beta[:, T:TS], 0.0)
        dve.wait_ge(acc_free, 2)
        dve_softplus(dve, gdec[:, 0:T], gdec[:, 0:T])
        dve.wait_ge(prep_act, 1)
        dve.tensor_scalar(gdec[:, 0:T], gdec[:, 0:T], rowvec[:, 4:5], -1.0, ALU.mult, ALU.mult).then_inc(prep_dve, 1)

    CW = NCH * 8

    def pe_prep(pe):
        pe.wait_ge(prep_dve, 1)
        for c in range(NCH):
            pe.transpose(ps[0:C, 4, c * 16:(c + 1) * 16], gdec[:, c * C:(c + 1) * C], ident[0:16, 0:16])
            mm = pe.transpose(ps[0:C, 5, c * 16:(c + 1) * 16], beta[:, c * C:(c + 1) * C], ident[0:16, 0:16])
        mm.then_inc(prep_pe, 1)
        pe.wait_ge(prep_act, 3)
        for u in range(2):
            g = tok_g[:, :, 8 * u:8 * u + 8]
            pe.matmul(ps[0:C, 6, CW * u:CW * (u + 1)].rearrange("p (c h) -> p c h", h=8), tri[:, u, :], g,
                      start=True, stop=True)
            mm = pe.matmul(ps[:, 7, CW * u:CW * (u + 1)].rearrange("p (c h) -> p c h", h=8), ones[0:C, :], g,
                           start=True, stop=True)
            for c in range(NCH):
                mm = pe.matmul(ps[0:16, 2 * u + c // 4, (c % 4) * C:(c % 4 + 1) * C], tok_g[:, c, :],
                               tri[:, u, :], start=True, stop=True)
        mm.then_inc(prep_pe, 1)

    def act_prep(act):
        act.wait_ge(prep_pe, 1)
        act.activation(tok_g[:, :, :], ps[0:C, 4, 0:NCH * 16].rearrange("p (c h) -> p c h", h=16),
                       ACT.Copy).then_inc(prep_act, 1)
        act.activation(tok_b[:, :, :], ps[0:C, 5, 0:NCH * 16].rearrange("p (c h) -> p c h", h=16),
                       ACT.Copy).then_inc(prep_act, 1)
        act.wait_ge(prep_pe, 2)
        flat = ps[0:C, 6, 0:2 * CW].rearrange("p (u c h) -> p u (c h)", u=2, h=8)
        act.activation(tok_cum[:, :, :, :].rearrange("p u c h -> p u (c h)"), flat, ACT.Copy).then_inc(prep_act, 1)
        act.activation(tok_neg[:, :, :, :].rearrange("p u c h -> p u (c h)"), flat, ACT.Exp).then_inc(prep_act, 1)
        act.activation(chunk_decay[:, :, :, :].rearrange("p u c h -> p u (c h)"),
                       ps[:, 7, 0:2 * CW].rearrange("p (u c h) -> p u (c h)", u=2, h=8), ACT.Exp)
        for u in range(2):
            act.activation(scum[:, u, 0:4 * C], ps[0:16, 2 * u, 0:4 * C], ACT.Copy)
            last = act.activation(scum[:, u, 4 * C:TS], ps[0:16, 2 * u + 1, 0:TS - 4 * C], ACT.Copy)
        last.then_inc(prep_act, 1)
        act.wait_ge(prep_dve, 2)
        act.activation(tok_bk[:, :, :, :], tok_bk[:, :, :, :], ACT.Exp).then_inc(prep_act, 1)

    def dve_prep(dve):
        dve.wait_ge(prep_act, 6)
        flat = "p u c h -> p u (c h)"
        dve.tensor_scalar(tok_neg[:, :, :, :], tok_neg[:, :, :, :], -1.0, None, ALU.mult)
        dve.scalar_tensor_tensor(tok_bk[:, :, :, :].rearrange(flat), tok_cum[:, :, :, :].rearrange(flat), -1.0,
                                 ps[0:C, 7, 0:2 * CW].rearrange("p (u c h) -> p u (c h)", u=2, h=8),
                                 ALU.mult, ALU.add).then_inc(prep_dve, 1)
        dve.wait_ge(prep_act, 7)
        for u in range(2):
            dve.tensor_tensor(tok_bk[:, u, :, :], tok_bk[:, u, :, :], tok_b[:, :, 8 * u:8 * u + 8], ALU.mult)
        dve.memset(oacc[:, :], 0.0)

    L = LEVELS
    NPE, NACT, NDVE, NPOOL = 6 + 3 * L, 9 + L, 7 + 2 * L, 4 + L

    def delta_loop(e, body):
        with e.Fori(0, NG) as g:
            with e.Fori(0, NCH) as c:
                body(g, c, g * NCH + c)

    def chunk_of(u, c):
        return c if u == 0 else c * -1 + (NCH - 1)

    def heads4(t, n):
        return t[:, :].rearrange("p (r n) -> p r n", n=n)

    def head_slices(n):
        return [slice(r * n, (r + 1) * n) for r in range(GH)]

    def pe_delta(pe):
        for u in range(2):
            pe.sem_inc(dpe[u], 1)

        def body(g, c, n):
            def on(u, who, k):
                s, per = {"act": (dact, NACT), "dve": (ddve, NDVE), "pool": (dpool, NPOOL)}[who]
                pe.wait_ge(s[u], n * per + (k + 1))

            def products4(out_, u, lhs, rhs, width=C, rows=C):
                for sl in head_slices(width):
                    mm = pe.matmul(ps[0:rows, 4 * u + out_, sl], lhs(sl), rhs(sl), start=True, stop=True)
                return mm

            for u in range(2):
                on(u, "pool", 1)
                on(u, "dve", 0)
                pe.matmul(ps[:, 4 * u + 3, 0:W4], ones[0:16, :], delta[u]["grow"][:, :], start=True,
                          stop=True).then_inc(dpe[u], 1)
            for u in range(2):
                d = delta[u]
                on(u, "act", 2)
                for r in range(GH):
                    pe.transpose(ps[0:C, 4 * u, r * P:(r + 1) * P], d["ks"][:, r * C:(r + 1) * C], ident[:, :])
                for r in range(GH):
                    mm = pe.transpose(ps[0:C, 4 * u + 1, r * P:(r + 1) * P], d["vs"][:, r * C:(r + 1) * C],
                                      ident[:, :])
                mm.then_inc(dpe[u], 1)
            for u in range(2):
                k = delta[u]["ks"]
                products4(2, u, lambda sl: k[:, sl], lambda sl: k[:, sl]).then_inc(dpe[u], 1)
            for u in range(2):
                d = delta[u]
                on(u, "pool", 2)
                on(u, "act", 4)
                products4(0, u, lambda sl: d["ks"][:, sl], lambda sl: d["qs"][:, sl]).then_inc(dpe[u], 1)
            for u in range(2):
                d = delta[u]
                on(u, "pool", 4)
                on(u, "act", 5)
                products4(1, u, lambda sl: d["ob"][:, sl], lambda sl: ident[0:C, 0:C]).then_inc(dpe[u], 1)
            for lv in range(1, L):
                for u in range(2):
                    d = delta[u]
                    on(u, "pool", 5 + lv)
                    on(u, "dve", 2 + 2 * lv)
                    products4(0, u, lambda sl: d["ob"][:, sl], lambda sl: d["xx"][:, sl]).then_inc(dpe[u], 1)
                for u in range(2):
                    d = delta[u]
                    on(u, "act", 6 + lv)
                    on(u, "dve", 3 + 2 * lv)
                    last = lv == L - 1
                    if not last:
                        products4(1, u, lambda sl: d["xt"][:, sl], lambda sl: d["pp"][:, sl]).then_inc(dpe[u], 1)
                    products4(2, u, lambda sl: d["pp"][:, sl], lambda sl: d["xt"][:, sl]
                              ).then_inc(dpe[u], 2 if last else 1)
            for u in range(2):
                d = delta[u]
                for r in range(GH):
                    mm = pe.matmul(ps[0:C, 4 * u, r * P:(r + 1) * P], d["ks"][:, r * C:(r + 1) * C],
                                   d["state"][:, r * P:(r + 1) * P], start=True, stop=True)
                mm.then_inc(dpe[u], 1)
            for u in range(2):
                d = delta[u]
                on(u, "dve", 4 + 2 * L)
                for r in range(GH):
                    mm = pe.matmul(ps[0:C, 4 * u + 1, r * P:(r + 1) * P], d["xt"][:, r * C:(r + 1) * C],
                                   d["rr"][:, r * P:(r + 1) * P], start=True, stop=True)
                mm.then_inc(dpe[u], 1)
            for u in range(2):
                d = delta[u]
                on(u, "pool", 5)
                on(u, "act", 9 + L)
                for r in range(GH):
                    o = ps[:, 4 * u + 2, r * C:(r + 1) * C]
                    pe.matmul(o, d["state"][:, r * P:(r + 1) * P], d["qd"][:, r * C:(r + 1) * C],
                              start=True, stop=False)
                    mm = pe.matmul(o, d["vn"][:, r * P:(r + 1) * P], d["qkm"][:, r * C:(r + 1) * C],
                                   start=False, stop=True)
                mm.then_inc(dpe[u], 1)
            for u in range(2):
                d = delta[u]
                on(u, "dve", 5 + 2 * L)
                for r in range(GH):
                    mm = pe.matmul(ps[:, 4 * u + 3, r * P:(r + 1) * P], d["kt"][:, r * P:(r + 1) * P],
                                   d["vk"][:, r * P:(r + 1) * P], start=True, stop=True)
                mm.then_inc(dpe[u], 1)

        delta_loop(pe, body)

    def pool_delta(pool):
        for u in range(2):
            pool.sem_inc(dpool[u], 1)
        q3 = qkv[:, :].rearrange("p (h t) -> p h t", t=TS)

        def body(g, c, n):
            t0 = [pool.snap(chunk_of(u, c) * C) for u in range(2)]
            h0 = pool.snap(g * GH)
            for u in range(2):
                d = delta[u]
                pool.wait_ge(dact[u], n * NACT + 1)
                pool.tensor_tensor(heads4(d["grow"], C),
                                   scum[:, u, bass.ds(t0[u], C)].unsqueeze(1).broadcast_to([16, GH, C]),
                                   sel[:, u, bass.ds(g, 1), :].rearrange("p a r -> p (a r)").unsqueeze(2)
                                   .broadcast_to([16, GH, C]), ALU.mult).then_inc(dpool[u], 1)
            for u in range(2):
                pool.tensor_copy(heads4(delta[u]["qs"], C), q3[:, bass.ds(h0, GH), bass.ds(t0[u], C)]
                                 ).then_inc(dpool[u], 1)
            for u in range(2):
                d = delta[u]
                pool.drain()
                pool.wait_ge(dact[u], n * NACT + 4)
                pool.tensor_tensor(d["qd"][:, :], d["qd"][:, :], d["qs"][:, :], ALU.mult).then_inc(dpool[u], 1)

            def masked(u, lv):
                d = delta[u]
                pool.tensor_tensor(heads4(d["ob"], C), heads4(d["mt"], C),
                                   masks[:, u, lv, :].unsqueeze(1).broadcast_to([C, GH, C]), ALU.mult
                                   ).then_inc(dpool[u], 1)

            for u in range(2):
                pool.wait_ge(ddve[u], n * NDVE + 3)
                masked(u, 0)
            for u in range(2):
                d = delta[u]
                pool.wait_ge(ddve[u], n * NDVE + 4)
                pool.tensor_tensor(heads4(d["qkm"], C), heads4(d["qkm"], C),
                                   tri[:, u, :].unsqueeze(1).broadcast_to([C, GH, C]), ALU.mult
                                   ).then_inc(dpool[u], 1)
            for lv in range(1, L):
                for u in range(2):
                    if lv == 1:
                        pool.wait_ge(ddve[u], n * NDVE + 6)
                    else:
                        pool.wait_ge(dpe[u], n * NPE + (3 * lv + 1))
                    masked(u, lv)

        delta_loop(pool, body)

    def act_delta(act):
        for u in range(2):
            act.sem_inc(dact[u], 1)
        q3 = qkv[:, :].rearrange("p (h t) -> p h t", t=TS)

        def body(g, c, n):
            h0 = act.snap(g * GH)
            ccs = [act.snap(chunk_of(u, c)) for u in range(2)]
            t0 = [act.snap(ccs[u] * C) for u in range(2)]
            for u in range(2):
                for name, t in (("ks", 8), ("vs", 16)):
                    act.activation(heads4(delta[u][name], C), q3[:, bass.ds(h0 + t, GH), bass.ds(t0[u], C)],
                                   ACT.Copy).then_inc(dact[u], 1)
            for u in range(2):
                d = delta[u]
                act.wait_ge(dpe[u], n * NPE + 2)
                act.activation(d["qd"][:, :], ps[:, 4 * u + 3, 0:W4], ACT.Exp).then_inc(dact[u], 1)
            for u in range(2):
                d = delta[u]
                act.wait_ge(dpe[u], n * NPE + 3)
                act.activation(d["kt"][:, :], ps[0:C, 4 * u, :], ACT.Copy).then_inc(dact[u], 1)
                act.activation(d["vt"][:, :], ps[0:C, 4 * u + 1, :], ACT.Copy).then_inc(dact[u], 1)
            for u in range(2):
                d = delta[u]
                act.wait_ge(ddve[u], n * NDVE + 2)
                act.activation(d["dec"][:, :], d["dec"][:, :], ACT.Exp).then_inc(dact[u], 1)
            for lv in range(1, L):
                for u in range(2):
                    act.wait_ge(dpe[u], n * NPE + (4 + 3 * lv))
                    act.activation(delta[u]["pp"][:, :], ps[0:C, 4 * u, 0:W4], ACT.Copy).then_inc(dact[u], 1)
            for u in range(2):
                d = delta[u]
                act.wait_ge(dpe[u], n * NPE + (5 + 3 * L))
                for r in range(GH):
                    act.activation(d["vn"][:, r * P:(r + 1) * P], ps[0:C, 4 * u + 1, r * P:(r + 1) * P], ACT.Copy,
                                   scale=tok_b[:, bass.ds(ccs[u], 1), bass.ds(h0 + (8 * u + r), 1)]
                                   .rearrange("p a b -> p (a b)")).then_inc(dact[u], 1)

        delta_loop(act, body)

    def dve_delta(dve):
        for u in range(2):
            dve.sem_inc(ddve[u], 1)
        o3 = oacc[:, :].rearrange("p (h t) -> p h t", t=TS)
        one = ident[0:C, 0:C].unsqueeze(1).broadcast_to([C, GH, C])

        def col(t, u, cc, h):
            return t[:, u, bass.ds(cc, 1), bass.ds(h, 1)].rearrange("p a b -> p (a b)")

        def body(g, c, n):
            ccs = [dve.snap(chunk_of(u, c)) for u in range(2)]
            tok0 = [dve.snap(ccs[u] * C) for u in range(2)]
            h0 = dve.snap(g * GH)
            for u in range(2):
                d = delta[u]
                dve.wait_ge(dact[u], n * NACT + 4)
                for r, sl in enumerate(head_slices(C)):
                    last = dve.tensor_scalar(d["dec"][:, sl], ps[0:C, 4 * u + 3, sl],
                                             col(tok_cum, u, ccs[u], h0 + r), 0.0, ALU.subtract, ALU.min)
                last.then_inc(ddve[u], 1)
            for u in range(2):
                d = delta[u]
                dve.wait_ge(dpe[u], n * NPE + 4)
                dve.wait_ge(dact[u], n * NACT + 7)
                for r, sl in enumerate(head_slices(C)):
                    b = tok_b[:, bass.ds(ccs[u], 1), bass.ds(h0 + (8 * u + r), 1)].rearrange("p a b -> p (a b)")
                    last = dve.scalar_tensor_tensor(d["mt"][:, sl], ps[0:C, 4 * u + 2, sl], b, d["dec"][:, sl],
                                                    ALU.mult, ALU.mult)
                last.then_inc(ddve[u], 1)
            for u in range(2):
                d = delta[u]
                dve.wait_ge(dpe[u], n * NPE + 5)
                dve.tensor_tensor(d["qkm"][:, :], ps[0:C, 4 * u, 0:W4], d["dec"][:, :], ALU.mult
                                  ).then_inc(ddve[u], 1)
            for u in range(2):
                d = delta[u]
                dve.wait_ge(dpe[u], n * NPE + 6)
                dve.tensor_tensor(heads4(d["xx"], C), one, heads4(ps[0:C, 4 * u + 1, 0:W4], C), ALU.subtract
                                  ).then_inc(ddve[u], 1)
                dve.tensor_tensor(heads4(d["xt"], C), one, heads4(d["ob"], C), ALU.subtract
                                  ).then_inc(ddve[u], 1)
            for lv in range(1, L):
                for u in range(2):
                    d = delta[u]
                    if lv < L - 1:
                        dve.wait_ge(dpe[u], n * NPE + (5 + 3 * lv))
                        dve.tensor_tensor(d["xx"][:, :], d["xx"][:, :], ps[0:C, 4 * u + 1, 0:W4], ALU.subtract
                                          ).then_inc(ddve[u], 1)
                    dve.wait_ge(dpe[u], n * NPE + (6 + 3 * lv))
                    dve.tensor_tensor(d["xt"][:, :], d["xt"][:, :], ps[0:C, 4 * u + 2, 0:W4], ALU.subtract
                                      ).then_inc(ddve[u], 1 if lv < L - 1 else 2)
            for u in range(2):
                d = delta[u]
                dve.wait_ge(dpe[u], n * NPE + (4 + 3 * L))
                for r, sl in enumerate(head_slices(P)):
                    last = dve.scalar_tensor_tensor(d["rr"][:, sl], ps[0:C, 4 * u, sl],
                                                    col(tok_neg, u, ccs[u], h0 + r), d["vt"][:, sl],
                                                    ALU.mult, ALU.add)
                last.then_inc(ddve[u], 1)
            for u in range(2):
                d = delta[u]
                dve.wait_ge(dact[u], n * NACT + (10 + L))
                for r, sl in enumerate(head_slices(P)):
                    last = dve.tensor_scalar(d["vk"][:, sl], ps[0:C, 4 * u + 1, sl],
                                             col(tok_bk, u, ccs[u], h0 + r), None, ALU.mult)
                last.then_inc(ddve[u], 1)
            for u in range(2):
                dve.drain()
                dve.wait_ge(dpe[u], n * NPE + (6 + 3 * L))
                o = o3[:, bass.ds(h0, GH), bass.ds(tok0[u], C)]
                dve.tensor_tensor(o, o, heads4(ps[:, 4 * u + 2, 0:W4], C), ALU.add).then_inc(ddve[u], 1)
            for u in range(2):
                d = delta[u]
                dve.wait_ge(dpe[u], n * NPE + (7 + 3 * L))
                for r, sl in enumerate(head_slices(P)):
                    last = dve.scalar_tensor_tensor(d["state"][:, sl], d["state"][:, sl],
                                                    col(chunk_decay, u, ccs[u], h0 + r),
                                                    ps[:, 4 * u + 3, sl], ALU.mult, ALU.add)
                last.then_inc(ddve[u], 1)

        with dve.Fori(0, NG) as g:
            dve.drain()
            for u in range(2):
                dve.memset(delta[u]["state"][:, :], 0.0)
            dve.drain()
            with dve.Fori(0, NCH) as c:
                body(g, c, g * NCH + c)

    def act_sc(act):
        b0 = SEGS["sc"].b0
        act.wait_ge(post_done, before["sc"] + 2)
        with act.Fori(0, 4) as i:
            for v in range(6):
                b = Blk(b0 + v, i * 3)
                split_hi(act, nxt(b))
                act.wait_ge(block_done, num(b) + 1)
                if v % 3 == 0:
                    act.wait_ge(post_done, i * 2 + (before["sc"] + v // 3 + 2))
                o = (bst[:, :], stage_at(0), stage_at(1))[v % 3]
                act.activation(two(o), acc(b), ACT.Copy).then_inc(acc_free, 1)

    def dve_sc(dve):
        b0 = SEGS["sc"].b0
        dve.memset(pc[:, 0:1], 0.0)
        dve.memset(pc[:, T + 1:T + 2], 0.0)
        with dve.Fori(0, 4) as i:
            for v in range(2):
                m = i * 2 + v
                dve.drain()
                dve.wait_ge(acc_free, i * 6 + (b0 + 3 * v + 3))
                dve.tensor_tensor(pc[:, 1:T + 1], stage_at(0), stage_at(1), ALU.mult)
                dve.drain()
                o = stage_at(0)
                for k in range(3):
                    tap = scw[:, bass.ds(m * 3 + k, 1)]
                    if k == 0:
                        dve.tensor_scalar(o, pc[:, 0:T], tap, None, ALU.mult)
                    else:
                        dve.scalar_tensor_tensor(o, pc[:, k:k + T], tap, o, ALU.mult, ALU.add)
                    dve.drain()
                dve.tensor_tensor(tile_at(scy, m), o, bst[:, :], ALU.mult).then_inc(post_done, 1)

    def dve_z(dve):
        def post(j, u):
            x = stage_at(u)
            dve.tensor_tensor(x, x, tile_at(oacc, j), ALU.mult)
            dve.drain()
            return split_store(dve, xbh, xbl, j, x)
        dve_segment(dve, "z", post)

    def dve_ya(dve):
        def post(j, u):
            split_store(dve, xah, xal, j, tile_at(scy, j))
            return dve.tensor_tensor(tile_at(gab, j), tile_at(gab, j), stage_at(u), ALU.mult)
        dve_segment(dve, "ya", post)

    def dve_yb(dve):
        def post(j, u):
            x = stage_at(u)
            dve.tensor_tensor(x, x, tile_at(gab, j + 8), ALU.mult)
            dve.drain()
            dve.tensor_tensor(x, x, tile_at(gab, j), ALU.add)
            dve.drain()
            return split_store(dve, xbh, xbl, j, x)
        dve_segment(dve, "yb", post)

    def act_gated(act, name):
        seg = SEGS[name]
        act.wait_ge(post_done, before[name] + 2)
        with act.Fori(0, seg.n // 2) as i:
            for u in range(2):
                b = Blk(seg.b0 + u, i)
                split_hi(act, nxt(b))
                act.wait_ge(block_done, num(b) + 1)
                if u == 0:
                    act.wait_ge(post_done, i + (before[name] + 2))
                act.activation(two(stage_at(u)), acc(b), ACT.Silu if u == 0 else ACT.Copy).then_inc(acc_free, 1)

    def dve_gated(dve, name):
        seg = SEGS[name]
        with dve.Fori(0, seg.n // 2) as m:
            dve.wait_ge(acc_free, m * 2 + (seg.b0 + 2))
            dve.tensor_tensor(stage_at(0), stage_at(0), stage_at(1), ALU.mult)
            dve.drain()
            split_store(dve, xbh, xbl, m, stage_at(0)).then_inc(post_done, 1)

    def dve_relu2(dve, name):
        def post(j, u):
            x = stage_at(u)
            dve.tensor_tensor(x, x, x, ALU.mult)
            dve.drain()
            return split_store(dve, xbh, xbl, j, x)
        dve_segment(dve, name, post)

    ropes = {"pe": 0, "dve": 0, "pool": 0}
    vts = {"pe": 0, "act": 0}
    vt2 = place("vtok_dsa", [C, NCH, 256], F32, phase_at + 24 * F)

    def tiles_odd(e, n, body):
        tiles(e, n, body)
        if n % 2:
            body(n - 1, 0)

    def pe_rope(pe, t0, n):
        k = ropes["pe"]
        ropes["pe"] += n

        def turn(m, u):
            pe.wait_ge(rope_dve, k + m + 1)
            for h in range(2):
                mm = pe.matmul(bank(4 + 2 * u + h), rot[:, :], tile_at(pf, m + t0, HT, h * HT),
                               start=True, stop=True)
            mm.then_inc(rope_pe, 1)

        tiles_odd(pe, n, turn)

    def pool_rope(pool, t0, n):
        k = ropes["pool"]
        ropes["pool"] += n

        def cosine(m, u):
            x = tile_at(pf, m + t0)
            pool.wait_ge(rope_pe, k + m + 1)
            pool.tensor_tensor(x, x, cossin[:, 0, :], ALU.mult).then_inc(rope_cos, 1)

        tiles_odd(pool, n, cosine)

    def dve_rope(dve, t0, n):
        k = ropes["dve"]
        ropes["dve"] += n

        def apply(m, u):
            x = tile_at(pf, m + t0)
            dve.drain()
            dve.wait_ge(rope_pe, k + m + 1)
            dve.tensor_tensor(two(sq[u][:, :]), pair_of(4 + 2 * u), two(cossin[:, 1, :]), ALU.mult)
            dve.drain()
            dve.wait_ge(rope_cos, k + m + 1)
            dve.tensor_tensor(x, x, sq[u][:, :], ALU.add).then_inc(rope_dve, 1)

        tiles_odd(dve, n, apply)

    def act_vtok(act, t0, n, dst):
        k = vts["act"]
        vts["act"] += n

        def move(m, u):
            act.wait_ge(vt_pe, k + m + 1)
            act.activation(stage_at(u), tile_at(pf, m + t0), ACT.Copy).then_inc(vt_in, 1)
            act.wait_ge(vt_pe, k + m + 3)
            act.activation(dst[:, 0:4, bass.ds(m * P, P)],
                           ps[0:C, 4 + 2 * u, :].rearrange("p (c n) -> p c n", n=P), ACT.Copy)
            last = act.activation(dst[0:ROWS[4], 4, bass.ds(m * P, P)], ps[0:ROWS[4], 5 + 2 * u, 0:P], ACT.Copy)
            last.then_inc(vt_out, 1)

        tiles(act, n, move)

    def pe_vtok(pe, n):
        k = vts["pe"]
        vts["pe"] += n

        def turn(m, u):
            pe.wait_ge(vt_in, k + m + 1)
            pe.wait_ge(vt_out, k + m + 1)
            for c in range(NCH):
                mm = pe.transpose(ps[0:ROWS[c], 4 + 2 * u + c // 4, (c % 4) * P:(c % 4 + 1) * P],
                                  stage[:, u * T + c * C:u * T + ENDS[c]], ident[:, :])
            mm.then_inc(vt_pe, 1)

        tiles(pe, n, turn)

    IX = 2 * (NCH - 1)

    def index_loop(e, body):
        with e.Fori(0, 2) as i:
            for v in range(2):
                body(i * 2 + v, v)

    def zero_halves(pool):
        for i in range(0, 4, 2):
            pool.memset(qz[64:P, i, :], 0.0)
            pool.memset(qz[0:64, i + 1, :], 0.0)

    def heads_apart(pool, x, v):
        pool.tensor_copy(qz[0:64, 2 * v, :], x[0:64])
        return pool.tensor_copy(qz[64:P, 2 * v + 1, :], x[64:P])

    def pool_index(pool):
        def body(m, v):
            x = tile_at(pf, pool.snap(m + 12))
            pool.wait_ge(ix_pe, m * IX + 2)
            heads_apart(pool, x, v).then_inc(ix_q, 1)
        zero_halves(pool)
        index_loop(pool, body)

    def pe_index(pe):
        pe.sem_inc(ix_pe, 2 + IX)

        def body(m, v):
            pe.wait_ge(ix_q, m + 1)
            for k in range(IX):
                hh, t = divmod(k, NCH - 1)
                t += 1
                pe.wait_ge(ix_act, m * IX + (k + 1))
                for x, (o, c) in enumerate(pieces(ENDS[t])):
                    mm = pe.matmul(ps[0:ROWS[t], 2 * (k % 2) + x, 0:c], qz[:, 2 * v + hh, C * t:ENDS[t]],
                                   pf[:, 16 * T + o:16 * T + o + c], start=True, stop=True)
                mm.then_inc(ix_pe, 1)
        index_loop(pe, body)

    def psum_cols(b, rows, n):
        return ps[0:rows, b, 0:n] if n <= 512 else pair_of(b, rows)

    def as_psum(ap, n):
        return ap if n <= 512 else two(ap)

    def act_index(act):
        act.sem_inc(ix_act, 2)

        def body(m, v):
            for k in range(IX):
                n, rows = ENDS[k % (NCH - 1) + 1], ROWS[k % (NCH - 1) + 1]
                act.wait_ge(ix_pe, m * IX + (IX + k + 3))
                act.wait_ge(ix_dve, m * IX + (k + 1))
                act.activation(as_psum(score[k % 2][0:rows, 0:n], n), psum_cols(2 * (k % 2), rows, n),
                               ACT.Relu).then_inc(ix_act, 1)
        index_loop(act, body)

    def rows_of(buf, t):
        return buf[0:ROWS[t], t, 0:ENDS[t]]

    def dve_index(dve):
        for t in range(1, NCH):
            dve.memset(rows_of(bias, t), 0.0)
        dve.sem_inc(ix_dve, 2)

        def body(m, v):
            for k in range(IX):
                hh, t = divmod(k, NCH - 1)
                t += 1
                if k % (NCH - 1) == 0:
                    dve.drain()
                    head = dve.snap(m * 2 + hh)
                dve.wait_ge(ix_act, m * IX + (k + 3))
                dve.scalar_tensor_tensor(rows_of(bias, t), score[k % 2][0:ROWS[t], 0:ENDS[t]],
                                         wit[0:ROWS[t], t, bass.ds(head, 1)], rows_of(bias, t),
                                         ALU.mult, ALU.add).then_inc(ix_dve, 1)
        index_loop(dve, body)

    def dve_topk(dve):
        dve.drain()
        for t in range(1, NCH):
            x = bias[0:ROWS[t], t, C * t:ENDS[t]]
            dve.scalar_tensor_tensor(x, causal[0:ROWS[t], 0:ROWS[t]], LOWEST / NEG, x, ALU.mult, ALU.add)
        dve.drain()
        for t in range(1, NCH):
            dve.tensor_copy(rows_of(work, t), rows_of(bias, t))
        dve.drain()
        with dve.Fori(0, TOPK // 8):
            for t in range(1, NCH):
                dve.max(top8[0:ROWS[t], 8 * t:8 * t + 8], rows_of(work, t))
            dve.drain()
            for t in range(1, NCH):
                dve.match_replace(rows_of(work, t), top8[0:ROWS[t], 8 * t:8 * t + 8], rows_of(work, t), LOWEST)
            dve.drain()
        for t in range(1, NCH):
            dve.tensor_tensor(rows_of(bias, t), rows_of(work, t), rows_of(bias, t), ALU.is_equal)
        dve.drain()
        for t in range(1, NCH):
            dve.tensor_scalar(rows_of(mask16, t), rows_of(bias, t), NEG, None, ALU.mult)
        dve.tensor_copy(mask16[:, 0, 0:C], causal[:, :])
        dve.tensor_copy(ident16[:, :], ident[:, 0:C])

    UN = 4 * NCH
    calls = {"pe": 0, "act": 0, "dve": 0, "pool": 0}

    def att_loop(e, who, body):
        call = calls[who]
        calls[who] += 1
        with e.Fori(0, 2) as a:
            with e.Fori(0, 2) as r:
                body(a, a * 4 + r * 2, a * 2 + r + 4 * call)

    def unit(k):
        return k // (2 * NCH), k // NCH % 2, k % NCH

    def pool_attention(pool):
        zero_halves(pool)
        pool.drain().then_inc(at_zero, 1)

    def pe_attention(pe, fox):
        v = vtok if fox else vt2
        if not fox:
            for ring in (at_s, at_pt, at_o):
                pe.sem_inc(ring, 2)

        def body(a, m, g):
            def scores(k):
                i, hh, t = unit(k)
                rows = ROWS[t]
                if k >= 2:
                    pe.wait_ge(at_p, g * UN + (k - 1))
                if k % (2 * NCH) == 0:
                    pe.wait_ge(at_q, g * 2 + (i + 1))
                kt_ = m + i if fox else a + 8
                for x, (o, c) in enumerate(pieces(ENDS[t])):
                    s = ps[0:rows, 2 * (k % 2) + x, 0:c]
                    pe.matmul(s, qz[:, 2 * i + hh, t * C:ENDS[t]], pf[:, bass.ds(kt_ * T + o, c)], start=True, stop=False)
                    if fox:
                        diagonal = o + c == ENDS[t]
                        mm = pe.matmul(s, headrow[:, 2 * i + hh, 0:rows], decay_row[:, o:o + c], start=False,
                                       stop=not diagonal)
                        if diagonal:
                            mm = pe.matmul(ps[0:rows, 2 * (k % 2) + x, c - rows:c], ident16[0:rows, 0:rows],
                                           mask16[0:rows, 0, 0:rows], start=False, stop=True)
                    else:
                        mm = pe.matmul(s, ident16[0:rows, 0:rows], mask16[0:rows, t, o:o + c], start=False,
                                       stop=True)
                mm.then_inc(at_s, 1)

            def turn(k):
                t = k % NCH
                pe.wait_ge(at_p, g * UN + (k + 1))
                pe.wait_ge(at_pte, g * UN + (k + 1))
                rows = ROWS[t]
                for kb in range(t + 1):
                    mm = pe.transpose(ps[0:ROWS[kb], 4 + kb // 4, (kb % 4) * rows:(kb % 4 + 1) * rows],
                                      prob[k % 2][0:rows, kb * C:ENDS[kb]], ident[0:rows, 0:rows])
                mm.then_inc(at_pt, 1)

            def values(k):
                i, hh, t = unit(k)
                pe.wait_ge(at_pte, g * UN + (k + 2))
                if k >= 2:
                    pe.wait_ge(at_oe, g * UN + (k - 1))
                rows = ROWS[t]
                for kb in range(t + 1):
                    mm = pe.matmul(ps[0:rows, 6 + k % 2, t * 64:(t + 1) * 64],
                                   ptr[k % 2][0:ROWS[kb], kb * rows:(kb + 1) * rows],
                                   v[0:ROWS[kb], kb, bass.ds((m + i if fox else a) * P + 64 * hh, 64)],
                                   start=(kb == 0), stop=(kb == t))
                mm.then_inc(at_o, 1)

            def turn_output(i):
                pe.wait_ge(at_oe, g * UN + 2 * NCH * (i + 1))
                pe.wait_ge(at_pte, g * UN + (2 * NCH * (i + 1) + 2 - i))
                for t in range(NCH):
                    for x in range(2):
                        lo, hi = max(t * C, x * HT), min(ENDS[t], (x + 1) * HT)
                        if lo < hi:
                            rows = slice(lo - t * C, hi - t * C)
                            mm = pe.matmul(ps[:, 4 + x, lo - x * HT:hi - x * HT],
                                           otok[0:ROWS[t], i, t * P:(t + 1) * P], ident[0:ROWS[t], rows],
                                           start=True, stop=True)
                mm.then_inc(at_ot, 1)

            if fox:
                pe.wait_ge(at_row, g - 3)
            scores(0)
            scores(1)
            for k in range(UN):
                if k + 2 < UN:
                    scores(k + 2)
                if k == 0:
                    pe.wait_ge(at_of, g * 2 + 1)
                if k == 2 * NCH + 1:
                    pe.wait_ge(at_of, g * 2 + 2)
                turn(k)
                if k:
                    values(k - 1)
                if k == 2 * NCH:
                    turn_output(0)
            values(UN - 1)
            turn_output(1)

        att_loop(pe, "pe", body)

    def act_attention(act, fox):
        if not fox:
            act.sem_inc(at_pte, 1)
        act.wait_ge(at_zero, 2 if fox else 1)

        def body(a, m, g):
            def exp(k):
                n, rows = ENDS[k % NCH], ROWS[k % NCH]
                act.wait_ge(at_mx, g * UN + (k + 1))
                act.wait_ge(at_pt, g * UN + (k + 1))
                act.activation(as_psum(prob[k % 2][0:rows, 0:n], n), psum_cols(2 * (k % 2), rows, n), ACT.Exp,
                               bias=rowmax[0:rows, k:k + 1], accum_out=rowsum[0:rows, k:k + 1]).then_inc(at_p, 1)

            def out(k):
                t = k % NCH
                n, rows = min(t + 1, 4) * ROWS[t], ROWS[t]
                act.wait_ge(at_pt, g * UN + (k + 3))
                act.wait_ge(at_o, g * UN + (k + 1))
                last = act.activation(ptr[k % 2][:, 0:n], ps[0:C, 4, 0:n], ACT.Copy)
                if t == 4:
                    last = act.activation(ptr[k % 2][0:rows, n:n + rows], ps[0:rows, 5, 0:rows], ACT.Copy)
                last.then_inc(at_pte, 1)

            for i in range(2):
                x = tile_at(pf, act.snap(m + (i + 16 if fox else i)))
                act.wait_ge(at_s, g * UN + 2)
                act.activation(qz[0:64, 2 * i, :], x[0:64], ACT.Copy)
                act.activation(qz[64:P, 2 * i + 1, :], x[64:P], ACT.Copy).then_inc(at_q, 1)
            exp(0)
            for k in range(UN):
                if k + 1 < UN:
                    exp(k + 1)
                out(k)

        att_loop(act, "act", body)

    def dve_attention(dve, fox):
        if not fox:
            dve.sem_inc(at_of, 1)
        else:
            dve.memset(headrow[:, :, :], 0.0)
            dve.drain()

        def body(a, m, g):
            def top(k):
                n, rows = ENDS[k % NCH], ROWS[k % NCH]
                dve.wait_ge(at_s, g * UN + (k + 3))
                dve.tensor_reduce(rowmax[0:rows, k:k + 1], psum_cols(2 * (k % 2), rows, n),
                                  AX.X if n <= 512 else AX.XY, ALU.max, negate=True).then_inc(at_mx, 1)

            def out(k):
                i, hh, t = unit(k)
                rows = ROWS[t]
                dve.wait_ge(at_o, g * UN + (k + 3))
                dve.reciprocal(rowinv[0:rows, k:k + 1], rowsum[0:rows, k:k + 1])
                dve.drain()
                dve.tensor_scalar(otok[0:rows, i, t * P + 64 * hh:t * P + 64 * hh + 64],
                                  ps[0:rows, 6 + k % 2, t * 64:(t + 1) * 64], rowinv[0:rows, k:k + 1], None,
                                  ALU.mult).then_inc(at_oe, 1)

            if fox:
                heads_ = [dve.snap(m * 2 + h) for h in range(4)]
                dve.wait_ge(at_s, g * UN + 2)
                for h in range(4):
                    for part in range(3):
                        last = dve.tensor_copy(headrow[32 * part:32 * part + 16, h, :],
                                               ident[0:16, bass.ds(heads_[h], 1)].broadcast_to([16, C]))
                last.then_inc(at_row, 1)

            def store(i):
                hi, lo = (two(tile_at(x, dve.snap(m + i))) for x in (xbh, xbl))
                dve.wait_ge(at_ot, g * 2 + (i + 1))
                dve.tensor_scalar(hi, pair_of(4), 1.0, None, ALU.mult)
                dve.drain()
                dve.tensor_tensor(lo, pair_of(4), hi.bitcast(F32), ALU.subtract).then_inc(at_of, 1)

            for k in range(UN):
                top(k)
                if k >= 2:
                    out(k - 2)
                if k == 2 * NCH + 1:
                    store(0)
            out(UN - 2)
            out(UN - 1)
            store(1)

        att_loop(dve, "dve", body)

    def pe_wit(pe):
        for c in range(NCH):
            mm = pe.transpose(ps[0:ROWS[c], 0, c * 8:(c + 1) * 8], wi[:, c * C:ENDS[c]], ident[0:8, 0:8])
        mm.then_inc(wit_pe, 1)

    def act_wit(act):
        act.wait_ge(wit_pe, 1)
        for c in range(NCH):
            act.activation(wit[0:ROWS[c], c, :], ps[0:ROWS[c], 0, c * 8:(c + 1) * 8], ACT.Copy)

    def act_dsa(act):
        def body(j, u, b):
            split_hi(act, nxt(b))
            act.wait_ge(block_done, num(b) + 1)
            if isinstance(j, int) and j == 17:
                act.activation(two(wi[:, :]), acc(b, 8), ACT.Copy, scale=8 ** -0.5 * 64 ** -0.5).then_inc(acc_free, 1)
            else:
                act.activation(two(tile_at(pf, j)), acc(b), ACT.Copy).then_inc(acc_free, 1)
        blocks(act, SEGS["dsa"], body, last=1)

    def act_foxf(act):
        b = Blk(SEGS["foxf"].b0, 0)
        split_hi(act, nxt(b))
        act.wait_ge(block_done, num(b) + 1)
        act.activation(two(lfneg[:, :]), acc(b, 16), ACT.Copy).then_inc(acc_free, 1)

    def dve_forget(dve):
        dve.tensor_scalar(lfneg[:, :], lfneg[:, :], rowvec[:, 2:3], -1.0, ALU.add, ALU.mult)
        dve.drain()
        dve_softplus(dve, cneg[:, :], lfneg[:, :])
        dve.memset(sp[0][:, :], 1.0)
        dve.drain()
        dve.tensor_tensor_scan(lfneg[:, :], sp[0][:, :], cneg[:, :], 0.0, ALU.mult, ALU.add)
        dve.memset(decay_row[:, :], 0.0)
        for part in range(3):
            dve.drain()
            rows = slice(32 * part, 32 * part + 16)
            dve.tensor_copy(decay_row[rows, :], lfneg[:, :])
            dve.drain()
            if part < 2:
                dve.tensor_tensor(lfneg[:, :], lfneg[:, :], decay_row[rows, :], ALU.subtract)

    def up(j, u):
        return stage_at(u)

    consts = (
        (res[:, :].rearrange("p (k t) -> p k t", t=T), io["x"].rearrange("k p t -> p k t")),
        (gains[:, :], io["gains"]), (headgain[:, 0:5], io["headgain"]), (rowvec[:, 0:4], io["rowvec"]),
        (ident[:, :], io["ident"]), (win128[:, :], io["win128"]), (win64[:, :], io["win64"]),
        (convw[:, :], io["convw"]), (scw[:, :], io["scw"]), (tri[:, :, :], io["tri"]),
        (masks[:, :, :, :], io["masks"]), (sel[:, :, :, :], io["sel"]))

    def loaded(e):
        e.wait_ge(const_in, 16 * len(consts))

    with nc.Block() as block:
        @block.tensor
        def _(pe):
            loaded(pe)
            for ring in (nused, hused, vt_pe):
                pe.sem_inc(ring, 2)
            pe.wait_ge(prep_dve_ones, 1)
            pe_norm(pe)
            barrier(pe, "pe")
            pe_segment(pe, "ba", xah, xal)
            pe_segment(pe, "qkv", xah, xal)
            pe_headnorm(pe, 16, P)
            barrier(pe, "pe")
            pe_prep(pe)
            barrier(pe, "pe")
            pe_delta(pe)
            barrier(pe, "pe")
            pe_headnorm(pe, 8, P)
            barrier(pe, "pe")
            pe_segment(pe, "z", xah, xal)
            pe_segment(pe, "sc", xah, xal)
            pe_segment(pe, "gates", xah, xal)
            pe_segment(pe, "ya", xbh, xbl)
            pe_segment(pe, "yb", xah, xal)
            pe_segment(pe, "wout", xbh, xbl, norm=True)
            for p in range(len(FF1_PARTS)):
                pe_segment(pe, f"gu{p}", xah, xal, fresh=1 if p == 0 else None)
                pe_segment(pe, f"dn{p}", xbh, xbl, norm=p == len(FF1_PARTS) - 1)
            barrier(pe, "pe")
            barrier(pe, "pe")
            pe_norm(pe)
            pe_segment(pe, "dsa", xah, xal, fresh=2)
            barrier(pe, "pe")
            pe_vtok(pe, 2)
            pe_wit(pe)
            pe_headnorm(pe, 8, 64)
            pe_headnorm(pe, 2, 64)
            barrier(pe, "pe")
            pe_rope(pe, 0, 10)
            pe_rope(pe, 12, 5)
            barrier(pe, "pe")
            pe_index(pe)
            barrier(pe, "pe")
            pe_attention(pe, False)
            barrier(pe, "pe")
            pe_segment(pe, "dsa_out", xbh, xbl, norm=True)
            for p in range(len(FF2_PARTS)):
                pe_segment(pe, f"up0_{p}", xah, xal, fresh=3 if p == 0 else None)
                pe_segment(pe, f"down0_{p}", xbh, xbl, norm=p == len(FF2_PARTS) - 1)
            pe_segment(pe, "foxkv", xah, xal, fresh=4)
            pe_segment(pe, "foxf", xah, xal)
            pe_segment(pe, "foxq", xbh, xbl, fresh=5)
            barrier(pe, "pe")
            pe_vtok(pe, 8)
            pe_headnorm(pe, 8, 64)
            pe_headnorm(pe, 8, 64)
            barrier(pe, "pe")
            pe_attention(pe, True)
            barrier(pe, "pe")
            pe_segment(pe, "fox_out", xbh, xbl, norm=True)
            for p in range(len(FF2_PARTS)):
                pe_segment(pe, f"up1_{p}", xah, xal, fresh=6 if p == 0 else None)
                pe_segment(pe, f"down1_{p}", xbh, xbl)
            barrier(pe, "pe")

        @block.scalar
        def _(act):
            loaded(act)
            for ring in (silu_done, vt_out):
                act.sem_inc(ring, 2)
            act.wait_ge(prep_dve_ones, 1)
            act_norm(act)
            act_norm_apply(act, xah)
            split_hi(act, Blk(0, 0))
            barrier(act, "act")
            act_ba(act)
            act_qkv(act)
            act.activation(rowvec[:, 4:5], rowvec[:, 1:2], ACT.Exp).then_inc(prep_act, 1)
            act_softplus(act, gdec[:, 0:T])
            act_headnorm(act, qkv, 0, 16, P, 1.0)
            barrier(act, "act")
            act_prep(act)
            barrier(act, "act")
            act_delta(act)
            barrier(act, "act")
            act_headnorm(act, oacc, 0, 8, P, 1.0 / P)
            barrier(act, "act")
            act_segment(act, "z", up, ACT.Silu, posts=True)
            act_sc(act)
            act_segment(act, "gates", lambda j, u: tile_at(gab, j), ACT.Sigmoid)
            for name in ("ya", "yb", "wout"):
                act_segment(act, name, up, posts=True, norm=name == "wout")
            act_norm(act, squares=False)
            act_norm_apply(act, xah)
            for p in range(len(FF1_PARTS)):
                act_gated(act, f"gu{p}")
                act_segment(act, f"dn{p}", up, posts=True, norm=p == len(FF1_PARTS) - 1)
            act_norm(act, squares=False)
            barrier(act, "act")
            for dst, src in ((res[:, :].rearrange("p (k t) -> p k t", t=T)[:, :, 0:NMETA],
                              io["meta2"].rearrange("k p t -> p k t")),
                             (causal[:, :], io["causal"]), (cossin[:, :, :], io["cossin"]), (rot[:, :], io["rot"])):
                act.dma_start(dst, src).then_inc(const2_in, 16)
            act.wait_ge(const2_in, 64)
            barrier(act, "act")
            act_norm(act)
            act_norm_apply(act, xah)
            act_dsa(act)
            barrier(act, "act")
            act_vtok(act, 10, 2, vt2)
            act_wit(act)
            act_headnorm(act, pf, 0, 8, 64, 1.0 / 64)
            act_headnorm(act, pf, 8, 2, 64, 1.0 / 64)
            barrier(act, "act")
            barrier(act, "act")
            act_index(act)
            barrier(act, "act")
            act_attention(act, False)
            barrier(act, "act")
            act_segment(act, "dsa_out", up, posts=True, norm=True)
            act_norm(act, squares=False)
            act_norm_apply(act, xah)
            for p in range(len(FF2_PARTS)):
                act_segment(act, f"up0_{p}", up, ACT.Relu, posts=True)
                act_segment(act, f"down0_{p}", up, posts=True, norm=p == len(FF2_PARTS) - 1)
            act_norm(act, squares=False)
            act_norm_apply(act, xah)
            act_norm_apply(act, xbh)
            act_segment(act, "foxkv", lambda j, u: tile_at(pf, j))
            act_foxf(act)
            act_segment(act, "foxq", lambda j, u: tile_at(pf, j + 16))
            barrier(act, "act")
            act_softplus(act, lfneg[:, :])
            act_vtok(act, 8, 8, vtok)
            act_headnorm(act, pf, 0, 8, 64, 1.0 / 64)
            act_headnorm(act, pf, 16, 8, 64, 1.0 / 64)
            barrier(act, "act")
            act_attention(act, True)
            barrier(act, "act")
            act_segment(act, "fox_out", up, posts=True, norm=True)
            act_norm(act, squares=False)
            act_norm_apply(act, xah)
            for p in range(len(FF2_PARTS)):
                act_segment(act, f"up1_{p}", up, ACT.Relu, posts=True)
                act_segment(act, f"down1_{p}", up, posts=True)
            barrier(act, "act")

        @block.vector
        def _(dve):
            for ring in (post_done, conv_done, happ, rope_dve):
                dve.sem_inc(ring, 2)
            dve.memset(ones[:, :], 1.0)
            dve.memset(eps[:, :], EPS)
            dve.drain().then_inc(prep_dve_ones, 1)
            loaded(dve)
            for k in (1, 4):
                dve.tensor_scalar(headgain[:, k:k + 1], headgain[:, k:k + 1], 64 ** -0.5, None, ALU.mult)
            dve_norm(dve)
            dve_norm_apply(dve, 0)
            barrier(dve, "dve")
            dve_qkv(dve)
            dve_decay(dve)
            dve_headnorm(dve, qkv, 0, 16, P, 1.0, rowvec[:, 3:4])
            barrier(dve, "dve")
            dve_prep(dve)
            barrier(dve, "dve")
            dve_delta(dve)
            barrier(dve, "dve")
            dve_headnorm(dve, oacc, 0, 8, P, headgain[:, 0:1])
            barrier(dve, "dve")
            dve_z(dve)
            dve_sc(dve)
            dve_ya(dve)
            dve_yb(dve)
            dve_segment(dve, "wout", add_residual(dve))
            dve_norm(dve)
            dve_norm_apply(dve, 1)
            for p in range(len(FF1_PARTS)):
                dve_gated(dve, f"gu{p}")
                dve_segment(dve, f"dn{p}", add_residual(dve))
            dve_norm(dve)
            tiles(dve, KT, lambda m, u: dve.scalar_tensor_tensor(
                tile_at(res, m), tile_at(res, m), gains[:, bass.ds(m + 2 * KT, 1)], rstd[:, :],
                ALU.mult, ALU.mult))
            barrier(dve, "dve")
            barrier(dve, "dve")
            dve_norm(dve)
            dve_norm_apply(dve, 3)
            barrier(dve, "dve")
            dve_headnorm(dve, pf, 0, 8, 64, headgain[:, 1:2])
            dve_headnorm(dve, pf, 8, 2, 64, headgain[:, 2:3])
            barrier(dve, "dve")
            dve_rope(dve, 0, 10)
            dve_rope(dve, 12, 5)
            barrier(dve, "dve")
            dve_index(dve)
            dve_topk(dve)
            barrier(dve, "dve")
            dve_attention(dve, False)
            barrier(dve, "dve")
            dve_segment(dve, "dsa_out", add_residual(dve))
            dve_norm(dve)
            dve_norm_apply(dve, 4)
            for p in range(len(FF2_PARTS)):
                dve_relu2(dve, f"up0_{p}")
                dve_segment(dve, f"down0_{p}", add_residual(dve))
            dve_norm(dve)
            dve_norm_apply(dve, 5)
            dve_norm_apply(dve, 6)
            barrier(dve, "dve")
            dve_forget(dve)
            dve_headnorm(dve, pf, 0, 8, 64, headgain[:, 3:4])
            dve_headnorm(dve, pf, 16, 8, 64, headgain[:, 4:5])
            barrier(dve, "dve")
            dve_attention(dve, True)
            barrier(dve, "dve")
            dve_segment(dve, "fox_out", add_residual(dve))
            dve_norm(dve)
            dve_norm_apply(dve, 7)
            for p in range(len(FF2_PARTS)):
                dve_relu2(dve, f"up1_{p}")
                dve_segment(dve, f"down1_{p}", add_residual(dve))
            barrier(dve, "dve")

        @block.gpsimd
        def _(pool):
            pool.sem_inc(nlo, 2)
            pool_norm_apply(pool, xah, xal)
            split_lo(pool, Blk(0, 0))
            barrier(pool, "pool")
            pool_segment(pool, "ba")
            pool_segment(pool, "qkv")
            barrier(pool, "pool")
            barrier(pool, "pool")
            pool_delta(pool)
            barrier(pool, "pool")
            barrier(pool, "pool")
            for name in ("z", "sc", "gates", "ya", "yb", "wout"):
                pool_segment(pool, name)
            pool_norm_apply(pool, xah, xal)
            for p in range(len(FF1_PARTS)):
                pool_segment(pool, f"gu{p}")
                pool_segment(pool, f"dn{p}")
            barrier(pool, "pool")
            barrier(pool, "pool")
            pool_norm_apply(pool, xah, xal)
            pool_segment(pool, "dsa")
            barrier(pool, "pool")
            barrier(pool, "pool")
            pool_rope(pool, 0, 10)
            pool_rope(pool, 12, 5)
            barrier(pool, "pool")
            pool_index(pool)
            barrier(pool, "pool")
            pool_attention(pool)
            barrier(pool, "pool")
            pool_segment(pool, "dsa_out")
            pool_norm_apply(pool, xah, xal)
            for p in range(len(FF2_PARTS)):
                pool_segment(pool, f"up0_{p}")
                pool_segment(pool, f"down0_{p}")
            pool_norm_apply(pool, xah, xal)
            pool_norm_apply(pool, xbh, xbl)
            pool_segment(pool, "foxkv")
            pool_segment(pool, "foxf")
            pool_segment(pool, "foxq")
            barrier(pool, "pool")
            barrier(pool, "pool")
            pool_attention(pool)
            barrier(pool, "pool")
            pool_segment(pool, "fox_out")
            pool_norm_apply(pool, xah, xal)
            for p in range(len(FF2_PARTS)):
                pool_segment(pool, f"up1_{p}")
                pool_segment(pool, f"down1_{p}")
            barrier(pool, "pool")

        @block.sync
        def _(sp):
            for dst, src in consts:
                sp.dma_start(dst, src).then_inc(const_in, 16)
            load_weights(sp)
            sp.wait_ge(phase_done, 4 * phases["pe"])
            sp.dma_start(out.rearrange("k p t -> p k t"),
                         res[:, :].rearrange("p (k t) -> p k t", t=T)[:, :, NMETA:T]).then_inc(out_sent, 16)
            sp.wait_ge(out_sent, 16)


def constants():
    f = np.float32
    ident = np.eye(P, dtype=f)
    win128 = np.zeros((P, 31), f)
    win128[:, 15] = 1
    win64 = np.zeros((P, 30), f)
    win64[0:64, 14] = 1
    win64[64:128, 15] = 1
    s, i = np.arange(C)[:, None], np.arange(C)[None, :]
    tri = np.stack([s <= i, s >= i], 1).astype(f)
    masks = np.zeros((C, 2, LEVELS, C), f)
    for lv in range(LEVELS):
        b = 2 ** lv
        same = (s // (2 * b)) == (i // (2 * b))
        lo, hi = (s // b) % 2 == 0, (i // b) % 2 == 1
        masks[:, 0, lv, :] = same & lo & hi
        masks[:, 1, lv, :] = same & ~lo & ~hi
    sel = np.zeros((16, 2, NG, GH), f)
    for u in range(2):
        for g in range(NG):
            for r in range(GH):
                sel[8 * u + GH * g + r, u, g, r] = 1
    causal = np.where(s >= i, 0.0, NEG).astype(f)
    inv = (1.0 / (np.float32(10000.0) ** (np.arange(0, 64, 2, dtype=f) / f(64)))).astype(f)
    ang = np.arange(T, dtype=f)[:, None] * inv[None, :]
    cossin = np.stack([np.tile(np.cos(ang).T, (4, 1)), np.tile(np.sin(ang).T, (4, 1))], 1).astype(f)
    rot = np.zeros((P, P), f)
    for h in range(2):
        for d in range(32):
            rot[64 * h + 32 + d, 64 * h + d] = -1
            rot[64 * h + d, 64 * h + 32 + d] = 1
    return dict(ident=ident, win128=win128, win64=win64, tri=tri, masks=masks, sel=sel, causal=causal,
                cossin=np.ascontiguousarray(cossin), rot=rot)


def columns(m):
    k, n = m.shape
    x = m.reshape(k // P, P, n // P, P).transpose(2, 1, 0, 3).reshape(n // P, P, k)
    return x if k == DM else np.concatenate([x, np.zeros((n // P, P, DM - k), x.dtype)], 2)


def widened(m):
    return np.concatenate([m, np.zeros((m.shape[0], P - m.shape[1]), m.dtype)], 1)


def lay_weights(a):
    wi_ = a["w_in"][0]
    cuts = np.cumsum([1024, 1024, 1024, 1024, 16, 16, 1024, 1024, 1024, 1024, 1024])
    q, k, v, z, b, aa, scb, scc, scx, ga, gb = np.split(wi_, cuts[:-1], axis=1)
    out = [columns(widened(b)), columns(widened(aa)), columns(q), columns(k), columns(v), columns(z)]
    out.append(np.stack([columns(scb), columns(scc), columns(scx)], 1).reshape(24, P, DM))
    out += [columns(ga), columns(gb), columns(a["w_branch_dn"][0]), columns(a["w_branch_sc"][0]),
            columns(a["w_out"][0])]
    gu, dn = a["w_gate_up"][0], a["w_down"][0]
    at = 0
    for n in FF1_PARTS:
        g = columns(gu[:, at:at + n * P])
        u = columns(gu[:, FF1 + at:FF1 + at + n * P])
        out.append(np.stack([g, u], 1).reshape(2 * n, P, DM))
        out.append(columns(dn[at:at + n * P]))
        at += n * P
    w = a["a_w_in_2"][0]
    q, k, v, qi, ki, wt = np.split(w, np.cumsum([1024, 256, 256, 512, 64]), axis=1)
    order = dsa_heads()
    q = q.reshape(DM, 16, 64)[:, order].reshape(DM, DM)
    out += [columns(q), columns(k), columns(v), columns(qi), columns(np.concatenate([ki, ki], 1)),
            columns(widened(wt)), columns(a["a_w_out_2"][0].reshape(16, 64, DM)[order].reshape(DM, DM))]

    def mlp(i):
        for p in range(4):
            out.append(columns(a["mlp_w1_2"][i][:, p * DM:(p + 1) * DM]))
            out.append(columns(a["mlp_w2_2"][i][p * DM:(p + 1) * DM]))

    mlp(0)
    kv = a["kv_w_2"]
    out += [columns(kv[:, :2 * DM]), columns(widened(kv[:, 2 * DM:])), columns(a["b_w_q_2"][0]),
            columns(a["b_w_out_2"][0])]
    mlp(1)
    out = np.concatenate(out, 0)
    assert out.shape == (NB, P, DM)
    return out


def dsa_heads():
    return [(2 * (m // 4) + h) * 4 + m % 4 for m in range(8) for h in range(2)]


def lay_inputs(inputs):
    a = {k: np.asarray(v) for k, v in inputs.items()}
    f = np.float32
    x = np.concatenate([a["meta_tokens"], a["x"][0]], 0)
    per = lambda v: v.reshape(KT, P).T
    gains = [a["norm1_w"][0], a["norm2_w"][0], a["final_norm_w"], a["attn_norm_2"][0], a["mlp_norm_2"][0],
             a["kv_norm_2"], a["attn_norm_2"][1], a["mlp_norm_2"][1]]
    twice = lambda v: np.concatenate([v, v])
    qscale = np.array([P ** -0.5] * 8 + [1.0] * 8, f)
    lay = dict(
        w=lay_weights(a),
        x=x.T.reshape(KT, P, T),
        meta2=a["meta_tokens_2"].T.reshape(KT, P, NMETA),
        gains=np.concatenate([per(g) for g in gains], 1),
        headgain=np.stack([a["dn_norm_w"][0], twice(a["a_q_gain_2"][0]), twice(a["a_k_gain_2"][0]),
                           twice(a["kv_k_gain_2"]), twice(a["b_q_gain_2"][0])], 1),
        rowvec=np.stack([a["dt_bias"][0].reshape(16), a["A_log"][0].reshape(16), a["kv_f_bias_2"], qscale], 1),
        convw=a["dn_conv_w"][0].reshape(5, 24, P).transpose(2, 1, 0).reshape(P, 120),
        scw=a["sc_conv_w"][0].reshape(3, 8, P).transpose(2, 1, 0).reshape(P, 24),
        **constants())
    return {k: np.ascontiguousarray(v) for k, v in lay.items()}


def kernel(**inputs):
    import concourse.bacc as bacc
    from concourse.bass_utils import run_bass_kernel_spmd

    nc = bacc.Bacc("TRN2", target_bir_lowering=False, num_devices=1)
    arrays, io = {}, {}
    for name, v in lay_inputs(inputs).items():
        arrays[f"in_{name}"] = v
        io[name] = nc.dram_tensor(f"in_{name}", v.shape, mybir.dt.from_np(v.dtype), kind="ExternalInput").ap()
    io["out"] = nc.dram_tensor("out", (KT, P, SEQ), F32, kind="ExternalOutput").ap()
    build_program(nc, io)
    got = run_bass_kernel_spmd(nc, [arrays], core_ids=[0]).results[0]["out"]
    return np.ascontiguousarray(got.reshape(DM, SEQ).T).reshape(1, SEQ, DM)
```
